# Optimizing a Trainium2 kernel written in Bass

```python
import jax, jax.numpy as jnp
from jax import lax
import numpy as np
import math

D_MODEL = 1024
BATCH = 1
SEQ = 256
DEPTH = 2

HEAD_DIM = 64
DIL_PAIRS = ((128, 1), (512, 4), (2048, 16))
N_DIL_GROUPS = len(DIL_PAIRS)
DIL_HEADS_PER_GROUP = 4
DIL_HEADS = N_DIL_GROUPS * DIL_HEADS_PER_GROUP
SB_HEADS = 4
DIL_WIDTH = DIL_HEADS * HEAD_DIM
SB_WIDTH = SB_HEADS * HEAD_DIM
DIL_OUT_WIDTH = DIL_HEADS_PER_GROUP * HEAD_DIM
N_BRANCHES = 2
IN_COLS = 3 * DIL_WIDTH + 3 * SB_WIDTH + N_BRANCHES * D_MODEL
D_FF = 2816
CONV_WIDTH = 3
ROPE_THETA = 500000.0
ROPE_DIM = HEAD_DIM // 4
Q_BLOCK = 128
NORM_EPS = 1e-5
MAX_POS_OFFSET = 4096
MASK_VALUE = -1e30


def rms_norm(x, gain):
    xf = x.astype(jnp.float32)
    xf = xf * lax.rsqrt(jnp.mean(xf * xf, axis=-1, keepdims=True) + NORM_EPS)
    return (xf * gain.astype(jnp.float32)).astype(x.dtype)

def rope_tables(positions, dtype):
    inv_freq = ROPE_THETA ** (-jnp.arange(0, ROPE_DIM, 2, dtype=jnp.float32) / ROPE_DIM)
    ang = positions.astype(jnp.float32)[..., None] * inv_freq
    return (jnp.cos(ang)[:, :, None, None, :].astype(dtype),
            jnp.sin(ang)[:, :, None, None, :].astype(dtype))

def apply_partial_rope(x, cos, sin):
    half = ROPE_DIM // 2
    x1, x2, rest = x[..., :half], x[..., half:ROPE_DIM], x[..., ROPE_DIM:]
    return jnp.concatenate([x1 * cos - x2 * sin, x2 * cos + x1 * sin, rest], axis=-1)

def dilated_attention(q, k, v):
    b, s = q.shape[0], q.shape[1]
    n_blocks = s // Q_BLOCK
    scale = HEAD_DIM ** -0.5
    qs = [q[:, :, g] for g in range(N_DIL_GROUPS)]
    ks = [k[:, :, g] for g in range(N_DIL_GROUPS)]
    vs = [v[:, :, g] for g in range(N_DIL_GROUPS)]

    def block(t0):
        t = t0 + jnp.arange(Q_BLOCK)
        outs, lses = [], []
        for g, (window, dil) in enumerate(DIL_PAIRS):
            n_keys = window // dil + 1
            idx = t[:, None] - dil * jnp.arange(n_keys)[None, :]
            valid = idx >= 0
            idx = jnp.maximum(idx, 0)
            qg = lax.dynamic_slice_in_dim(qs[g], t0, Q_BLOCK, axis=1)
            kg = ks[g][:, idx]
            vg = vs[g][:, idx]
            sc = jnp.einsum('bqhd,bqkhd->bhqk', qg, kg).astype(jnp.float32) * scale
            sc = jnp.where(valid[None, None], sc, MASK_VALUE)
            m = jnp.max(sc, axis=-1, keepdims=True)
            p = jnp.exp(sc - m)
            den = jnp.sum(p, axis=-1)
            o = jnp.einsum('bhqk,bqkhd->bqhd', p, vg.astype(jnp.float32))
            o = o / jnp.transpose(den, (0, 2, 1))[..., None]
            outs.append(o)
            lses.append(m[..., 0] + jnp.log(den))
        o_all = jnp.stack(outs, axis=0)
        w = jax.nn.softmax(jnp.stack(lses, axis=0), axis=0)
        w = jnp.transpose(w, (0, 1, 3, 2))[..., None]
        return jnp.sum(w * o_all, axis=0).astype(q.dtype)

    out = lax.map(block, jnp.arange(n_blocks) * Q_BLOCK)
    return jnp.moveaxis(out, 0, 1).reshape(b, s, DIL_OUT_WIDTH)

def stick_breaking_attention(q, k, v):
    b, s = q.shape[0], q.shape[1]
    n_blocks = s // Q_BLOCK
    scale = HEAD_DIM ** -0.5
    key_pos = jnp.arange(s)

    def block(t0):
        qb = lax.dynamic_slice_in_dim(q, t0, Q_BLOCK, axis=1)
        z = jnp.einsum('bqhd,bkhd->bhqk', qb, k).astype(jnp.float32) * scale
        t = t0 + jnp.arange(Q_BLOCK)
        causal = key_pos[None, :] < t[:, None]
        log_keep = jnp.where(causal, jax.nn.log_sigmoid(-z), 0.0)
        suffix = lax.cumsum(log_keep, axis=3, reverse=True) - log_keep
        attn = jnp.where(causal, jnp.exp(jax.nn.log_sigmoid(z) + suffix), 0.0)
        return jnp.einsum('bhqk,bkhd->bqhd', attn, v.astype(jnp.float32)).astype(q.dtype)

    out = lax.map(block, jnp.arange(n_blocks) * Q_BLOCK)
    return jnp.moveaxis(out, 0, 1).reshape(b, s, SB_WIDTH)

def conv_ffn(h, w_up, conv_w, conv_b, w_down):
    up = h @ w_up
    a, bval = up[..., :D_FF], up[..., D_FF:]
    a = lax.conv_general_dilated(a, conv_w[:, None, :].astype(a.dtype), window_strides=(1,),
                                 padding=((CONV_WIDTH - 1, 0),),
                                 dimension_numbers=('NWC', 'WIO', 'NWC'),
                                 feature_group_count=D_FF) + conv_b
    return (jax.nn.silu(a) * bval) @ w_down

def first_inputs(seed: int = 0) -> dict:
    key = jax.random.key(seed)
    ks = jax.random.split(key, 16)
    f32 = jnp.float32
    nrm = lambda k, shape, s: jax.random.normal(k, shape, f32) * s
    x = jax.random.normal(ks[0], (BATCH, SEQ, D_MODEL), f32)
    offset = jax.random.randint(ks[1], (BATCH, 1), 0, MAX_POS_OFFSET, dtype=jnp.int32)
    positions = offset + jnp.arange(SEQ, dtype=jnp.int32)[None, :]
    return {
        "x": x,
        "positions": positions,
        "norm_mix": 1.0 + nrm(ks[2], (DEPTH, D_MODEL), 0.05),
        "w_in": nrm(ks[3], (DEPTH, D_MODEL, IN_COLS), D_MODEL ** -0.5),
        "b_gate": nrm(ks[4], (DEPTH, N_BRANCHES * D_MODEL), 0.1),
        "w_proj_a": nrm(ks[5], (DEPTH, DIL_OUT_WIDTH, D_MODEL), DIL_OUT_WIDTH ** -0.5),
        "w_proj_b": nrm(ks[6], (DEPTH, SB_WIDTH, D_MODEL), SB_WIDTH ** -0.5),
        "w_out": nrm(ks[7], (DEPTH, D_MODEL, D_MODEL), D_MODEL ** -0.5),
        "norm_ffn": 1.0 + nrm(ks[8], (DEPTH, D_MODEL), 0.05),
        "w_up": nrm(ks[9], (DEPTH, D_MODEL, 2 * D_FF), D_MODEL ** -0.5),
        "conv_w": nrm(ks[10], (DEPTH, CONV_WIDTH, D_FF), CONV_WIDTH ** -0.5),
        "conv_b": nrm(ks[11], (DEPTH, D_FF), 0.02),
        "w_down": nrm(ks[12], (DEPTH, D_FF, D_MODEL), D_FF ** -0.5),
        "norm_final": 1.0 + nrm(ks[13], (D_MODEL,), 0.05),
    }

def first_block(x, positions, norm_mix, w_in, b_gate, w_proj_a, w_proj_b, w_out,
              norm_ffn, w_up, conv_w, conv_b, w_down, norm_final):
    b, s, _ = x.shape
    cos, sin = rope_tables(positions, x.dtype)
    splits = np.cumsum([DIL_WIDTH, DIL_WIDTH, DIL_WIDTH, SB_WIDTH, SB_WIDTH, SB_WIDTH]).tolist()
    for l in range(DEPTH):
        h = rms_norm(x, norm_mix[l])
        proj = h @ w_in[l]
        dq, dk, dv, sq, sk, sv, gate_logits = jnp.split(proj, splits, axis=-1)
        dshape = (b, s, N_DIL_GROUPS, DIL_HEADS_PER_GROUP, HEAD_DIM)
        dq = apply_partial_rope(dq.reshape(dshape), cos, sin)
        dk = apply_partial_rope(dk.reshape(dshape), cos, sin)
        dv = dv.reshape(dshape)
        sshape = (b, s, SB_HEADS, HEAD_DIM)
        y_a = dilated_attention(dq, dk, dv) @ w_proj_a[l]
        y_b = stick_breaking_attention(sq.reshape(sshape), sk.reshape(sshape), sv.reshape(sshape)) @ w_proj_b[l]
        gates = jax.nn.sigmoid(gate_logits + b_gate[l])
        mixed = gates[..., :D_MODEL] * y_a + gates[..., D_MODEL:] * y_b
        x = x + mixed @ w_out[l]
        h = rms_norm(x, norm_ffn[l])
        x = x + conv_ffn(h, w_up[l], conv_w[l], conv_b[l], w_down[l])
    return rms_norm(x, norm_final)


CHUNK = 64
N_MEM = 256
EPS = 1e-6
NEG_INF = -1e30

H_A = 8
DH_A = 64
D_LAT = 128
H_IDX = 8
DH_IDX = 64
TOPK_MAX = 256

H_B = 4
DH_B = 64

H_C = 16
H_C_KV = 2
G_C = H_C // H_C_KV
DH_C = 64
WINDOW = 128
WIN_CHUNKS = WINDOW // CHUNK
BAND = (WIN_CHUNKS + 1) * CHUNK

H_X = 4
DH_X = 64

D_FF_2 = 4 * D_MODEL

N_BUCKETS = 32
MAX_DIST = 1024
H_BIAS = H_A + H_B + H_C

N_EVEN = (DEPTH + 1) // 2
N_ODD = DEPTH // 2

EVEN_SIZES = (H_A * DH_A, D_LAT, H_IDX * DH_IDX, DH_IDX, H_IDX, 2 * H_B * DH_B, 2 * H_B * DH_B, 2 * H_B * DH_B)
EVEN_COLS = sum(EVEN_SIZES)
ODD_SIZES = (H_C * DH_C, H_C_KV * DH_C, H_C_KV * DH_C)
ODD_COLS = sum(ODD_SIZES)


def _split_points(sizes):
    pts, acc = [], 0
    for s in sizes[:-1]:
        acc += s
        pts.append(acc)
    return pts

def rms_norm_2(x, g):
    xf = x.astype(jnp.float32)
    y = xf * lax.rsqrt(jnp.mean(xf * xf, axis=-1, keepdims=True) + EPS)
    return (y * g.astype(jnp.float32)).astype(x.dtype)

def t5_bucket(rel):
    nb = N_BUCKETS // 2
    max_exact = nb // 2
    n = jnp.abs(rel)
    nf = jnp.maximum(n, 1).astype(jnp.float32)
    large = max_exact + (jnp.log(nf / max_exact) / math.log(MAX_DIST / max_exact) * (nb - max_exact)).astype(jnp.int32)
    large = jnp.minimum(large, nb - 1)
    return jnp.where(rel > 0, nb, 0) + jnp.where(n < max_exact, n, large)

def chunk_id(pos):
    return pos // CHUNK

def dsa_attention(q_a, c_kv, q_idx, k_idx, w_idx, w_uk, w_uv, table_a):
    B, S = q_a.shape[0], q_a.shape[1]
    topk = min(TOPK_MAX, S // 4)
    n_blk = S // Q_BLOCK
    spos = jnp.arange(S)
    scale = DH_A ** -0.5
    q_lat = jnp.einsum('bshd,hdl->bshl', q_a, w_uk)

    def block(i):
        t0 = i * Q_BLOCK
        tpos = t0 + jnp.arange(Q_BLOCK)
        ql = lax.dynamic_slice_in_dim(q_lat, t0, Q_BLOCK, axis=1)
        qi = lax.dynamic_slice_in_dim(q_idx, t0, Q_BLOCK, axis=1)
        wi = lax.dynamic_slice_in_dim(w_idx, t0, Q_BLOCK, axis=1)
        act = jax.nn.relu(jnp.einsum('bqhd,bsd->bqhs', qi, k_idx).astype(jnp.float32))
        score = jnp.einsum('bqhs,bqh->bqs', act, wi.astype(jnp.float32))
        adm = chunk_id(spos)[None, :] <= chunk_id(tpos)[:, None]
        score = jnp.where(adm[None], score, -jnp.inf)
        _, sel = lax.top_k(score, topk)
        valid = chunk_id(sel) <= chunk_id(tpos)[None, :, None]
        c_sel = jax.vmap(lambda c, ix: c[ix])(c_kv, sel)
        bias = table_a[t5_bucket(sel - tpos[None, :, None])]
        s = jnp.einsum('bqhl,bqkl->bqkh', ql, c_sel).astype(jnp.float32) * scale + bias
        s = jnp.where(valid[..., None], s, NEG_INF)
        p = jax.nn.softmax(s, axis=2)
        return jnp.einsum('bqkh,bqkl->bqhl', p.astype(c_sel.dtype), c_sel)

    o = lax.map(block, jnp.arange(n_blk))
    o = jnp.moveaxis(o, 0, 1).reshape(B, S, H_A, D_LAT)
    o = jnp.einsum('bshl,hld->bshd', o, w_uv)
    return o.reshape(B, S, H_A * DH_A)

def diff_attention(q_b, k_b, v_b, b_lambda, b_subln, table_b, lam_init):
    B, S = q_b.shape[0], q_b.shape[1]
    n_blk = S // Q_BLOCK
    spos = jnp.arange(S)
    scale = DH_B ** -0.5
    lf = b_lambda.astype(jnp.float32)
    lam = jnp.exp(jnp.sum(lf[0] * lf[1])) - jnp.exp(jnp.sum(lf[2] * lf[3])) + lam_init

    def block(i):
        t0 = i * Q_BLOCK
        tpos = t0 + jnp.arange(Q_BLOCK)
        qb = lax.dynamic_slice_in_dim(q_b, t0, Q_BLOCK, axis=1)
        bias = jnp.moveaxis(table_b[t5_bucket(spos[None, :] - tpos[:, None])], -1, 0)
        adm = chunk_id(spos)[None, :] <= chunk_id(tpos)[:, None]
        s = jnp.einsum('bqhmd,bshmd->bhmqs', qb, k_b).astype(jnp.float32) * scale + bias[None, :, None]
        s = jnp.where(adm, s, NEG_INF)
        p = jax.nn.softmax(s, axis=-1)
        a = p[:, :, 0] - lam * p[:, :, 1]
        return jnp.einsum('bhqs,bshe->bqhe', a.astype(v_b.dtype), v_b)

    o = lax.map(block, jnp.arange(n_blk))
    o = jnp.moveaxis(o, 0, 1).reshape(B, S, H_B, 2 * DH_B)
    o = rms_norm_2(o, b_subln) * (1.0 - lam_init)
    return o.reshape(B, S, H_B * 2 * DH_B)

def even_mixer(h, w_in, a_kv_norm, w_uk, w_uv, b_lambda, b_subln, w_out, table, lam_init):
    B, S, _ = h.shape
    z = h @ w_in
    q_a, c_kv, q_i, k_i, w_i, q_b, k_b, v_b = jnp.split(z, _split_points(EVEN_SIZES), axis=-1)
    c_kv = rms_norm_2(c_kv, a_kv_norm)
    o_a = dsa_attention(q_a.reshape(B, S, H_A, DH_A), c_kv, q_i.reshape(B, S, H_IDX, DH_IDX), k_i, w_i,
                        w_uk, w_uv, table[:, :H_A])
    o_b = diff_attention(q_b.reshape(B, S, H_B, 2, DH_B), k_b.reshape(B, S, H_B, 2, DH_B),
                         v_b.reshape(B, S, H_B, 2 * DH_B), b_lambda, b_subln, table[:, H_A:H_A + H_B], lam_init)
    return jnp.concatenate([o_a, o_b], axis=-1) @ w_out

def odd_mixer(h, w_in, sinks, w_out, table):
    B, S, _ = h.shape
    nc = S // CHUNK
    q, k, v = jnp.split(h @ w_in, _split_points(ODD_SIZES), axis=-1)
    q = q.reshape(B, nc, CHUNK, H_C_KV, G_C, DH_C)
    k = k.reshape(B, nc, CHUNK, H_C_KV, DH_C)
    v = v.reshape(B, nc, CHUNK, H_C_KV, DH_C)

    def band(t):
        tp = jnp.pad(t, ((0, 0), (WIN_CHUNKS, 0), (0, 0), (0, 0), (0, 0)))
        return jnp.concatenate([tp[:, j:j + nc] for j in range(WIN_CHUNKS + 1)], axis=2)

    kb, vb = band(k), band(v)
    rel = (jnp.arange(BAND)[None, :] - WIN_CHUNKS * CHUNK) - jnp.arange(CHUNK)[:, None]
    bias = jnp.moveaxis(table[:, H_A + H_B:][t5_bucket(rel)], -1, 0).reshape(H_C_KV, G_C, CHUNK, BAND)
    s = jnp.einsum('bcqkgd,bcskd->bckgqs', q, kb).astype(jnp.float32) * (DH_C ** -0.5) + bias
    valid = (jnp.arange(nc)[:, None] - WIN_CHUNKS + jnp.arange(BAND)[None, :] // CHUNK) >= 0
    s = jnp.where(valid[None, :, None, None, None, :], s, NEG_INF)
    sink = jnp.broadcast_to(sinks.astype(jnp.float32).reshape(H_C_KV, G_C)[None, None, :, :, None, None],
                            s.shape[:-1] + (1,))
    p = jax.nn.softmax(jnp.concatenate([s, sink], axis=-1), axis=-1)[..., :-1]
    o = jnp.einsum('bckgqs,bcskd->bcqkgd', p.astype(vb.dtype), vb).reshape(B, S, H_C * DH_C)
    return o @ w_out

def memory_cross_attention(h, mem, wq, wkv, wo, mem_norm):
    B, S, _ = h.shape
    M = mem.shape[1]
    q = (h @ wq).reshape(B, S, H_X, DH_X)
    kv = (rms_norm_2(mem, mem_norm) @ wkv).reshape(B, M, 2, H_X, DH_X)
    s = jnp.einsum('bshd,bmhd->bhsm', q, kv[:, :, 0]).astype(jnp.float32) * (DH_X ** -0.5)
    p = jax.nn.softmax(s, axis=-1)
    o = jnp.einsum('bhsm,bmhd->bshd', p.astype(kv.dtype), kv[:, :, 1]).reshape(B, S, H_X * DH_X)
    return o @ wo

def sq_relu_mlp(h, w1, w2):
    return jnp.square(jax.nn.relu(h @ w1)) @ w2

def second_inputs(seed: int = 0) -> dict:
    key = jax.random.key(seed)
    ks = jax.random.split(key, 20)

    def nrm(k, shape, scale):
        return jax.random.normal(k, shape, jnp.float32) * scale

    D = D_MODEL
    return {
        "x": nrm(ks[0], (BATCH, SEQ, D), 1.0),
        "mem": nrm(ks[1], (BATCH, N_MEM, D), 1.0),
        "rel_bias_table": nrm(ks[2], (N_BUCKETS, H_BIAS), 0.3),
        "norm_g": 1.0 + nrm(ks[3], (DEPTH, 6, D), 0.05),
        "ev_w_in": nrm(ks[4], (N_EVEN, D, EVEN_COLS), D ** -0.5),
        "ev_a_kv_norm": 1.0 + nrm(ks[5], (N_EVEN, D_LAT), 0.05),
        "ev_a_w_uk": nrm(ks[6], (N_EVEN, H_A, DH_A, D_LAT), DH_A ** -0.5),
        "ev_a_w_uv": nrm(ks[7], (N_EVEN, H_A, D_LAT, DH_A), D_LAT ** -0.5),
        "ev_b_lambda": nrm(ks[8], (N_EVEN, 4, DH_B), 0.1),
        "ev_b_subln": 1.0 + nrm(ks[9], (N_EVEN, 2 * DH_B), 0.05),
        "ev_w_out": nrm(ks[10], (N_EVEN, H_A * DH_A + 2 * H_B * DH_B, D), D ** -0.5),
        "od_w_in": nrm(ks[11], (N_ODD, D, ODD_COLS), D ** -0.5),
        "od_sinks": nrm(ks[12], (N_ODD, H_C), 0.5),
        "od_w_out": nrm(ks[13], (N_ODD, H_C * DH_C, D), (H_C * DH_C) ** -0.5),
        "xa_wq": nrm(ks[14], (DEPTH, D, H_X * DH_X), D ** -0.5),
        "xa_wkv": nrm(ks[15], (DEPTH, D, 2 * H_X * DH_X), D ** -0.5),
        "xa_wo": nrm(ks[16], (DEPTH, H_X * DH_X, D), (H_X * DH_X) ** -0.5),
        "xa_mem_norm": 1.0 + nrm(ks[17], (DEPTH, D), 0.05),
        "mlp_w1": nrm(ks[18], (DEPTH, D, D_FF_2), D ** -0.5),
        "mlp_w2": nrm(ks[19], (DEPTH, D_FF_2, D), D_FF_2 ** -0.5),
    }

def second_block(x, mem, rel_bias_table, norm_g, ev_w_in, ev_a_kv_norm, ev_a_w_uk, ev_a_w_uv, ev_b_lambda,
              ev_b_subln, ev_w_out, od_w_in, od_sinks, od_w_out, xa_wq, xa_wkv, xa_wo, xa_mem_norm,
              mlp_w1, mlp_w2):
    for l in range(DEPTH):
        g = norm_g[l]
        h = rms_norm_2(x, g[0])
        if l % 2 == 0:
            e = l // 2
            lam_init = 0.8 - 0.6 * math.exp(-0.3 * l)
            y = even_mixer(h, ev_w_in[e], ev_a_kv_norm[e], ev_a_w_uk[e], ev_a_w_uv[e], ev_b_lambda[e],
                           ev_b_subln[e], ev_w_out[e], rel_bias_table, lam_init)
        else:
            o = l // 2
            y = odd_mixer(h, od_w_in[o], od_sinks[o], od_w_out[o], rel_bias_table)
        x = x + rms_norm_2(y, g[1])
        h = rms_norm_2(x, g[2])
        y = memory_cross_attention(h, mem, xa_wq[l], xa_wkv[l], xa_wo[l], xa_mem_norm[l])
        x = x + rms_norm_2(y, g[3])
        h = rms_norm_2(x, g[4])
        y = sq_relu_mlp(h, mlp_w1[l], mlp_w2[l])
        x = x + rms_norm_2(y, g[5])
    return x


def setup_inputs(seed=0):
    out = dict(first_inputs(seed))
    for name, value in second_inputs(seed + 1).items():
        if name != "x":
            out[name + "_2"] = value
    return out


def reference(
    x, positions, norm_mix, w_in, b_gate, w_proj_a, w_proj_b, w_out, norm_ffn, w_up, conv_w,
    conv_b, w_down, norm_final, mem_2, rel_bias_table_2, norm_g_2, ev_w_in_2, ev_a_kv_norm_2,
    ev_a_w_uk_2, ev_a_w_uv_2, ev_b_lambda_2, ev_b_subln_2, ev_w_out_2, od_w_in_2, od_sinks_2,
    od_w_out_2, xa_wq_2, xa_wkv_2, xa_wo_2, xa_mem_norm_2, mlp_w1_2, mlp_w2_2,
):
    x = first_block(
        x, positions, norm_mix, w_in, b_gate, w_proj_a, w_proj_b, w_out, norm_ffn, w_up, conv_w,
        conv_b, w_down, norm_final,
    )
    return second_block(
        x, mem_2, rel_bias_table_2, norm_g_2, ev_w_in_2, ev_a_kv_norm_2, ev_a_w_uk_2,
        ev_a_w_uv_2, ev_b_lambda_2, ev_b_subln_2, ev_w_out_2, od_w_in_2, od_sinks_2, od_w_out_2,
        xa_wq_2, xa_wkv_2, xa_wo_2, xa_mem_norm_2, mlp_w1_2, mlp_w2_2,
    )


_drawn_inputs = setup_inputs


def setup_inputs(seed=0):
    import zlib

    import numpy as np

    out = dict(_drawn_inputs(seed))
    spreads = {}
    factors = {'od_sinks_2': 8.0}
    for name, (base, spread) in spreads.items():
        noise = np.random.default_rng([zlib.crc32(name.encode()), seed]).standard_normal(out[name].shape)
        drawn = base * np.exp(spread * noise) if base else spread * noise
        out[name] = __import__('jax').numpy.asarray(drawn.astype(out[name].dtype))
    for name, factor in factors.items():
        out[name] = (out[name] * factor).astype(out[name].dtype)
    return out
```

```python
from contextlib import ExitStack

import concourse.bass as bass
import numpy as np
from concourse import mybir

F32 = mybir.dt.float32
F32R = mybir.dt.float32r
I32 = mybir.dt.int32
ALU = mybir.AluOpType
ACT = mybir.ActivationFunctionType
AX = mybir.AxisListType

P = 128
TT = 2
SEQ = TT * P
D = 1024
KD = D // P
DEPTH = 2
HD = 64
DIL = (1, 4, 16)
DIL_WINDOW = (128, 512, 2048)
NG, HG = 3, 4
QKV1 = 3072
FF1 = 2816
FB = 256
NFB = FF1 // FB
FF2 = 4096
MB = 512
NMB = FF2 // MB
EV_COLS = 2760
OD_COLS = 1280
HA, HB, HC, HX = 8, 4, 16, 4
TOPK = 64
NBUCKET = 32
NBIAS = HA + HB + HC
BIG = 1e30
SENTINEL = -3e38
SCALE = HD ** -0.5
EPS1, EPS2 = 1e-5, 1e-6
LAM_INIT = 0.8 - 0.6
TWO_PI = 2.0 * np.pi
PI_HI, PI_MID = 6.28125, float(np.float32(TWO_PI - 6.28125))
PI_LO = float(np.float32(TWO_PI - 6.28125 - np.float64(np.float32(TWO_PI - 6.28125))))
ROUND = 12582912.0

CH = 2048
RAW = 3
HALF = CH // 2
HL = 4

C_ID, C_ONE, C_TRI, C_SBM, C_ADM, C_HOT, C_INV = 0, 128, 256, 384, 768, 1024, 1536
C_COLS = 1544
M_COLS = 3 * P + 3 * SEQ
BAND_W = 512
PITCH = 512


def shape_constants():
    c = np.zeros((P, C_COLS), np.float32)
    i = np.arange(P)
    c[:, C_ID:C_ID + P] = np.eye(P)
    c[:, C_ONE:C_ONE + P] = 1.0
    c[:, C_TRI:C_TRI + P] = i[:, None] >= i[None, :]
    q = np.arange(SEQ)
    c[:, C_SBM:C_SBM + SEQ] = BIG * (i[:, None] >= q[None, :])
    c[:, C_SBM + SEQ:C_SBM + SEQ + P] = BIG * (i[:, None] >= i[None, :])
    c[:64, C_ADM + 192:C_ADM + 256] = -BIG
    r = np.arange(383)
    rel = r - 255
    n = np.abs(rel)
    nf = np.maximum(n, 1).astype(np.float32)
    large = 8 + (np.log(nf / np.float32(8)) / np.float32(np.log(128.0)) * np.float32(8)).astype(np.int32)
    bucket = np.where(rel > 0, 16, 0) + np.where(n < 8, n, np.minimum(large, 15))
    c[bucket, C_HOT + r] = 1.0
    inv = np.float32(500000.0) ** (-np.arange(0, 16, 2, dtype=np.float32) / np.float32(16))
    c[:, C_INV:C_INV + 8] = inv
    m = np.zeros((P, M_COLS), np.float32)
    for qt in range(TT):
        nk = P * (qt + 1)
        for g in range(NG):
            gap = (qt * P + i)[:, None] - np.arange(nk)[None, :]
            ok = (gap >= 0) & (gap <= DIL_WINDOW[g]) & (gap % DIL[g] == 0)
            at = (0, 3 * P)[qt] + g * nk
            m[:, at:at + nk] = BIG * ~ok
    return c, m


class Plan:

    def __init__(self):
        self.chunks = []
        self.jobs = {}
        self.landed = []
        self.slot_total = [0] * RAW
        self.groups = {}
        self.by_number = []
        self.n_act = self.n_dve = 0

    def job(self, key, pieces):
        ids = []
        for kc, n, srcs in pieces:
            s = len(self.chunks) % RAW
            self.slot_total[s] += 16 * len(srcs)
            ids.append(len(self.chunks))
            self.chunks.append((kc, n, srcs))
            self.landed.append(self.slot_total[s])
        self.jobs[key] = ids

    def group(self, key, mode):
        self.n_act += mode in ("act", "split")
        self.n_dve += mode in ("dve", "split")
        self.groups[key] = len(self.by_number)
        self.by_number.append((mode, self.n_act, self.n_dve))


def build_network(nc, a, out):
    plan = Plan()

    def rows(w, k0, kc, c0, n):
        return w[k0 * P:(k0 + kc) * P, c0:c0 + n].rearrange("(k p) n -> p k n", p=P)

    def wide(w, c0, n):
        return [(KD // 2, n, [(0, n, rows(w, k, KD // 2, c0, n))]) for k in (0, KD // 2)]

    def tall(w, r0, k):
        return [(2, D, [(0, D, rows(w, r0 // P + j, 2, 0, D))]) for j in range(0, k, 2)]

    plan.group("gains", "act")
    plan.group("conv", "act")
    plan.group("bias", "act")
    for l in range(DEPTH):
        w = a["w_in"][l]
        for g in range(4):
            plan.group(("x1", l, g), "split")
        for j in range(10):
            plan.job(("in1", l, j), wide(w, 512 * j, 512))
        for g in range(8):
            plan.group(("qk1", l, g), "act" if g % 2 else "dve")
        for g in ("a", "b"):
            plan.group(("y1", l, g), "split")
        plan.job(("pa", l), tall(a["w_proj_a"][l], 0, 2))
        plan.job(("pb", l), tall(a["w_proj_b"][l], 0, 2))
        for g in range(4):
            plan.group(("mix", l, g), "split")
        for j in range(2):
            plan.job(("out1", l, j), wide(a["w_out"][l], 512 * j, 512))
        for g in range(4):
            plan.group(("xf", l, g), "split")

        def up(b):
            w = a["w_up"][l]
            plan.job(("up", l, b), [(4, 2 * FB, [(0, FB, rows(w, k, 4, b * FB, FB)),
                                                (FB, FB, rows(w, k, 4, FF1 + b * FB, FB))]) for k in (0, 4)])

        def down(b):
            plan.job(("down", l, b), tall(a["w_down"][l], b * FB, 2))

        up(0)
        for b in range(NFB):
            plan.group(("ta", l, b), "dve")
            plan.group(("tb", l, b), "dve")
            if b + 1 < NFB:
                up(b + 1)
            if b:
                down(b - 1)
        down(NFB - 1)
    for l in range(DEPTH):
        even = l % 2 == 0
        for g in range(4):
            plan.group(("x2", l, g), "split")
        w, cols = (a["ev_w_in_2"][0], EV_COLS) if even else (a["od_w_in_2"][0], OD_COLS)
        nj = -(-cols // 512)
        for j in range(nj):
            plan.job(("in2", l, j), wide(w, 512 * j, min(512, cols - 512 * j)))
        for g in range(4):
            plan.group(("mem", l, g), "split")
        plan.job(("kv", l), wide(a["xa_wkv_2"][l], 0, 512))
        if even:
            for g in range(2):
                plan.group(("qi", l, g), "act")
            plan.group(("ki", l), "act")
            for qt in range(TT):
                for g in range(HA // 2):
                    plan.group(("idx", l, qt, g), "act")
            for g in range(4):
                plan.group(("qkb", l, g), "act")
            for g in range(2):
                plan.group(("qa", l, g), "act")
            plan.group(("uk", l), "act")
            for g in range(2):
                plan.group(("ka", l, g), "act")
            for t in range(TT):
                plan.group(("va", l, t), "act")
        else:
            for g in range(5):
                plan.group(("qk2", l, g), "act" if g % 2 else "dve")
        for g in range(4):
            plan.group(("o2", l, g), "split")
        w = a["ev_w_out_2"][0] if even else a["od_w_out_2"][0]
        for j in range(2):
            plan.job(("out2", l, j), wide(w, 512 * j, 512))
        for g in range(4):
            plan.group(("xx", l, g), "split")
        plan.job(("wq", l), wide(a["xa_wq_2"][l], 0, 256))
        for g in range(2):
            plan.group(("qkx", l, g), "act" if g % 2 else "dve")
        plan.group(("ox", l), "split")
        plan.job(("wo", l), tall(a["xa_wo_2"][l], 0, 2))
        for g in range(4):
            plan.group(("xm", l, g), "split")
        plan.job(("w1", l, 0), wide(a["mlp_w1_2"][l], 0, MB))
        for b in range(NMB):
            for g in range(2):
                plan.group(("tm", l, b, g), "split")
            if b + 1 < NMB:
                plan.job(("w1", l, b + 1), wide(a["mlp_w1_2"][l], MB * (b + 1), MB))
            plan.job(("w2", l, b), tall(a["mlp_w2_2"][l], MB * b, MB // P))
    NCH = len(plan.chunks)

    norms = []
    for l in range(DEPTH):
        norms += [("x1", l), ("xf", l)]
    norms += [("final",), ]
    for l in range(DEPTH):
        norms += [("x2", l), ("mem", l)] + ([("ckv", l)] if l % 2 == 0 else [])
        norms += [("sub", l)] * (l % 2 == 0)
        norms += [("y2", l), ("xx", l), ("yx", l), ("xm", l), ("ym", l)]
    NORM = {k: i for i, k in enumerate(norms)}
    GAIN_ROWS = 18
    gain_row = {}
    for l in range(DEPTH):
        gain_row["x1", l] = l
        gain_row["xf", l] = 2 + l
        gain_row["x2", l], gain_row["xx", l], gain_row["xm", l] = 4 + 6 * l, 6 + 6 * l, 8 + 6 * l
        gain_row["mem", l] = 16 + l

    with ExitStack() as ctx:
        def sb(name, shape, dt=F32):
            return ctx.enter_context(nc.sbuf_tensor(name, shape, dt))

        def sem(name):
            return ctx.enter_context(nc.semaphore(name))

        cst = sb("cst", [P, C_COLS])
        raw = sb("raw", [P, RAW, CH])
        whi = sb("whi", [P, HL, HALF], F32R)
        wlo = sb("wlo", [P, HL, HALF], F32R)
        x = sb("x", [P, TT, D])
        ahi = sb("ahi", [P, KD, SEQ], F32R)
        alo = sb("alo", [P, KD, SEQ], F32R)
        mhi = sb("mhi", [P, KD, SEQ], F32R)
        mlo = sb("mlo", [P, KD, SEQ], F32R)
        proj = sb("proj", [P, TT, QKV1])
        region = sb("region", [P, 7296])
        qT = sb("qT", [P, 16, SEQ])
        work = sb("work", [P, 4608])
        o_nat = sb("o_nat", [P, TT, D])
        gain_b = sb("gain_b", [P, D])
        misc = sb("misc", [P, 528])
        gains = sb("gains", [P, KD, GAIN_ROWS])
        conv = sb("conv", [P, FF1 // P, 8])
        ss = sb("ss", [P, len(norms), 4])
        rstd = sb("rstd", [P, len(norms), 4])
        small = sb("small", [P, 16, 16])
        pos_i = sb("pos_i", [P, TT], I32)
        den = sb("den", [P, TT, 16])
        rden = sb("rden", [P, TT, 16])
        low = sb("low", [P, TT, 16])
        ps = ctx.enter_context(nc.psum_tensor("ps", [P, 8, 512], F32))
        band_dram = nc.dram_tensor("band", [NBIAS, P * (PITCH + 1) + PITCH], F32, kind="Internal").ap()

        ident = cst[:, C_ID:C_ID + P]
        ones = cst[:, C_ONE:C_ONE + P]
        tri = cst[:, C_TRI:C_TRI + P]
        gates = region[:, 0:4096].rearrange("p (t n) -> p t n", t=TT)
        gate_bias = region[:, 4096:6144]
        dil_mask = region[:, 6144:6144 + M_COLS]
        band = region[:, 0:4096].rearrange("p (h c) -> p h c", h=16)
        kvn = region[:, 4096:5120].rearrange("p (t n) -> p t n", t=TT)
        qiT = region[:, 3072:4096].rearrange("p (b n) -> p b n", b=4)
        kicT = region[:, 5120:5632].rearrange("p (b n) -> p b n", b=2)
        relu_i = region[:, 5632:6656].rearrange("p (s n) -> p s n", s=2)
        sel = region[:, 6656:7040]
        cand = region[:, 7040:7296]
        sc = work[:, 0:1536].rearrange("p (s n) -> p s n", s=2)
        ex = work[:, 1536:3072].rearrange("p (s n) -> p s n", s=2)
        eT = work[:, 3072:4608].rearrange("p (s n) -> p s n", s=2)
        nat = work[:, 0:2048].rearrange("p (s t n) -> p s t n", s=2, t=TT)
        cv = work[:, 2048:2560]
        sl = work[:, 2560:3072]
        ut = work[:, 3072:3584]
        junk = work[:, 3072:4096]
        junk_act = work[:, 0:2048].rearrange("p (i n) -> p i n", i=4)
        ystep = work[:, 2048:4096].rearrange("p (t n) -> p t n", t=TT)
        rt = work[:, 0:1536].rearrange("p (i t h d) -> p i t h d", i=4, t=TT, h=24)
        gain_rows = work[0:GAIN_ROWS, 0:1024]
        conv_rows = work[0:8, 1024:1024 + FF1]
        band_rows = work[0:NBIAS, 4096:4608]
        uk_nat = work[:, 0:512].rearrange("p (b n) -> p b n", b=4)
        ukT = work[:, 512:1024].rearrange("p (b n) -> p b n", b=4)
        uv = work[:, 1024:1536]
        kdup = work[:, 1536:2048]
        lam_rows = misc[:, 0:256]
        subln = misc[:, 256:384]
        akv = misc[:, 384:512]
        sinks = misc[:, 512:528]

        landed = [sem(f"landed{i}") for i in range(RAW)]
        cst_in = sem("cst_in")
        x_in = sem("x_in")
        rows_in = sem("rows_in")
        mask_in = sem("mask_in")
        bgate_in = sem("bgate_in")
        gainb_in = sem("gainb_in")
        mem_in = sem("mem_in")
        misc_in = sem("misc_in")
        small_w_in = sem("small_w_in")
        band_out = sem("band_out")
        band_in = sem("band_in")
        stored = sem("stored")
        hi_done = sem("hi_done")
        lo_done = sem("lo_done")
        pe_out = sem("pe_out")
        pe_grp = sem("pe_grp")
        grp_act = sem("grp_act")
        grp_dve = sem("grp_dve")
        ev_act = sem("ev_act")
        ev_dve = sem("ev_dve")
        x_ready = sem("x_ready")
        ss_ready = sem("ss_ready")
        rstd_ready = sem("rstd_ready")
        pool_chain = sem("pool_chain")
        chain = sem("chain")
        act_chain = sem("act_chain")
        rope_done = sem("rope_done")
        trig_arg = sem("trig_arg")
        trig_done = sem("trig_done")
        gate_pre = sem("gate_pre")
        gate_done = sem("gate_done")
        at_s = sem("at_s")
        at_t = sem("at_t")
        at_e = sem("at_e")
        at_x = sem("at_x")
        at_ya = sem("at_ya")
        at_yd = sem("at_yd")
        at_o = sem("at_o")
        o_ready = sem("o_ready")
        sb_z = sem("sb_z")
        sb_abs = sem("sb_abs")
        sb_ln = sem("sb_ln")
        sb_keep = sem("sb_keep")
        sb_sum = sem("sb_sum")
        sb_arg = sem("sb_arg")
        sb_att = sem("sb_att")
        sb_o = sem("sb_o")
        mixed = sem("mixed")
        silu_ready = sem("silu_ready")
        uhi = sem("uhi")
        ulo = sem("ulo")
        sq_ready = sem("sq_ready")
        relu_ready = sem("relu_ready")
        idx_used = sem("idx_used")
        sel_ready = sem("sel_ready")
        c_ready = sem("c_ready")
        kdup_ready = sem("kdup_ready")
        lam_arg = sem("lam_arg")
        lam_exp = sem("lam_exp")
        sink_arg = sem("sink_arg")
        sink_exp = sem("sink_exp")
        sub_sq = sem("sub_sq")
        block = ctx.enter_context(nc.Block())

        def yb(tt, c):
            return 2 * tt + c % 2

        def unit(qt, slot, w, parts, bias, pv, o_bank, o_col, sel_mask=None):
            return dict(qt=qt, slot=slot, w=w, parts=parts, bias=bias, pv=pv, o_bank=o_bank, o_col=o_col, sel=sel_mask)

        def half(i):
            return 64 * (i % 2)

        def dilated_units():
            us = []
            for qt in range(TT):
                nk = P * (qt + 1)
                for h in range(HG):
                    parts, pv = [], []
                    for g in range(NG):
                        i = g * HG + h
                        b = half(i)
                        parts.append((g * nk, nk, qT[b:b + 64, i // 2, qt * P:qt * P + P], qT[b:b + 64, 6 + i // 2, 0:nk]))
                        pv += [proj[:, s, 1536 + i * HD:1536 + i * HD + HD] for s in range(qt + 1)]
                    at = (0, 3 * P)[qt]
                    us.append(unit(qt, h, 3 * nk, parts, dil_mask[:, at:at + 3 * nk], pv, 6 + qt, h * HD))
            return us

        def head_units(heads):
            us = []
            for qt in range(TT):
                for (q, k, nk_of, bias, v, slot, vw, m) in heads:
                    nk = nk_of(qt)
                    parts = [(0, nk, q(qt), k(nk))]
                    pv = [v(s) for s in range(nk // P)]
                    col = slot * vw
                    us.append(unit(qt, slot, nk, parts, bias(qt, nk), pv, (6, 2)[qt] + col // 512, col % 512,
                                   sel[:, (0, P)[qt]:(0, P)[qt] + nk] if m else None))
            return us

        def causal(qt):
            return P * (qt + 1)

        def band_of(h):
            return lambda qt, nk: band[:, h, SEQ - nk:SEQ]

        def even_heads():
            hs = []
            for i in range(2 * HB):
                b = half(i)
                hs.append((lambda qt, i=i, b=b: qT[b:b + 64, i // 2, qt * P:qt * P + P],
                           lambda nk, i=i, b=b: qT[b:b + 64, 4 + i // 2, 0:nk], causal, band_of(HA + i // 2),
                           lambda s, i=i: proj[:, s, 2248 + P * (i // 2):2248 + P * (i // 2) + P], i, P, False))
            return hs

        def dsa_heads():
            hs = []
            for i in range(HA):
                b = half(i)
                hs.append((lambda qt, i=i, b=b: qT[b:b + 64, 8 + i // 2, qt * P:qt * P + P],
                           lambda nk, i=i, b=b: qT[b:b + 64, 12 + i // 2, 0:nk], causal, band_of(i),
                           lambda s, i=i: proj[:, s, HD * i:HD * i + HD], i, HD, True))
            return hs

        def odd_heads():
            hs = []
            for i in range(HC):
                b, kv = half(i), i // 8
                hs.append((lambda qt, i=i, b=b: qT[b:b + 64, i // 2, qt * P:qt * P + P],
                           lambda nk, kv=kv, b=b: qT[b:b + 64, 8 + kv, 0:nk], causal, band_of(i),
                           lambda s, kv=kv: proj[:, s, 1152 + HD * kv:1152 + HD * kv + HD], i, HD, False))
            return hs

        def cross_heads():
            hs = []
            for i in range(HX):
                b = half(i)
                hs.append((lambda qt, i=i, b=b: qT[b:b + 64, i // 2, qt * P:qt * P + P],
                           lambda nk, i=i, b=b: qT[b:b + 64, 2 + i // 2, 0:nk], lambda qt: SEQ, lambda qt, nk: None,
                           lambda s, i=i: kvn[:, s, 256 + HD * i:256 + HD * i + HD], i, HD, False))
            return hs

        stages = []
        for l in range(DEPTH):
            stages.append((("dil", l), dilated_units()))
        for l in range(DEPTH):
            if l % 2 == 0:
                stages += [(("diff", l), head_units(even_heads())), (("dsa", l), head_units(dsa_heads()))]
            else:
                stages.append((("odd", l), head_units(odd_heads())))
            stages.append((("cross", l), head_units(cross_heads())))
        first_unit, n_units = {}, 0
        units_of = {}
        for k, us in stages:
            for d in us:
                d["wide"] = us[-1]["w"] > SEQ
            first_unit[k], units_of[k] = n_units, us
            n_units += len(us)

        def copies(u):
            return u // 2 + 1, (u + 1) // 2

        def wait_copied(eng, u):
            d, s = copies(u)
            if u % 2 == 0:
                eng.wait_ge(at_yd, d)
            else:
                eng.wait_ge(at_ya, s)

        def x_count(what, l=0):
            if what == "mix":
                return 2 * (2 * l + 1)
            if what == "ffn":
                return 2 * (2 * l + 2)
            if what == "final":
                return 2 * (2 * DEPTH + 1)
            return 2 * (2 * DEPTH + 1 + 3 * l + ("y2", "yx", "ym").index(what) + 1)


        def evs_act(l, what, b=None):
            per1 = 2 * (6 + NFB)
            if b is not None:
                return per1 * l + 12 + 2 * (b + 1)
            return per1 * l + 2 * (what + 1)

        def evs_act2(l, what, j=0):
            base = 2 * (6 + NFB) * DEPTH
            for i in range(l):
                base += 2 * (-(-(EV_COLS if i % 2 == 0 else OD_COLS) // 512) + 2)
            nj = -(-(EV_COLS if l % 2 == 0 else OD_COLS) // 512)
            return base + 2 * (("in2", "kv", "wq").index(what) and nj + ("kv", "wq").index(what) + 1 or j + 1)

        def wait_product(eng, l, j):
            if j < 6:
                eng.wait_ge(ev_act, evs_act(l, j))
            else:
                eng.wait_ge(gate_pre, 8 * l + 2 * (j - 5))

        order = [(k, l) for l in range(DEPTH) for k in ("dil", "sb")]
        order += [("diff", 0), ("dsa", 0), ("cross", 0), ("odd", 1), ("cross", 1)]
        o_counts = {k: 2 * (i + 1) for i, k in enumerate(order)}

        rs_count, total = {}, 0
        for k in norms:
            total += 2 if k[0] == "sub" else 1
            rs_count[k] = total

        def sbk(h):
            return work[:, 3072 + 384 * h:3072 + 384 * (h + 1)]

        def sba(h):
            return work[:, 1536 + 384 * h:1536 + 384 * (h + 1)]

        def sbz(h):
            return work[:, 384 * h:384 * (h + 1)]

        def kdup2(tt, kv):
            return kdup[:, (2 * tt + kv) * P:(2 * tt + kv + 1) * P]

        def turned(u, d):
            if d["w"] > SEQ or d["wide"]:
                return ps[:, 4:6, :].rearrange("p b n -> p (b n)")[:, 0:d["w"]]
            return ps[:, 4 + u % 2, 0:d["w"]]

        def group_ready(eng, key):
            eng.wait_ge(pe_grp, plan.groups[key] + 1)

        @block.sync
        def _(sp):
            sp.dma_start(cst[:], a["cst"]).then_inc(cst_in, 16)
            sp.dma_start(x[:], a["x"][0].rearrange("(t p) d -> p t d", p=P)).then_inc(x_in, 16)
            for l in range(DEPTH):
                for i, name in enumerate(("norm_mix", "norm_ffn")):
                    sp.dma_start(gain_rows[2 * i + l:2 * i + l + 1, :], a[name][l:l + 1, :]).then_inc(rows_in, 16)
            sp.dma_start(gain_rows[4:16, :], a["norm_g_2"].rearrange("l i d -> (l i) d")).then_inc(rows_in, 16)
            sp.dma_start(gain_rows[16:18, :], a["xa_mem_norm_2"]).then_inc(rows_in, 16)
            sp.dma_start(conv_rows[0:6, :], a["conv_w"].rearrange("l i d -> (l i) d")).then_inc(rows_in, 16)
            sp.dma_start(conv_rows[6:8, :], a["conv_b"]).then_inc(rows_in, 16)
            sp.dma_start(work[0:NBUCKET, 3840:3840 + NBIAS], a["rel_bias_table_2"]).then_inc(rows_in, 16)
            for n in range(NCH):
                kc, cols, srcs = plan.chunks[n]
                if n >= RAW:
                    sp.wait_ge(hi_done, 2 * (n - RAW + 1))
                    sp.wait_ge(lo_done, 2 * (n - RAW + 1))
                dst = raw[:, n % RAW, 0:kc * cols].rearrange("p (k n) -> p k n", k=kc)
                for c0, w, src in srcs:
                    sp.dma_start(dst[:, :, c0:c0 + w], src).then_inc(landed[n % RAW], 16)
            sp.wait_ge(x_ready, x_count("ym", DEPTH - 1))
            sp.dma_start(out[0].rearrange("(t p) d -> p t d", p=P), x[:]).then_inc(stored, 16)
            sp.wait_ge(stored, 16)

        @block.gpsimd
        def _(pool):
            pool.dma_start(pos_i[:], a["positions"].rearrange("a (t p) -> p (a t)", p=P),
                           allow_slow_non_contiguous=True).then_inc(misc_in, 16)
            pool.dma_start(dil_mask, a["masks"]).then_inc(mask_in, 16)
            pool.dma_start(gate_bias, a["b_gate"][0].partition_broadcast(P)).then_inc(bgate_in, 16)
            pool.dma_start(gain_b[:], a["norm_final"].partition_broadcast(P)).then_inc(gainb_in, 16)
            n_chain = [0]

            def link(ins):
                n_chain[0] += 1
                ins.then_inc(pool_chain, 1)
                pool.wait_ge(pool_chain, n_chain[0])

            link(nc.gpsimd.memset(small[:, 0, :], -0.5))
            n_ss = [0]

            def root(key, width, count, eps, halves=False, cols=4):
                i = NORM[key]
                n_ss[0] += count
                pool.wait_ge(ss_ready, n_ss[0])
                if halves:
                    link(nc.gpsimd.tensor_tensor(ss[:, i, 0:2], ss[:, i, 0:2], ss[:, i, 2:4], ALU.add))
                    cols = 2
                link(nc.gpsimd.tensor_scalar(ss[:, i, 0:cols], ss[:, i, 0:cols], 1.0 / width, eps, ALU.mult, ALU.add))
                nc.gpsimd.tensor_tensor(rstd[:, i, 0:cols], ss[:, i, 0:cols], small[:, 0, 0:cols], ALU.pow).then_inc(rstd_ready, 1)

            pool.wait_ge(grp_act, 3)
            pool.dma_start(bass.AP(band_dram.tensor, 0, [[P * (PITCH + 1) + PITCH, NBIAS], [PITCH + 1, P], [1, PITCH]]),
                           band_rows.unsqueeze(1).to_broadcast([NBIAS, P, PITCH])).then_inc(band_out, 16)

            def band_load(h0, n):
                return bass.AP(band_dram.tensor, h0 * (P * (PITCH + 1) + PITCH) + P - 1,
                               [[PITCH, P], [P * (PITCH + 1) + PITCH, n], [1, SEQ]])

            for l in range(DEPTH):
                root(("x1", l), D, 2, EPS1, cols=2)
                if l == 0:
                    pool.wait_ge(gate_pre, 8)
                    pool.dma_start(gate_bias, a["b_gate"][1].partition_broadcast(P)).then_inc(bgate_in, 16)
                root(("xf", l), D, 2, EPS1, cols=2)
            root(("final",), D, 2, EPS1, cols=2)
            n_final = x_count("final")
            pool.wait_ge(x_ready, n_final)
            pool.wait_ge(band_out, 16)
            pool.dma_start(band[:, 0:12, :], band_load(0, 12)).then_inc(band_in, 16)
            pool.dma_start(o_nat[:], a["mem_2"][0].rearrange("(t p) d -> p t d", p=P)).then_inc(mem_in, 16)
            pool.dma_start(gain_b[:], a["norm_g_2"][0, 1].partition_broadcast(P)).then_inc(gainb_in, 16)
            pool.dma_start(lam_rows, a["ev_b_lambda_2"][0].rearrange("a d -> (a d)").partition_broadcast(P)).then_inc(misc_in, 16)
            pool.dma_start(subln, a["ev_b_subln_2"][0].partition_broadcast(P)).then_inc(misc_in, 16)
            pool.dma_start(akv, a["ev_a_kv_norm_2"][0].partition_broadcast(P)).then_inc(misc_in, 16)
            pool.dma_start(sinks, a["od_sinks_2"][0].partition_broadcast(P)).then_inc(misc_in, 16)
            root(("x2", 0), D, 2, EPS2, cols=2)
            pool.dma_start(uk_nat, a["ev_a_w_uk_2"][0].rearrange("(b h) d l -> (h d) b l", h=2)).then_inc(small_w_in, 16)
            pool.dma_start(uv.rearrange("p (h d) -> p h d", h=HA), a["ev_a_w_uv_2"][0].rearrange("h l d -> l h d")).then_inc(small_w_in, 16)
            for l in range(DEPTH):
                if l > 0:
                    pool.wait_ge(x_ready, x_count("ym", l - 1))
                    pool.dma_start(gain_b[:], a["norm_g_2"][l, 1].partition_broadcast(P)).then_inc(gainb_in, 16)
                    pool.dma_start(band[:, 0:16, :], band_load(HA + HB, HC)).then_inc(band_in, 16)
                    pool.dma_start(o_nat[:], a["mem_2"][0].rearrange("(t p) d -> p t d", p=P)).then_inc(mem_in, 16)
                    root(("x2", l), D, 2, EPS2, cols=2)
                root(("mem", l), D, 2, EPS2, cols=2)
                if l % 2 == 0:
                    root(("ckv", l), P, 2, EPS2, cols=2)
                    for qt in range(TT):
                        i = NORM["sub", l]
                        n_ss[0] += 1
                        pool.wait_ge(ss_ready, n_ss[0])
                        t = small[:, 2 + qt, 0:HB]
                        link(nc.gpsimd.tensor_scalar(t, t, 1.0 / P, EPS2, ALU.mult, ALU.add))
                        nc.gpsimd.tensor_tensor(small[:, 4 + qt, 0:HB], t, small[:, 0, 0:HB], ALU.pow).then_inc(rstd_ready, 1)
                for k, key in enumerate(("y2", "yx", "ym")):
                    root((key, l), D, 4, EPS2, halves=True)
                    pool.wait_ge(x_ready, x_count(key, l))
                    if k < 2:
                        pool.dma_start(gain_b[:], a["norm_g_2"][l, 3 + 2 * k].partition_broadcast(P)).then_inc(gainb_in, 16)
                        root((("xx", "xm")[k], l), D, 2, EPS2, cols=2)

        @block.tensor
        def _(pe):
            def half_chunk(n, h, hi, lo, k0, outs, first, final, stream=None):
                kc, cols, _ = plan.chunks[n]
                kh, m = kc // 2, 2 * n + h
                last_group = (k0 + (h + 1) * kh - 1) // 2
                if stream:
                    stream["need"](last_group)
                pe.wait_ge(lo_done, m + 1)
                wh = whi[:, m % HL, 0:kh * cols].rearrange("p (k n) -> p k n", k=kh)
                wl = wlo[:, m % HL, 0:kh * cols].rearrange("p (k n) -> p k n", k=kh)
                for tt in range(TT):
                    rows_ = slice(tt * P, tt * P + P)
                    for k in range(kh):
                        kx = k0 + h * kh + k
                        for c0, w, bank in outs[tt]:
                            o = ps[:, bank, 0:w]
                            nc.tensor.matmul(o, hi[:, kx, rows_], wh[:, k, c0:c0 + w], start=first and h == 0 and k == 0, stop=False)
                        for c0, w, bank in outs[tt]:
                            o = ps[:, bank, 0:w]
                            nc.tensor.matmul(o, hi[:, kx, rows_], wl[:, k, c0:c0 + w], start=False, stop=False)
                        for c0, w, bank in outs[tt]:
                            o = ps[:, bank, 0:w]
                            mm = nc.tensor.matmul(o, lo[:, kx, rows_], wh[:, k, c0:c0 + w], start=False,
                                                  stop=final and h == 1 and k == kh - 1)
                    mm.then_inc(pe_out, 1)
                if stream:
                    stream["turn_to"](last_group + 2)

            def wide_job(key, hi, lo, banks, n=512, stream=None, between=None):
                ids = plan.jobs[key]
                for j, i in enumerate(ids):
                    if between and j == 1:
                        between()
                    for h in range(2):
                        half_chunk(i, h, hi, lo, j * (KD // 2), [[(0, n, banks[tt])] for tt in range(TT)], j == 0, j == len(ids) - 1, stream)

            def tall_job(key, hi, lo, k0, bank, first, final, between=None, stream=None):
                ids = plan.jobs[key]
                for j, i in enumerate(ids):
                    outs = [[(0, 512, bank(tt, 0)), (512, 512, bank(tt, 1))] for tt in range(TT)]
                    for h in range(2):
                        half_chunk(i, h, hi, lo, k0 + 2 * j, outs, first and j == 0, final and j == len(ids) - 1, stream)
                        if between and 2 * j + h == len(ids) - 1:
                            between()

            def group_bank(key):
                t = plan.groups[key]
                if t >= 2:
                    mode, na, nd = plan.by_number[t - 2]
                    if mode == "act":
                        pe.wait_ge(grp_act, na)
                    else:
                        pe.wait_ge(grp_dve, nd)
                return ps[:, 4 + t % 2, :]

            def turn_blocks(key, srcs):
                bank = group_bank(key)
                for j, src in enumerate(srcs):
                    mm = nc.tensor.transpose(bank[:, j * P:j * P + P], src, ident)
                mm.then_inc(pe_grp, 1)

            def stream(tag, l, src, ready):
                turned, waited = [0], [0]

                def turn_to(g):
                    while turned[0] <= min(g, 3):
                        t = turned[0]
                        if t % 2 == 0:
                            ready(t // 2)
                        turn_blocks((tag, l, t), [src[:, tt, (2 * t + b) * P:(2 * t + b + 1) * P] for b in range(2) for tt in range(TT)])
                        turned[0] += 1

                def need(g):
                    while waited[0] <= g:
                        turn_to(waited[0] + 1)
                        pe.wait_ge(grp_dve, plan.by_number[plan.groups[tag, l, waited[0]]][2])
                        waited[0] += 1

                return dict(turn_to=turn_to, need=need)

            def x_half(n):
                return lambda h: pe.wait_ge(x_ready, n - 1 + h)

            def attention(key):
                us, u0 = units_of[key], first_unit[key]
                wide_units = us[-1]["w"] > SEQ

                def s_bank(u):
                    return 2 * (u % 2) if wide_units else u % 2

                def scores(i):
                    u, d = u0 + i, us[i]
                    if u >= 2:
                        pe.wait_ge(at_t, u - 1)
                    flat = ps[:, s_bank(u):s_bank(u) + (2 if wide_units else 1), :].rearrange("p b n -> p (b n)")
                    for c0, n, q, k in d["parts"]:
                        mm = nc.tensor.matmul(flat[:, c0:c0 + n], q, k, start=True, stop=d["sel"] is None)
                    if d["sel"] is not None:
                        mm = nc.tensor.matmul(flat[:, 0:d["w"]], ident, d["sel"], start=False, stop=True)
                    mm.then_inc(at_s, 1)

                def turn(i):
                    u, d = u0 + i, us[i]
                    pe.wait_ge(at_e, u + 1)
                    back = 1 if wide_units else 2
                    if u >= back:
                        wait_copied(pe, u - back)
                    for b in range(d["w"] // P):
                        at = b * P
                        o = ps[:, 4 + at // 512, at % 512:at % 512 + P] if wide_units else ps[:, 4 + u % 2, at:at + P]
                        mm = nc.tensor.transpose(o, ex[:, u % 2, at:at + P], ident)
                    mm.then_inc(at_x, 1)

                def values(i):
                    u, d = u0 + i, us[i]
                    wait_copied(pe, u)
                    vw = d["pv"][0].shape[-1]
                    o = ps[:, d["o_bank"], d["o_col"]:d["o_col"] + vw]
                    for b, v in enumerate(d["pv"]):
                        mm = nc.tensor.matmul(o, eT[:, u % 2, b * P:b * P + P], v, start=b == 0, stop=b == len(d["pv"]) - 1)
                    mm.then_inc(at_o, 1)

                n = len(us)
                for i in range(n + 3):
                    if i < n:
                        scores(i)
                    if 2 <= i < n + 2:
                        turn(i - 2)
                    if 3 <= i:
                        values(i - 3)

            pe.wait_ge(cst_in, 16)
            pe.wait_ge(rows_in, 16 * 9)
            bank = group_bank("gains")
            for k in range(KD):
                mm = nc.tensor.transpose(bank[:, k * GAIN_ROWS:(k + 1) * GAIN_ROWS], gain_rows[:, k * P:k * P + P], ident[0:GAIN_ROWS, 0:GAIN_ROWS])
            mm.then_inc(pe_grp, 1)
            bank = group_bank("conv")
            for k in range(FF1 // P):
                mm = nc.tensor.transpose(bank[:, k * 8:(k + 1) * 8], conv_rows[:, k * P:k * P + P], ident[0:8, 0:8])
            mm.then_inc(pe_grp, 1)
            bank = group_bank("bias")
            nc.tensor.matmul(bank[0:NBIAS, :], work[0:NBUCKET, 3840:3840 + NBIAS], cst[0:NBUCKET, C_HOT:C_HOT + BAND_W],
                             start=True, stop=True).then_inc(pe_grp, 1)

            for l in range(DEPTH):
                sx = stream("x1", l, x, x_half(x_count("ffn", l - 1)) if l else lambda h: pe.wait_ge(x_in, 16))
                for j in range(10):
                    if j >= 2:
                        wait_product(pe, l, j - 2)
                    wide_job(("in1", l, j), ahi, alo, [yb(0, j), yb(1, j)], stream=sx if j == 0 else None)
                pe.wait_ge(rope_done, l + 1)
                pe.wait_ge(ev_act, evs_act(l, 5))
                for g in range(8):
                    c0 = 2 * P * g if g < 6 else 2304 + 2 * P * (g - 6)
                    turn_blocks(("qk1", l, g), [proj[:, tt, c0 + b * P:c0 + (b + 1) * P] for b in range(2) for tt in range(TT)])
                pe.wait_ge(grp_act, plan.by_number[plan.groups["qk1", l, 7]][1])
                pe.wait_ge(grp_dve, plan.by_number[plan.groups["qk1", l, 7]][2])
                wait_product(pe, l, 8)
                wait_product(pe, l, 9)
                attention(("dil", l))
                pe.wait_ge(at_t, first_unit["dil", l] + len(units_of["dil", l]))
                for h in range(HG):
                    b, blk = half(h), 12 + h // 2
                    z = ps[:, h, 0:384]
                    nc.tensor.matmul(z[:, 0:SEQ], qT[b:b + 64, blk + 2, 0:P], qT[b:b + 64, blk, :], start=True, stop=True)
                    nc.tensor.matmul(z[:, SEQ:384], qT[b:b + 64, blk + 2, P:SEQ], qT[b:b + 64, blk, P:SEQ], start=True, stop=True).then_inc(sb_z, 1)
                pe.wait_ge(o_ready, o_counts["dil", l])
                for h in range(HG):
                    pe.wait_ge(sb_keep, HG * l + h + 1)
                    keep = sbk(h)
                    c = ps[:, h, 0:384]
                    nc.tensor.matmul(c[:, 0:P], tri, keep[:, 0:P], start=True, stop=True)
                    nc.tensor.matmul(c[:, P:SEQ], tri, keep[:, P:SEQ], start=True, stop=False)
                    nc.tensor.matmul(c[:, P:SEQ], ones, keep[:, SEQ:384], start=False, stop=True)
                    nc.tensor.matmul(c[:, SEQ:384], tri, keep[:, SEQ:384], start=True, stop=True).then_inc(sb_sum, 1)
                for h in range(HG):
                    pe.wait_ge(sb_att, HG * l + h + 1)
                    att = sba(h)
                    v = [proj[:, s, 2816 + h * HD:2816 + (h + 1) * HD] for s in range(TT)]
                    nc.tensor.matmul(ps[:, 6, h * HD:(h + 1) * HD], att[:, 0:P], v[0], start=True, stop=True)
                    nc.tensor.matmul(ps[:, 7, h * HD:(h + 1) * HD], att[:, P:SEQ], v[0], start=True, stop=False)
                    nc.tensor.matmul(ps[:, 7, h * HD:(h + 1) * HD], att[:, SEQ:384], v[1], start=False, stop=True).then_inc(sb_o, 1)
                pe.wait_ge(o_ready, o_counts["sb", l])
                for i, g in enumerate(("a", "b")):
                    turn_blocks(("y1", l, g), [o_nat[:, tt, 512 * i + b * P:512 * i + (b + 1) * P] for b in range(2) for tt in range(TT)])
                pe.wait_ge(grp_dve, plan.by_number[plan.groups["y1", l, "b"]][2])
                tall_job(("pa", l), mhi, mlo, 0, lambda tt, c: yb(tt, c), True, True)
                tall_job(("pb", l), mhi, mlo, 2, lambda tt, c: 4 + 2 * c + tt, True, True)
                sx = stream("mix", l, o_nat, lambda h: pe.wait_ge(mixed, 4 * l + 2 * h + 2))
                sf = stream("xf", l, x, x_half(x_count("mix", l)))
                wide_job(("out1", l, 0), mhi, mlo, [yb(0, 0), yb(1, 0)], stream=sx)
                wide_job(("out1", l, 1), mhi, mlo, [yb(0, 1), yb(1, 1)], between=lambda: sf["turn_to"](1))
                wide_job(("up", l, 0), ahi, alo, [6, 7], stream=sf)
                def turn_step(b):
                    pe.wait_ge(ev_act, evs_act(l, "up", b))
                    for i, t in enumerate(("ta", "tb")):
                        turn_blocks((t, l, b), [nat[:, b % 2, tt, i * FB + f * P:i * FB + (f + 1) * P] for f in range(2) for tt in range(TT)])

                def down(b, between=None):
                    pe.wait_ge(ulo, NFB * l + b + 1)
                    tall_job(("down", l, b), mhi, mlo, 2 * (b % 4), lambda tt, c: yb(tt, c), b == 0, b == NFB - 1, between)

                turn_step(0)
                for b in range(NFB):
                    if b + 1 < NFB:
                        wide_job(("up", l, b + 1), ahi, alo, [6, 7])
                    if b == 0:
                        turn_step(1)
                    elif b < NFB - 1:
                        down(b - 1, (lambda: turn_step(NFB - 1)) if b == NFB - 2 else None)
                        if b < NFB - 2:
                            turn_step(b + 1)
                    else:
                        down(b - 1)
                down(NFB - 1)

            for l in range(DEPTH):
                even = l % 2 == 0
                sx = stream("x2", l, x, x_half(x_count("final") if l == 0 else x_count("ym", l - 1)))
                cols = EV_COLS if even else OD_COLS
                nj = -(-cols // 512)
                for j in range(nj):
                    if j >= 2:
                        pe.wait_ge(ev_act, evs_act2(l, "in2", j - 2))
                    wide_job(("in2", l, j), mhi, mlo, [yb(0, j), yb(1, j)], min(512, cols - 512 * j), stream=sx if j == 0 else None)
                sm = stream("mem", l, o_nat, lambda h: pe.wait_ge(mem_in, 16 * (l + 1)))
                wide_job(("kv", l), ahi, alo, [6, 7], stream=sm)
                pe.wait_ge(ev_act, evs_act2(l, "in2", nj - 1))
                if even:
                    for g in range(2):
                        turn_blocks(("qi", l, g), [proj[:, tt, 640 + (2 * g + b) * P:640 + (2 * g + b + 1) * P] for b in range(2) for tt in range(TT)])
                    pe.wait_ge(kdup_ready, 1)
                    pe.wait_ge(c_ready, 2)
                    turn_blocks(("ki", l), [kdup[:, tt * P:tt * P + P] for tt in range(TT)] + [proj[:, tt, 512:640] for tt in range(TT)])
                    pe.wait_ge(grp_act, plan.by_number[plan.groups["ki", l]][1])
                    for qt in range(TT):
                        nk = causal(qt)
                        for g in range(HA // 2):
                            bank = group_bank(("idx", l, qt, g))
                            for i in range(2):
                                h = 4 * (g // 2) + g % 2 + 2 * i
                                b = half(h)
                                mm = nc.tensor.matmul(bank[:, i * SEQ:i * SEQ + nk], qiT[b:b + 64, h // 2, qt * P:qt * P + P],
                                                      kicT[b:b + 64, 0, 0:nk], start=True, stop=True)
                            mm.then_inc(pe_grp, 1)
                    for g in range(4):
                        c0 = 1224 + 2 * P * g
                        turn_blocks(("qkb", l, g), [proj[:, tt, c0 + b * P:c0 + (b + 1) * P] for b in range(2) for tt in range(TT)])
                    for g in range(2):
                        turn_blocks(("qa", l, g), [proj[:, tt, (2 * g + b) * P:(2 * g + b + 1) * P] for b in range(2) for tt in range(TT)])
                    pe.wait_ge(small_w_in, 32)
                    turn_blocks(("uk", l), [uk_nat[:, b, :] for b in range(4)])
                    pe.wait_ge(grp_act, plan.by_number[plan.groups["uk", l]][1])
                    for g in range(2):
                        bank = group_bank(("ka", l, g))
                        for b in range(2):
                            mm = nc.tensor.matmul(bank[:, b * SEQ:(b + 1) * SEQ], ukT[:, 2 * g + b, :], kicT[:, 1, :], start=True, stop=True)
                        mm.then_inc(pe_grp, 1)
                    for t in range(TT):
                        bank = group_bank(("va", l, t))
                        nc.tensor.matmul(bank, kicT[:, 1, t * P:t * P + P], uv, start=True, stop=True).then_inc(pe_grp, 1)
                    pe.wait_ge(grp_act, plan.by_number[plan.groups["va", l, 1]][1])
                    pe.wait_ge(ev_act, evs_act2(l, "kv"))
                    attention(("diff", l))
                    pe.wait_ge(o_ready, o_counts["diff", l])
                    pe.wait_ge(sel_ready, 2)
                    attention(("dsa", l))
                    pe.wait_ge(o_ready, o_counts["dsa", l])
                else:
                    pe.wait_ge(kdup_ready, 2)
                    for g in range(5):
                        srcs = ([proj[:, tt, (2 * g + b) * P:(2 * g + b + 1) * P] for b in range(2) for tt in range(TT)] if g < 4 else
                                [kdup2(tt, kv) for kv in range(2) for tt in range(TT)])
                        turn_blocks(("qk2", l, g), srcs)
                    pe.wait_ge(grp_dve, plan.by_number[plan.groups["qk2", l, 4]][2])
                    pe.wait_ge(grp_act, plan.by_number[plan.groups["qk2", l, 4]][1])
                    pe.wait_ge(ev_act, evs_act2(l, "kv"))
                    attention(("odd", l))
                    pe.wait_ge(o_ready, o_counts["odd", l])
                so = stream("o2", l, o_nat, lambda h: None)
                for j in range(2):
                    wide_job(("out2", l, j), ahi, alo, [yb(0, j), yb(1, j)], stream=so if j == 0 else None)
                wide_job(("wq", l), mhi, mlo, [6, 7], 256, stream=stream("xx", l, x, x_half(x_count("y2", l))))
                turn_blocks(("qkx", l, 0), [kvn[:, tt, b * P:(b + 1) * P] for b in range(2) for tt in range(TT)])
                pe.wait_ge(ev_act, evs_act2(l, "wq"))
                turn_blocks(("qkx", l, 1), [proj[:, tt, b * P:(b + 1) * P] for b in range(2) for tt in range(TT)])
                pe.wait_ge(grp_dve, plan.by_number[plan.groups["qkx", l, 1]][2])
                pe.wait_ge(grp_act, plan.by_number[plan.groups["qkx", l, 1]][1])
                attention(("cross", l))
                pe.wait_ge(o_ready, o_counts["cross", l])
                turn_blocks(("ox", l), [o_nat[:, tt, b * P:(b + 1) * P] for b in range(2) for tt in range(TT)])
                pe.wait_ge(grp_dve, plan.by_number[plan.groups["ox", l]][2])
                tall_job(("wo", l), mhi, mlo, 0, lambda tt, c: yb(tt, c), True, True)
                wide_job(("w1", l, 0), ahi, alo, [6, 7], stream=stream("xm", l, x, x_half(x_count("yx", l))))

                def turn_step2(b):
                    pe.wait_ge(sq_ready, 2 * (NMB * l + b + 1))
                    for g in range(2):
                        turn_blocks(("tm", l, b, g), [nat[:, b % 2, tt, (2 * g + f) * P:(2 * g + f + 1) * P] for f in range(2) for tt in range(TT)])

                for b in range(NMB):
                    if b < NMB - 1:
                        turn_step2(b)
                    if b + 1 < NMB:
                        wide_job(("w1", l, b + 1), ahi, alo, [6, 7])
                    pe.wait_ge(grp_dve, plan.by_number[plan.groups["tm", l, b, 1]][2])
                    tall_job(("w2", l, b), mhi, mlo, 4 * (b % 2), lambda tt, c: yb(tt, c), b == 0, b == NMB - 1,
                             (lambda: turn_step2(NMB - 1)) if b == NMB - 2 else None)

        @block.scalar
        def _(act):
            n_split = [0]
            n_link = [0]

            def link(ins):
                n_link[0] += 1
                ins.then_inc(act_chain, 1)
                act.wait_ge(act_chain, n_link[0])

            def split_half(m_last):
                while n_split[0] <= min(m_last, 2 * NCH - 1):
                    m = n_split[0]
                    n, h = divmod(m, 2)
                    kc, cols, _ = plan.chunks[n]
                    w = kc // 2 * cols
                    if h == 0:
                        act.wait_ge(landed[n % RAW], plan.landed[n])
                    if m >= HL:
                        act.wait_ge(pe_out, 2 * (m - HL + 1))
                    nc.scalar.copy(whi[:, m % HL, 0:w], raw[:, n % RAW, h * w:h * w + w]).then_inc(hi_done, 1)
                    n_split[0] += 1

            def split_to(n):
                split_half(2 * n + 1)

            def product(key, tt):
                act.wait_ge(pe_out, 4 * plan.jobs[key][-1] + 3 + tt)

            def scaled(key, norm, dst, n, banks, func=ACT.Copy, signal=ev_act):
                act.wait_ge(rstd_ready, rs_count[norm])
                for tt in range(TT):
                    product(key, tt)
                    nc.scalar.activation(dst(tt), ps[:, banks[tt], 0:n], func, scale=rstd[:, NORM[norm], tt:tt + 1]).then_inc(signal, 1)

            def stream_hi(tag, l, hi, row=None, gs=range(4)):
                for g in gs:
                    key = (tag, l, g)
                    group_ready(act, key)
                    bank = ps[:, 4 + plan.groups[key] % 2, :]
                    if row is None:
                        nc.scalar.copy(hi[:, 2 * g:2 * g + 2, :].rearrange("p b n -> p (b n)"), bank).then_inc(grp_act, 1)
                    else:
                        nc.scalar.activation(hi[:, 2 * g, :], bank[:, 0:SEQ], ACT.Copy, scale=gains[:, 2 * g, row:row + 1])
                        nc.scalar.activation(hi[:, 2 * g + 1, :], bank[:, SEQ:512], ACT.Copy,
                                             scale=gains[:, 2 * g + 1, row:row + 1]).then_inc(grp_act, 1)

            def take(key, dst, scale=1.0, cols=512, func=ACT.Copy):
                group_ready(act, key)
                bank = ps[:, 4 + plan.groups[key] % 2, 0:cols]
                nc.scalar.activation(dst, bank, func, scale=scale).then_inc(grp_act, 1)

            def blocks(t, b0, n=2):
                return t[:, b0:b0 + n, :].rearrange("p b n -> p (b n)")

            def attention(key, half_done=None):
                us, u0 = units_of[key], first_unit[key]
                n = len(us)
                for i in range(n + 2):
                    if i < n:
                        u, d = u0 + i, us[i]
                        act.wait_ge(at_t, u + 1)
                        if u >= 2:
                            act.wait_ge(at_x, u - 1)
                        s = d["slot"]
                        nc.scalar.activation(ex[:, u % 2, 0:d["w"]], sc[:, u % 2, 0:d["w"]], ACT.Exp, scale=-1.0,
                                             bias=low[:, d["qt"], s:s + 1], accum_out=den[:, d["qt"], s:s + 1]).then_inc(at_e, 1)
                    if i >= 2 and (u0 + i - 2) % 2 == 1:
                        u, d = u0 + i - 2, us[i - 2]
                        act.wait_ge(at_x, u + 1)
                        if u >= 2:
                            act.wait_ge(at_o, u - 1)
                        nc.scalar.copy(eT[:, u % 2, 0:d["w"]], turned(u, d)).then_inc(at_ya, 1)
                    if half_done and i == n // 2 + 5:
                        half_done(0)
                if half_done:
                    half_done(1)

            take("gains", gains[:].rearrange("p k r -> p (k r)"), cols=KD * GAIN_ROWS)
            take("conv", conv[:].rearrange("p k r -> p (k r)"), cols=8 * (FF1 // P))
            group_ready(act, "bias")
            nc.scalar.activation(band_rows, ps[0:NBIAS, 4 + plan.groups["bias"] % 2, :], ACT.Copy, scale=-1.0).then_inc(grp_act, 1)
            split_to(1)
            act.wait_ge(trig_arg, 1)
            nc.scalar.activation(small[:, 10:12, :], small[:, 8:10, :], ACT.Sin).then_inc(trig_done, 1)

            for l in range(DEPTH):
                stream_hi("x1", l, ahi, row=gain_row["x1", l])
                for j in range(10):
                    m = plan.jobs["in1", l, j][-1]
                    split_to(m + 2)
                    if j < 6:
                        scaled(("in1", l, j), ("x1", l), lambda tt: proj[:, tt, 512 * j:512 * j + 512], 512, [yb(0, j), yb(1, j)])
                    else:
                        for tt in range(TT):
                            act.wait_ge(gate_pre, 8 * l + 2 * (j - 6) + tt + 1)
                            gt = gates[:, tt, 512 * (j - 6):512 * (j - 5)]
                            nc.scalar.activation(gt, gt, ACT.Sigmoid).then_inc(gate_done, 1)
                for g in range(1, 8, 2):
                    take(("qk1", l, g), blocks(qT, 2 * g), scale=-SCALE if g in (0, 1, 2, 6) else 1.0)
                if l == 0:
                    act.wait_ge(band_out, 16)
                attention(("dil", l))
                for h in range(HG):
                    act.wait_ge(sb_abs, HG * l + h + 1)
                    link(nc.scalar.activation(sba(h), sba(h), ACT.Exp, scale=-1.0))
                for h in range(HG):
                    nc.scalar.activation(sba(h), sba(h), ACT.Ln, bias=1.0).then_inc(sb_ln, 1)
                for h in range(HG):
                    act.wait_ge(sb_arg, HG * l + h + 1)
                    nc.scalar.activation(sba(h), sba(h), ACT.Exp).then_inc(sb_att, 1)
                for i, g in enumerate(("a", "b")):
                    take(("y1", l, g), blocks(mhi, 2 * i))
                split_to(plan.jobs["pb", l][-1] + 2)
                stream_hi("mix", l, mhi)
                n0 = 2 * plan.jobs["out1", l, 1][0]
                split_half(n0 + 3)
                stream_hi("xf", l, ahi, row=gain_row["xf", l], gs=(0, 1))
                split_half(n0 + 7)
                stream_hi("xf", l, ahi, row=gain_row["xf", l], gs=(2, 3))

                def up_out(b):
                    scaled(("up", l, b), ("xf", l), lambda tt: nat[:, b % 2, tt, :], 512, [6, 7])

                up_out(0)
                split_to(plan.jobs["up", l, 0][-1] + 2)
                for b in range(NFB):
                    n0 = 2 * plan.jobs["up", l, min(b + 1, NFB - 1)][0]
                    if b + 1 < NFB:
                        split_half(n0 + 3)
                    act.wait_ge(grp_dve, plan.by_number[plan.groups["ta", l, b]][2])
                    nc.scalar.activation(sl, cv, ACT.Silu).then_inc(silu_ready, 1)
                    if b + 1 < NFB:
                        split_half(n0 + 4)
                    act.wait_ge(grp_dve, plan.by_number[plan.groups["tb", l, b]][2])
                    nc.scalar.copy(blocks(mhi, 2 * (b % 4)), ut).then_inc(uhi, 1)
                    if b + 1 < NFB:
                        split_half(n0 + 6)
                        up_out(b + 1)
                        if b:
                            split_half(n0 + 8)
                split_half(2 * plan.jobs["down", l, NFB - 1][-1] + 4)

            def squares(job, key, l, banks):
                i = NORM[key, l]
                for c in range(2):
                    for tt in range(TT):
                        product(job(c), tt)
                        nc.scalar.activation(junk_act[:, 2 * c + tt, :], ps[:, yb(tt, c), :], ACT.Square,
                                             accum_out=ss[:, i, 2 * c + tt:2 * c + tt + 1]).then_inc(ss_ready, 1)

            for l in range(DEPTH):
                even = l % 2 == 0
                stream_hi("x2", l, mhi, row=gain_row["x2", l])
                cols = EV_COLS if even else OD_COLS
                nj = -(-cols // 512)
                for j in range(nj):
                    n = min(512, cols - 512 * j)
                    split_to(plan.jobs["in2", l, j][-1] + 2)
                    scaled(("in2", l, j), ("x2", l), lambda tt: proj[:, tt, 512 * j:512 * j + n], n, [yb(0, j), yb(1, j)])
                stream_hi("mem", l, ahi, row=gain_row["mem", l])
                split_to(plan.jobs["kv", l][-1] + 2)
                scaled(("kv", l), ("mem", l), lambda tt: kvn[:, tt, :], 512, [6, 7])
                if even:
                    for g in range(2):
                        take(("qi", l, g), blocks(qiT, 2 * g))
                    take(("ki", l), blocks(kicT, 0))
                    for qt in range(TT):
                        nk = causal(qt)
                        for g in range(HA // 2):
                            key = ("idx", l, qt, g)
                            group_ready(act, key)
                            t = qt * (HA // 2) + g
                            if t >= 2:
                                act.wait_ge(idx_used, t - 1)
                            src = ps[:, 4 + plan.groups[key] % 2, :].rearrange("p (h n) -> p h n", h=2)[:, :, 0:nk]
                            dst = relu_i[:, t % 2, :].rearrange("p (h n) -> p h n", h=2)[:, :, 0:nk]
                            nc.scalar.activation(dst, src, ACT.Relu).then_inc(grp_act, 1)
                    for g in range(4):
                        take(("qkb", l, g), blocks(qT, 2 * g), scale=-SCALE if g < 2 else 1.0)
                    for g in range(2):
                        take(("qa", l, g), blocks(qT, 8 + 2 * g), scale=-SCALE)
                    take(("uk", l), blocks(ukT, 0, 4))
                    for g in range(2):
                        take(("ka", l, g), blocks(qT, 12 + 2 * g))
                    for t in range(TT):
                        take(("va", l, t), proj[:, t, 0:512])
                    act.wait_ge(lam_arg, 2)
                    nc.scalar.activation(small[:, 7, 0:2], small[:, 6, 0:2], ACT.Exp).then_inc(lam_exp, 1)
                    attention(("diff", l))
                    attention(("dsa", l))
                else:
                    for g in range(1, 5, 2):
                        take(("qk2", l, g), blocks(qT, 2 * g), scale=-SCALE)
                    def sink_share(qt):
                        act.wait_ge(sink_arg, qt + 1)
                        nc.scalar.activation(small[:, 12 + qt, :], small[:, 14 + qt, :], ACT.Exp).then_inc(sink_exp, 1)

                    attention(("odd", l), sink_share)
                stream_hi("o2", l, ahi)
                for j in range(2):
                    split_to(plan.jobs["out2", l, j][-1] + j)
                squares(lambda c: ("out2", l, c), "y2", l, None)
                split_to(plan.jobs["out2", l, 1][-1] + 2)
                stream_hi("xx", l, mhi, row=gain_row["xx", l])
                scaled(("wq", l), ("xx", l), lambda tt: proj[:, tt, 0:256], 256, [6, 7])
                split_to(plan.jobs["wq", l][-1] + 2)
                take(("qkx", l, 1), blocks(qT, 0), scale=-SCALE)
                attention(("cross", l))
                take(("ox", l), blocks(mhi, 0))
                squares(lambda c: ("wo", l), "yx", l, None)
                split_to(plan.jobs["wo", l][-1] + 2)
                stream_hi("xm", l, ahi, row=gain_row["xm", l])

                def mlp_out(b):
                    scaled(("w1", l, b), ("xm", l), lambda tt: nat[:, b % 2, tt, :], MB, [6, 7], ACT.Relu, relu_ready)

                mlp_out(0)
                split_to(plan.jobs["w1", l, 0][-1] + 2)
                for b in range(NMB):
                    for g in range(2):
                        take(("tm", l, b, g), blocks(mhi, 4 * (b % 2) + 2 * g))
                    n0 = plan.jobs["w2", l, b][0]
                    split_to(n0 + 1)
                    if b + 1 < NMB:
                        mlp_out(b + 1)
                    split_half(2 * n0 + (6 if b != NMB - 2 else 5))
                squares(lambda c: ("w2", l, NMB - 1), "ym", l, None)

        @block.vector
        def _(dve):
            n_split = [0]
            n_link = [0]

            def mark(ins):
                n_link[0] += 1
                ins.then_inc(chain, 1)
                return n_link[0]

            def after(n):
                dve.wait_ge(chain, n)

            def link(ins):
                after(mark(ins))

            def split_half(m_last):
                while n_split[0] <= min(m_last, 2 * NCH - 1):
                    m = n_split[0]
                    n, h = divmod(m, 2)
                    kc, cols, _ = plan.chunks[n]
                    w = kc // 2 * cols
                    dve.wait_ge(hi_done, m + 1)
                    nc.vector.tensor_tensor(wlo[:, m % HL, 0:w], raw[:, n % RAW, h * w:h * w + w],
                                            whi[:, m % HL, 0:w].bitcast(F32), ALU.subtract).then_inc(lo_done, 1)
                    n_split[0] += 1

            def split_to(n):
                split_half(2 * n + 1)

            def product(key, tt):
                dve.wait_ge(pe_out, 4 * plan.jobs[key][-1] + 3 + tt)

            def group_bank(key):
                return ps[:, 4 + plan.groups[key] % 2, :]

            def hi_ready(key):
                dve.wait_ge(grp_act, plan.by_number[plan.groups[key]][1])

            def stream_lo(tag, l, hi, lo, row=None, gs=range(4)):
                for g in gs:
                    key = (tag, l, g)
                    hi_ready(key)
                    bank = group_bank(key)
                    if row is None:
                        nc.vector.tensor_tensor(blocks(lo, 2 * g), bank, blocks(hi, 2 * g).bitcast(F32), ALU.subtract).then_inc(grp_dve, 1)
                    else:
                        for b in range(2):
                            ins = nc.vector.scalar_tensor_tensor(out=lo[:, 2 * g + b, :], in0=bank[:, b * SEQ:(b + 1) * SEQ],
                                                                 scalar=gains[:, 2 * g + b, row:row + 1],
                                                                 in1=hi[:, 2 * g + b, :].bitcast(F32), op0=ALU.mult, op1=ALU.subtract)
                        ins.then_inc(grp_dve, 1)

            def blocks(t, b0, n=2):
                return t[:, b0:b0 + n, :].rearrange("p b n -> p (b n)")

            def lo_of(key, hi, lo, b0):
                hi_ready(key)
                nc.vector.tensor_tensor(blocks(lo, b0), group_bank(key), blocks(hi, b0).bitcast(F32), ALU.subtract).then_inc(grp_dve, 1)

            n_sq = [0]

            def squares(key, src, width):
                i = NORM[key]
                for tt in range(TT):
                    if n_sq[0]:
                        dve.wait_ge(ss_ready, n_sq[0])
                    nc.vector.tensor_tensor_reduce(out=junk[:, 0:width], in0=src(tt), in1=src(tt), scale=1.0, scalar=0.0, op0=ALU.mult,
                                                   op1=ALU.add, accum_out=ss[:, i, tt:tt + 1]).then_inc(ss_ready, 1)
                    n_sq[0] += 1

            def attention(key, half_done):
                us, u0 = units_of[key], first_unit[key]
                wide_units = us[-1]["w"] > SEQ
                n = len(us)
                done = 0
                for i in range(n + 2):
                    if i < n:
                        u, d = u0 + i, us[i]
                        dve.wait_ge(at_s, u + 1)
                        if u >= 2:
                            dve.wait_ge(at_e, u - 1)
                        b0 = 2 * (u % 2) if wide_units else u % 2
                        flat = ps[:, b0:b0 + (2 if wide_units else 1), :].rearrange("p b n -> p (b n)")[:, 0:d["w"]]
                        s = d["slot"]
                        bias = zero_bias if d["bias"] is None else d["bias"]
                        nc.vector.tensor_tensor_reduce(out=sc[:, u % 2, 0:d["w"]], in0=flat, in1=bias, scale=1.0,
                                                       scalar=nsink[:, s:s + 1] if key[0] == "odd" else 3e38, op0=ALU.add, op1=ALU.min,
                                                       accum_out=low[:, d["qt"], s:s + 1]).then_inc(at_t, 1)
                    if i >= 2 and (u0 + i - 2) % 2 == 0:
                        u, d = u0 + i - 2, us[i - 2]
                        dve.wait_ge(at_x, u + 1)
                        if u >= 2:
                            dve.wait_ge(at_o, u - 1)
                        nc.vector.tensor_copy(eT[:, u % 2, 0:d["w"]], turned(u, d)).then_inc(at_yd, 1)
                    if i == n // 2 + 5:
                        half_done(0)
                        done = 1
                for qt in range(done, TT):
                    half_done(qt)

            def norm_out(key, heads, dst):
                us, u0 = units_of[key], first_unit[key]
                first = us[0]["o_bank"], us[len(us) // 2]["o_bank"]

                def run(qt):
                    dve.wait_ge(at_o, u0 + (len(us) // 2) * (qt + 1))
                    if key[0] == "odd":
                        link(nc.vector.tensor_tensor(small[:, 14 + qt, :], low[:, qt, :], nsink, ALU.subtract))
                        nc.vector.tensor_copy(rden[:, qt, :], den[:, qt, :]).then_inc(sink_arg, 1)
                        dve.wait_ge(sink_exp, qt + 1)
                        dve.wait_ge(sink_arg, qt + 1)
                        link(nc.vector.tensor_tensor(rden[:, qt, :], rden[:, qt, :], small[:, 12 + qt, :], ALU.add))
                        link(nc.vector.reciprocal(rden[:, qt, 0:heads], rden[:, qt, 0:heads]))
                    else:
                        link(nc.vector.reciprocal(rden[:, qt, 0:heads], den[:, qt, 0:heads]))
                    nb = -(-heads * HD // 512)
                    flat = ps[:, first[qt]:first[qt] + nb, :].rearrange("p b n -> p (b n)")[:, 0:heads * HD]
                    nc.vector.tensor_tensor(dst(qt), flat.rearrange("p (h d) -> p h d", d=HD),
                                            rden[:, qt, 0:heads].unsqueeze(2).to_broadcast([P, heads, HD]), ALU.mult).then_inc(o_ready, 1)
                return run

            def heads_of(t, tt, c0, n, d=HD):
                return t[:, tt, c0:c0 + n * d].rearrange("p (h d) -> p h d", d=d)

            nsink = misc[:, 512:528]
            zero_bias = relu_i[:, 0, 0:SEQ]

            dve.wait_ge(misc_in, 16)
            dve.wait_ge(cst_in, 16)
            pf = small[:, 1, 0:TT]
            link(nc.vector.tensor_copy(pf, pos_i[:]))
            ang, turns, wrap = small[:, 2, :], small[:, 3, :], small[:, 4, :]
            arg = small[:, 8:10, :]
            link(nc.vector.tensor_tensor(ang.rearrange("p (t f) -> p t f", t=TT), pf.unsqueeze(2).to_broadcast([P, TT, 8]),
                                         cst[:, C_INV:C_INV + 8].unsqueeze(1).to_broadcast([P, TT, 8]), ALU.mult))
            link(nc.vector.tensor_scalar(turns, ang, 1.0 / TWO_PI, ROUND, ALU.mult, ALU.add))
            link(nc.vector.tensor_scalar(turns, turns, ROUND, None, ALU.subtract))
            for part in (PI_HI, PI_MID, PI_LO):
                link(nc.vector.scalar_tensor_tensor(out=ang, in0=turns, scalar=-part, in1=ang, op0=ALU.mult, op1=ALU.add))
            link(nc.vector.tensor_copy(arg[:, 0, :], ang))
            link(nc.vector.tensor_scalar(arg[:, 1, :], ang, float(np.pi / 2), None, ALU.add))
            pi = float(np.float32(np.pi))
            for i in range(2):
                for cmp, lim, step in ((ALU.is_gt, pi, -TWO_PI), (ALU.is_lt, -pi, TWO_PI)):
                    link(nc.vector.tensor_scalar(wrap, arg[:, i, :], lim, step, cmp, ALU.mult))
                    link(nc.vector.tensor_tensor(arg[:, i, :], arg[:, i, :], wrap, ALU.add))
            link(nc.vector.tensor_scalar(arg, arg, pi, None, ALU.min))
            nc.vector.tensor_scalar(arg, arg, -pi, None, ALU.max).then_inc(trig_arg, 1)
            sin, cos = (small[:, 10 + i, :].rearrange("p (t f) -> p t f", t=TT).unsqueeze(2).to_broadcast([P, TT, 24, 8]) for i in range(2))
            split_to(1)

            for l in range(DEPTH):
                stream_lo("x1", l, ahi, alo, row=gain_row["x1", l])
                if l == 0:
                    dve.wait_ge(x_in, 16)
                squares(("x1", l), lambda tt: x[:, tt, :], D)
                for j in range(10):
                    m = plan.jobs["in1", l, j][-1]
                    split_to(m + 2)
                    if j == 3:
                        dve.wait_ge(ev_act, evs_act(l, 2))
                        dve.wait_ge(trig_done, 1)
                        qk = proj[:, :, 0:1536].rearrange("p t (h d) -> p t h d", d=HD)
                        x1, x2 = qk[:, :, :, 0:8], qk[:, :, :, 8:16]
                        for i, (u, v) in enumerate(((x1, cos), (x2, sin), (x2, cos), (x1, sin))):
                            n = mark(nc.vector.tensor_tensor(rt[:, i], u, v, ALU.mult))
                        after(n)
                        nc.vector.tensor_tensor(x1, rt[:, 0], rt[:, 1], ALU.subtract)
                        nc.vector.tensor_tensor(x2, rt[:, 2], rt[:, 3], ALU.add).then_inc(rope_done, 1)
                    if j >= 6:
                        if j == 6:
                            dve.wait_ge(bgate_in, 16 * (l + 1))
                            dve.wait_ge(rstd_ready, rs_count["x1", l])
                        for tt in range(TT):
                            product(("in1", l, j), tt)
                            at = slice(512 * (j - 6), 512 * (j - 5))
                            nc.vector.scalar_tensor_tensor(out=gates[:, tt, at], in0=ps[:, yb(tt, j), :],
                                                           scalar=rstd[:, NORM["x1", l], tt:tt + 1], in1=gate_bias[:, at],
                                                           op0=ALU.mult, op1=ALU.add).then_inc(gate_pre, 1)
                for g in range(0, 8, 2):
                    key = ("qk1", l, g)
                    group_ready(dve, key)
                    if g in (0, 2, 6):
                        nc.vector.tensor_scalar(blocks(qT, 2 * g), group_bank(key), -SCALE, None, ALU.mult).then_inc(grp_dve, 1)
                    else:
                        nc.vector.tensor_copy(blocks(qT, 2 * g), group_bank(key)).then_inc(grp_dve, 1)
                if l == 0:
                    dve.wait_ge(mask_in, 16)
                    dve.wait_ge(band_out, 16)
                attention(("dil", l), norm_out(("dil", l), HG, lambda qt: heads_of(o_nat, qt, 0, HG)))
                for h in range(HG):
                    dve.wait_ge(sb_z, HG * l + h + 1)
                    n = mark(nc.vector.tensor_tensor(sbz(h), ps[:, h, 0:384], cst[:, C_SBM:C_SBM + 384], ALU.add))
                    after(n)
                    nc.vector.scalar_tensor_tensor(out=sba(h), in0=sbz(h), scalar=-1.0, in1=sbz(h), op0=ALU.mult, op1=ALU.max).then_inc(sb_abs, 1)
                for h in range(HG):
                    dve.wait_ge(sb_ln, HG * l + h + 1)
                    nc.vector.scalar_tensor_tensor(out=sbk(h), in0=sbz(h), scalar=0.0, in1=sba(h), op0=ALU.min,
                                                   op1=ALU.subtract).then_inc(sb_keep, 1)
                for h in range(HG):
                    dve.wait_ge(sb_sum, HG * l + h + 1)
                    nc.vector.tensor_tensor(sba(h), ps[:, h, 0:384], sbz(h), ALU.subtract).then_inc(sb_arg, 1)
                dve.wait_ge(sb_o, HG * (l + 1))
                for tt in range(TT):
                    nc.vector.tensor_copy(o_nat[:, tt, 512:768], ps[:, 6 + tt, 0:256]).then_inc(o_ready, 1)
                for i, g in enumerate(("a", "b")):
                    lo_of(("y1", l, g), mhi, mlo, 2 * i)
                split_to(plan.jobs["pb", l][-1] + 1)
                dve.wait_ge(gate_done, 8 * (l + 1))
                for tt in range(TT):
                    product(("pa", l), tt)
                    for c in range(2):
                        nc.vector.tensor_tensor(o_nat[:, tt, 512 * c:512 * c + 512], ps[:, yb(tt, c), :],
                                                gates[:, tt, 512 * c:512 * c + 512], ALU.mult)
                split_half(2 * plan.jobs["pb", l][-1] + 3)
                for c in range(2):
                    for tt in range(TT):
                        product(("pb", l), tt)
                        gt = gates[:, tt, D + 512 * c:D + 512 * c + 512]
                        n = mark(nc.vector.tensor_tensor(gt, ps[:, 4 + 2 * c + tt, :], gt, ALU.mult))
                    after(n)
                    for tt in range(TT):
                        o = o_nat[:, tt, 512 * c:512 * c + 512]
                        nc.vector.tensor_tensor(o, o, gates[:, tt, D + 512 * c:D + 512 * c + 512], ALU.add).then_inc(mixed, 1)
                split_to(plan.jobs["pb", l][-1] + 2)
                stream_lo("mix", l, mhi, mlo)

                def add_out(j):
                    for tt in range(TT):
                        product(("out1", l, j), tt)
                        xs = x[:, tt, 512 * j:512 * j + 512]
                        ins = nc.vector.tensor_tensor(xs, xs, ps[:, yb(tt, j), :], ALU.add)
                    ins.then_inc(x_ready, 1)

                n0 = 2 * plan.jobs["out1", l, 1][0]
                split_half(n0 + 1)
                add_out(0)
                split_half(n0 + 3)
                stream_lo("xf", l, ahi, alo, row=gain_row["xf", l], gs=(0, 1))
                split_half(n0 + 5)
                add_out(1)
                split_half(n0 + 7)
                dve.wait_ge(x_ready, x_count("mix", l))
                stream_lo("xf", l, ahi, alo, row=gain_row["xf", l], gs=(2,))
                squares(("xf", l), lambda tt: x[:, tt, :], D)
                stream_lo("xf", l, ahi, alo, row=gain_row["xf", l], gs=(3,))
                split_to(plan.jobs["up", l, 0][-1] + 2)
                for b in range(NFB):
                    n0 = 2 * plan.jobs["up", l, min(b + 1, NFB - 1)][0]
                    group_ready(dve, ("ta", l, b))
                    bank = group_bank(("ta", l, b))
                    if b:
                        dve.wait_ge(silu_ready, NFB * l + b)
                    for f in range(2):
                        w = [conv[:, 2 * b + f, i:i + 1] for i in (3 * l, 3 * l + 1, 3 * l + 2, 6 + l)]
                        n = mark(nc.vector.tensor_scalar(cv[:, f * SEQ:(f + 1) * SEQ], bank[:, f * SEQ:(f + 1) * SEQ], w[2], w[3], ALU.mult, ALU.add))
                    for lag in (1, 2):
                        after(n)
                        for f in range(2):
                            w = conv[:, 2 * b + f, 3 * l + 2 - lag:3 * l + 3 - lag]
                            o = cv[:, f * SEQ + lag:(f + 1) * SEQ]
                            ins = nc.vector.scalar_tensor_tensor(out=o, in0=bank[:, f * SEQ:(f + 1) * SEQ - lag], scalar=w, in1=o,
                                                                 op0=ALU.mult, op1=ALU.add)
                            if lag == 2 and f == 1:
                                ins.then_inc(grp_dve, 1)
                            else:
                                n = mark(ins)
                    if b + 1 < NFB:
                        split_half(n0 + 4)
                    group_ready(dve, ("tb", l, b))
                    dve.wait_ge(silu_ready, NFB * l + b + 1)
                    if b:
                        dve.wait_ge(ulo, NFB * l + b)
                    nc.vector.tensor_tensor(ut, sl, group_bank(("tb", l, b)), ALU.mult).then_inc(grp_dve, 1)
                    dve.wait_ge(grp_dve, plan.by_number[plan.groups["tb", l, b]][2])
                    dve.wait_ge(uhi, NFB * l + b + 1)
                    nc.vector.tensor_tensor(blocks(mlo, 2 * (b % 4)), ut, blocks(mhi, 2 * (b % 4)).bitcast(F32), ALU.subtract).then_inc(ulo, 1)
                    if b + 1 < NFB:
                        split_half(n0 + (8 if b else 6))
                split_half(2 * plan.jobs["down", l, NFB - 1][-1] + 4)
                for c in range(2):
                    for tt in range(TT):
                        product(("down", l, NFB - 1), tt)
                        xs = x[:, tt, 512 * c:512 * c + 512]
                        ins = nc.vector.tensor_tensor(xs, xs, ps[:, yb(tt, c), :], ALU.add)
                    ins.then_inc(x_ready, 1)
                dve.wait_ge(x_ready, x_count("ffn", l))

            squares(("final",), lambda tt: x[:, tt, :], D)
            dve.wait_ge(gainb_in, 16)
            dve.wait_ge(rstd_ready, rs_count["final",])
            for c in range(2):
                cs = slice(512 * c, 512 * c + 512)
                for tt in range(TT):
                    ins = nc.vector.scalar_tensor_tensor(out=x[:, tt, cs], in0=x[:, tt, cs], scalar=rstd[:, NORM["final",], tt:tt + 1],
                                                         in1=gain_b[:, cs], op0=ALU.mult, op1=ALU.mult)
                ins.then_inc(x_ready, 1)

            n_gain = [1]

            def add_normed(key, l, jobs):
                n_gain[0] += 1
                n_sq[0] += 4
                dve.wait_ge(gainb_in, 16 * n_gain[0])
                for c in range(2):
                    for tt in range(TT):
                        product(jobs[c], tt)
                        dve.wait_ge(ss_ready, n_sq[0] - 3 + 2 * c + tt)
                        cs = slice(512 * c, 512 * c + 512)
                        n = mark(nc.vector.tensor_tensor(ystep[:, tt, cs], ps[:, yb(tt, c), :], gain_b[:, cs], ALU.mult))
                dve.wait_ge(rstd_ready, rs_count[key, l])
                after(n)
                for c in range(2):
                    for tt in range(TT):
                        cs = slice(512 * c, 512 * c + 512)
                        ins = nc.vector.scalar_tensor_tensor(out=x[:, tt, cs], in0=ystep[:, tt, cs], scalar=rstd[:, NORM[key, l], tt:tt + 1],
                                                             in1=x[:, tt, cs], op0=ALU.mult, op1=ALU.add)
                    ins.then_inc(x_ready, 1)
                dve.wait_ge(x_ready, x_count(key, l))

            for l in range(DEPTH):
                even = l % 2 == 0
                stream_lo("x2", l, mhi, mlo, row=gain_row["x2", l])
                if l == 0:
                    dve.wait_ge(x_ready, x_count("final"))
                squares(("x2", l), lambda tt: x[:, tt, :], D)
                cols = EV_COLS if even else OD_COLS
                nj = -(-cols // 512)
                for j in range(nj):
                    split_to(plan.jobs["in2", l, j][-1] + 2)
                dve.wait_ge(mem_in, 16 * (l + 1))
                stream_lo("mem", l, ahi, alo, row=gain_row["mem", l])
                squares(("mem", l), lambda tt: o_nat[:, tt, :], D)
                dve.wait_ge(band_in, 16 * (l + 1))
                n = mark(nc.vector.memset(band[0:64, 0:(HA + HB) if even else HC, 192:256], BIG))
                dve.wait_ge(ev_act, evs_act2(l, "in2", nj - 1))
                if even:
                    kd = kdup[:, 0:256].rearrange("p (t i d) -> p t i d", t=TT, i=2)
                    nc.vector.tensor_copy(kd, proj[:, :, 1152:1216].unsqueeze(2).to_broadcast([P, TT, 2, HD])).then_inc(kdup_ready, 1)
                    squares(("ckv", l), lambda tt: proj[:, tt, 512:640], P)
                    dve.wait_ge(misc_in, 16 * 5)
                    for i in range(2):
                        if i:
                            dve.wait_ge(lam_arg, i)
                        nc.vector.tensor_tensor_reduce(out=junk[:, 512:576], in0=lam_rows[:, 128 * i:128 * i + 64], in1=lam_rows[:, 128 * i + 64:128 * i + 128],
                                                       scale=1.0, scalar=0.0, op0=ALU.mult, op1=ALU.add,
                                                       accum_out=small[:, 6, i:i + 1]).then_inc(lam_arg, 1)
                    link(nc.vector.tensor_scalar(nsink, nsink, -1.0, None, ALU.mult))
                    dve.wait_ge(rstd_ready, rs_count["ckv", l])
                    for tt in range(TT):
                        c = proj[:, tt, 512:640]
                        nc.vector.scalar_tensor_tensor(out=c, in0=c, scalar=rstd[:, NORM["ckv", l], tt:tt + 1], in1=akv,
                                                       op0=ALU.mult, op1=ALU.mult).then_inc(c_ready, 1)
                    for qt in range(TT):
                        nk = causal(qt)
                        adm = cst[:, C_ADM + SEQ - nk:C_ADM + SEQ]
                        for g in range(HA // 2):
                            t = qt * (HA // 2) + g
                            dve.wait_ge(grp_act, plan.by_number[plan.groups["idx", l, qt, g]][1])
                            for i in range(2):
                                h = 4 * (g // 2) + g % 2 + 2 * i
                                ins = nc.vector.scalar_tensor_tensor(out=cand[:, 0:nk], in0=relu_i[:, t % 2, i * SEQ:i * SEQ + nk],
                                                                     scalar=proj[:, qt, 1216 + h:1217 + h], in1=adm if h == 0 else cand[:, 0:nk],
                                                                     op0=ALU.mult, op1=ALU.add)
                                if i == 0:
                                    link(ins)
                                else:
                                    ins.then_inc(idx_used, 1)
                                    dve.wait_ge(idx_used, t + 1)
                        top = small[:, 13, 0:8]
                        for r in range(TOPK // 8):
                            link(nc.vector.max(top, cand[:, 0:nk]))
                            link(nc.vector.match_replace(cand[:, 0:nk], top, cand[:, 0:nk], SENTINEL))
                        nc.vector.tensor_scalar(sel[:, (0, P)[qt]:(0, P)[qt] + nk], cand[:, 0:nk], SENTINEL / 2, BIG, ALU.is_gt, ALU.mult).then_inc(sel_ready, 1)
                        dve.wait_ge(sel_ready, qt + 1)
                    split_to(plan.jobs["kv", l][-1] + 2)
                    dve.wait_ge(lam_exp, 1)
                    nlam = small[:, 7, 2:3]
                    link(nc.vector.tensor_tensor(nlam, small[:, 7, 1:2], small[:, 7, 0:1], ALU.subtract))
                    link(nc.vector.tensor_scalar(nlam, nlam, -LAM_INIT, None, ALU.add))

                    def diff_out(qt):
                        us, u0 = units_of["diff", l], first_unit["diff", l]
                        dve.wait_ge(at_o, u0 + 2 * HB * (qt + 1))
                        link(nc.vector.reciprocal(rden[:, qt, 0:8], den[:, qt, 0:8]))
                        r = rden[:, qt, 0:8].rearrange("p (h m) -> p h m", m=2)
                        link(nc.vector.tensor_scalar(r[:, :, 1], r[:, :, 1], nlam, None, ALU.mult))
                        b0 = us[0]["o_bank"] if qt == 0 else us[len(us) // 2]["o_bank"]
                        y = ps[:, b0:b0 + 2, :].rearrange("p b (h m d) -> p (b h) m d", m=2, d=P)
                        o = heads_of(o_nat, qt, 512, HB, P)
                        t = heads_of(o_nat, qt, 0, HB, P)
                        n = mark(nc.vector.tensor_tensor(o, y[:, :, 0, :], r[:, :, 0].unsqueeze(2).to_broadcast([P, HB, P]), ALU.mult))
                        n = mark(nc.vector.tensor_tensor(t, y[:, :, 1, :], r[:, :, 1].unsqueeze(2).to_broadcast([P, HB, P]), ALU.mult))
                        after(n)
                        link(nc.vector.tensor_tensor(o, o, t, ALU.add))
                        link(nc.vector.tensor_tensor(t, o, o, ALU.mult))
                        nc.vector.tensor_reduce(small[:, 2 + qt, 0:HB], t, AX.X, ALU.add).then_inc(ss_ready, 1)
                        n_sq[0] += 1
                        dve.wait_ge(rstd_ready, rs_count["ckv", l] + qt + 1)
                        link(nc.vector.tensor_tensor(o, o, small[:, 4 + qt, 0:HB].unsqueeze(2).to_broadcast([P, HB, P]), ALU.mult))
                        nc.vector.scalar_tensor_tensor(out=o, in0=o, scalar=1.0 - LAM_INIT, in1=subln.unsqueeze(1).to_broadcast([P, HB, P]),
                                                       op0=ALU.mult, op1=ALU.mult).then_inc(o_ready, 1)

                    attention(("diff", l), diff_out)
                    attention(("dsa", l), norm_out(("dsa", l), HA, lambda qt: heads_of(o_nat, qt, 0, HA)))
                else:
                    link(nc.vector.memset(band[64:128, 0:HC, 0:64], BIG))
                    kd = kdup.rearrange("p (t k i d) -> p t k i d", t=TT, k=2, i=2)
                    for tt in range(TT):
                        ins = nc.vector.tensor_copy(kd[:, tt], proj[:, tt, 1024:1152].rearrange("p (k d) -> p k d", d=HD).unsqueeze(2)
                                                    .to_broadcast([P, 2, 2, HD]))
                    ins.then_inc(kdup_ready, 1)
                    split_to(plan.jobs["kv", l][-1] + 2)
                    for g in range(0, 5, 2):
                        key = ("qk2", l, g)
                        group_ready(dve, key)
                        if g < 4:
                            nc.vector.tensor_scalar(blocks(qT, 2 * g), group_bank(key), -SCALE, None, ALU.mult).then_inc(grp_dve, 1)
                        else:
                            nc.vector.tensor_copy(blocks(qT, 2 * g), group_bank(key)).then_inc(grp_dve, 1)
                    attention(("odd", l), norm_out(("odd", l), HC, lambda qt: heads_of(o_nat, qt, 0, HC)))
                stream_lo("o2", l, ahi, alo)
                for j in range(2):
                    split_to(plan.jobs["out2", l, j][-1] + 1 + j)
                add_normed("y2", l, [("out2", l, 0), ("out2", l, 1)])
                stream_lo("xx", l, mhi, mlo, row=gain_row["xx", l], gs=(0, 1))
                squares(("xx", l), lambda tt: x[:, tt, :], D)
                stream_lo("xx", l, mhi, mlo, row=gain_row["xx", l], gs=(2, 3))
                split_to(plan.jobs["wq", l][-1] + 2)
                key = ("qkx", l, 0)
                group_ready(dve, key)
                nc.vector.tensor_copy(blocks(qT, 2), group_bank(key)).then_inc(grp_dve, 1)
                link(nc.vector.memset(zero_bias, 0.0))
                attention(("cross", l), norm_out(("cross", l), HX, lambda qt: heads_of(o_nat, qt, 0, HX)))
                lo_of(("ox", l), mhi, mlo, 0)
                split_to(plan.jobs["wo", l][-1] + 1)
                add_normed("yx", l, [("wo", l)] * 2)
                split_to(plan.jobs["wo", l][-1] + 2)
                stream_lo("xm", l, ahi, alo, row=gain_row["xm", l])
                squares(("xm", l), lambda tt: x[:, tt, :], D)

                def square(b):
                    for tt in range(TT):
                        dve.wait_ge(relu_ready, 2 * (NMB * l + b) + tt + 1)
                        nc.vector.tensor_tensor(nat[:, b % 2, tt, :], nat[:, b % 2, tt, :], nat[:, b % 2, tt, :], ALU.mult).then_inc(sq_ready, 1)

                square(0)
                split_to(plan.jobs["w1", l, 0][-1] + 2)
                for b in range(NMB):
                    for g in range(2):
                        lo_of(("tm", l, b, g), mhi, mlo, 4 * (b % 2) + 2 * g)
                    n0 = plan.jobs["w2", l, b][0]
                    split_to(n0 + 1)
                    if b + 1 < NMB:
                        square(b + 1)
                    split_half(2 * n0 + (6 if b != NMB - 2 else 5))
                add_normed("ym", l, [("w2", l, NMB - 1)] * 2)


INPUTS = [
    "x", "positions", "norm_mix", "w_in", "b_gate", "w_proj_a", "w_proj_b", "w_out", "norm_ffn", "w_up", "conv_w", "conv_b", "w_down",
    "norm_final", "mem_2", "rel_bias_table_2", "norm_g_2", "ev_w_in_2", "ev_a_kv_norm_2", "ev_a_w_uk_2", "ev_a_w_uv_2", "ev_b_lambda_2",
    "ev_b_subln_2", "ev_w_out_2", "od_w_in_2", "od_sinks_2", "od_w_out_2", "xa_wq_2", "xa_wkv_2", "xa_wo_2", "xa_mem_norm_2", "mlp_w1_2",
    "mlp_w2_2",
]


def kernel(**inputs):
    import numpy as np
    import concourse.bacc as bacc
    from concourse import mybir
    from concourse.bass_utils import run_bass_kernel_spmd

    nc = bacc.Bacc("TRN2", target_bir_lowering=False, num_devices=1)
    cst, masks = shape_constants()
    arrays = {"in_" + n: np.ascontiguousarray(inputs[n]) for n in INPUTS}
    arrays["in_cst"], arrays["in_masks"] = cst, masks
    aps = {n[3:]: nc.dram_tensor(n, v.shape, mybir.dt.from_np(v.dtype), kind="ExternalInput").ap() for n, v in arrays.items()}
    out = nc.dram_tensor("out", (1, SEQ, D), mybir.dt.float32, kind="ExternalOutput").ap()
    build_network(nc, aps, out)
    r = run_bass_kernel_spmd(nc, [arrays], core_ids=[0])
    return r.results[0]["out"]
```

```python
from contextlib import ExitStack

import concourse.bass as bass
import numpy as np
from concourse import mybir

F32 = mybir.dt.float32
F32R = mybir.dt.float32r
BF16 = mybir.dt.bfloat16
I32 = mybir.dt.int32
ALU = mybir.AluOpType
ACT = mybir.ActivationFunctionType
AX = mybir.AxisListType

P = 128
TT = 2
SEQ = TT * P
D = 1024
KD = D // P
DEPTH = 2
HD = 64
DIL = (1, 4, 16)
DIL_WINDOW = (128, 512, 2048)
NG, HG = 3, 4
QKV1 = 3072
GC = 256
NGC = 2 * D // GC
FF1 = 2816
FB = 256
NFB = FF1 // FB
FF2 = 4096
MB = 512
NMB = FF2 // MB
EV_COLS = 2760
OD_COLS = 1280
HA, HB, HC, HX = 8, 4, 16, 4
TOPK = 64
IN2_ORDER = ((1, 2, 0, 3, 4, 5), (0, 2, 1))
EVEN_GROUPS = {9: [("qi", 0), ("qi", 1)], 10: [("ki",), ("uk",)], 11: [("idx", 0, 0), ("idx", 0, 1)], 12: [("idx", 0, 2), ("idx", 0, 3)],
               13: [("ck",), ("qkb", 0)], 14: [("idx", 1, 0), ("qa", 0)], 15: [("idx", 1, 1), ("qa", 1)], 16: [("idx", 1, 2)],
               17: [("idx", 1, 3), ("qkb", 1)], 18: [("qkb", 2), ("ka", 0)], 19: [("ka", 1), ("va", 0)], 20: [("va", 1)], 99: [("qkb", 3)]}
ODD_GROUPS = {5: [("qk2", 0)], 6: [("qk2", 1)], 9: [("qk2", 4)], 99: [("qk2", 2), ("qk2", 3)]}
CROSS_SPLITS = (4, 5, 8, 9)
LATE_SPLITS = (9, 10, 14, 15)
O2_GROUPS = (2, 3, 0, 1), (0, 1, 2, 3)
O2_CHUNKS = (KD // 2, 0), (0, KD // 2)
NBUCKET = 32
NBIAS = HA + HB + HC
BIG = 1e30
SENTINEL = -3e38
SCALE = HD ** -0.5
EPS1, EPS2 = 1e-5, 1e-6
LAM_INIT = 0.8 - 0.6
TWO_PI = 2.0 * np.pi
PI_HI, PI_MID = 6.28125, float(np.float32(TWO_PI - 6.28125))
PI_LO = float(np.float32(TWO_PI - 6.28125 - np.float64(np.float32(TWO_PI - 6.28125))))
ROUND = 12582912.0

CH = 2048
RAW = 3
HALF = CH // 2
HL = 4

C_ID, C_ONE, C_TRI, C_SBM, C_ADM, C_HOT, C_INV = 0, 128, 256, 384, 768, 1024, 1536
C_COLS = 1544
M_COLS = 3 * P + 3 * SEQ
BAND_PARTS = 7
BAND_W = 512
PITCH = 512


def shape_constants():
    c = np.zeros((P, C_COLS), np.float32)
    i = np.arange(P)
    c[:, C_ID:C_ID + P] = np.eye(P)
    c[:, C_ONE:C_ONE + P] = 1.0
    c[:, C_TRI:C_TRI + P] = i[:, None] >= i[None, :]
    q = np.arange(SEQ)
    c[:, C_SBM:C_SBM + SEQ] = BIG * (i[:, None] >= q[None, :])
    c[:, C_SBM + SEQ:C_SBM + SEQ + P] = BIG * (i[:, None] >= i[None, :])
    c[:64, C_ADM + 192:C_ADM + 256] = -BIG
    r = np.arange(383)
    rel = r - 255
    n = np.abs(rel)
    nf = np.maximum(n, 1).astype(np.float32)
    large = 8 + (np.log(nf / np.float32(8)) / np.float32(np.log(128.0)) * np.float32(8)).astype(np.int32)
    bucket = np.where(rel > 0, 16, 0) + np.where(n < 8, n, np.minimum(large, 15))
    c[bucket, C_HOT + r] = 1.0
    inv = np.float32(500000.0) ** (-np.arange(0, 16, 2, dtype=np.float32) / np.float32(16))
    c[:, C_INV:C_INV + 8] = inv
    m = np.zeros((P, M_COLS), np.float32)
    for qt in range(TT):
        nk = P * (qt + 1)
        for g in range(NG):
            gap = (qt * P + i)[:, None] - np.arange(nk)[None, :]
            ok = (gap >= 0) & (gap <= DIL_WINDOW[g]) & (gap % DIL[g] == 0)
            at = (0, 3 * P)[qt] + g * nk
            m[:, at:at + nk] = BIG * ~ok
    return c, m


class Plan:

    def __init__(self):
        self.chunks = []
        self.jobs = {}
        self.landed = []
        self.slot_total = [0] * RAW
        self.groups = {}
        self.by_number = []
        self.n_act = self.n_dve = 0

    def job(self, key, pieces):
        ids = []
        for kc, n, srcs in pieces:
            s = len(self.chunks) % RAW
            self.slot_total[s] += 16 * len(srcs)
            ids.append(len(self.chunks))
            self.chunks.append((kc, n, srcs))
            self.landed.append(self.slot_total[s])
        self.jobs[key] = ids

    def group(self, key, mode):
        self.n_act += mode in ("act", "split")
        self.n_dve += mode in ("dve", "split")
        self.groups[key] = len(self.by_number)
        self.by_number.append((mode, self.n_act, self.n_dve))


def build_network(nc, a, out):
    plan = Plan()

    def rows(w, k0, kc, c0, n):
        return w[k0 * P:(k0 + kc) * P, c0:c0 + n].rearrange("(k p) n -> p k n", p=P)

    def wide(w, c0, n, ks=(0, KD // 2)):
        return [(KD // 2, n, [(0, n, rows(w, k, KD // 2, c0, n))]) for k in ks]

    def tall(w, r0, k):
        return [(2, D, [(0, D, rows(w, r0 // P + j, 2, 0, D))]) for j in range(0, k, 2)]

    plan.group("gains", "act")
    for l in range(DEPTH):
        w = a["w_in"][l]
        for g in range(4):
            plan.group(("x1", l, g), "split")
        if l == 0:
            plan.group("conv", "act")
            plan.group("bias", "act")
        for j in range(QKV1 // 512):
            plan.job(("in1", l, j), wide(w, 512 * j, 512))
        for i in range(NGC):
            plan.job(("gate", l, i), [(KD, GC, [(0, GC, rows(w, 0, KD, QKV1 + GC * i, GC))])])
        for g in range(8):
            plan.group(("qk1", l, g), "act" if g % 2 else "dve")
        for g in ("b", "a"):
            plan.group(("y1", l, g), "split")
        plan.job(("pb", l), tall(a["w_proj_b"][l], 0, 2))
        plan.job(("pa", l), tall(a["w_proj_a"][l], 0, 2))
        for g in range(4):
            plan.group(("mix", l, g), "split")
        for j in range(2):
            plan.job(("out1", l, j), wide(a["w_out"][l], 512 * j, 512))
        for g in range(4):
            plan.group(("xf", l, g), "split")

        def up(b):
            w = a["w_up"][l]
            plan.job(("up", l, b), [(4, 2 * FB, [(0, FB, rows(w, k, 4, b * FB, FB)),
                                                (FB, FB, rows(w, k, 4, FF1 + b * FB, FB))]) for k in (0, 4)])

        def down(b):
            plan.job(("down", l, b), tall(a["w_down"][l], b * FB, 2))

        up(0)
        for b in range(NFB):
            plan.group(("ta", l, b), "dve")
            plan.group(("tb", l, b), "dve")
            if b + 1 < NFB:
                up(b + 1)
            if b:
                down(b - 1)
        down(NFB - 1)
    for l in range(DEPTH):
        even = l % 2 == 0
        for g in range(4):
            plan.group(("mem", l, g), "split")
        plan.job(("kv", l), wide(a["xa_wkv_2"][l], 0, 512))
        for g in range(4):
            plan.group(("x2", l, g), "split")
        w, cols = (a["ev_w_in_2"][0], EV_COLS) if even else (a["od_w_in_2"][0], OD_COLS)
        for j in IN2_ORDER[l % 2]:
            plan.job(("in2", l, j), wide(w, 512 * j, min(512, cols - 512 * j)))
        for keys in (EVEN_GROUPS if even else ODD_GROUPS).values():
            for k in keys:
                plan.group((k[0], l) + k[1:], "dve" if k[0] == "qk2" and k[1] % 2 == 0 else "act")
        for g in O2_GROUPS[l % 2]:
            plan.group(("o2", l, g), "split")
        w = a["ev_w_out_2"][0] if even else a["od_w_out_2"][0]
        for j in range(2):
            plan.job(("out2", l, j), wide(w, 512 * j, 512, O2_CHUNKS[l % 2]))
        plan.group(("qkx", l, 0), "dve")
        for g in range(4):
            plan.group(("xx", l, g), "split")
        plan.job(("wq", l), wide(a["xa_wq_2"][l], 0, 256))
        plan.group(("qkx", l, 1), "act")
        plan.group(("ox", l), "split")
        plan.job(("wo", l), tall(a["xa_wo_2"][l], 0, 2))
        for g in range(4):
            plan.group(("xm", l, g), "split")
        plan.job(("w1", l, 0), wide(a["mlp_w1_2"][l], 0, MB))
        for b in range(NMB):
            for g in range(2):
                plan.group(("tm", l, b, g), "split")
            if b + 1 < NMB:
                plan.job(("w1", l, b + 1), wide(a["mlp_w1_2"][l], MB * (b + 1), MB))
            plan.job(("w2", l, b), tall(a["mlp_w2_2"][l], MB * b, MB // P))
    NCH = len(plan.chunks)

    norms = []
    for l in range(DEPTH):
        norms += [("x1", l), ("xf", l)]
    norms += [("mem", 0), ("final",)]
    for l in range(DEPTH):
        norms += [("x2", l)] + ([("ckv", l)] if l % 2 == 0 else [])
        norms += [("sub", l)] * (l % 2 == 0)
        norms += [("y2", l), ("xx", l), ("yx", l), ("xm", l)]
        norms += [("mem", l + 1)] * (l + 1 < DEPTH) + [("ym", l)]
    NORM = {k: i for i, k in enumerate(norms)}
    GAIN_ROWS = 18
    gain_row = {}
    for l in range(DEPTH):
        gain_row["x1", l] = l
        gain_row["xf", l] = 2 + l
        gain_row["x2", l], gain_row["xx", l], gain_row["xm", l] = 4 + 6 * l, 6 + 6 * l, 8 + 6 * l
        gain_row["mem", l] = 16 + l

    with ExitStack() as ctx:
        def sb(name, shape, dt=F32):
            return ctx.enter_context(nc.sbuf_tensor(name, shape, dt))

        def sem(name):
            return ctx.enter_context(nc.semaphore(name))

        cst = sb("cst", [P, C_COLS])
        raw = sb("raw", [P, RAW, CH])
        whi = sb("whi", [P, HL, HALF], F32R)
        wlo = sb("wlo", [P, HL, HALF], F32R)
        x = sb("x", [P, TT, D])
        ahi = sb("ahi", [P, KD, SEQ], F32R)
        alo = sb("alo", [P, KD, SEQ], F32R)
        mhi = sb("mhi", [P, KD, SEQ], F32R)
        mlo = sb("mlo", [P, KD, SEQ], F32R)
        proj = sb("proj", [P, TT, QKV1])
        region = sb("region", [P, 7296])
        qT = sb("qT", [P, 16, SEQ])
        work = sb("work", [P, 4608])
        o_nat = sb("o_nat", [P, TT, D])
        gain_b = sb("gain_b", [P, D])
        misc = sb("misc", [P, 528])
        gains = sb("gains", [P, KD, GAIN_ROWS])
        conv = sb("conv", [P, FF1 // P, 8])
        ss = sb("ss", [P, len(norms), 4])
        rstd = sb("rstd", [P, len(norms), 4])
        small = sb("small", [P, 16, 16])
        pos_i = sb("pos_i", [P, TT], I32)
        sel = sb("sel", [P, 3 * P], BF16)
        ident_b = sb("ident_b", [P, P], BF16)
        den = sb("den", [P, TT, 16])
        rden = sb("rden", [P, TT, 16])
        low = sb("low", [P, TT, 16])
        ps = ctx.enter_context(nc.psum_tensor("ps", [P, 8, 512], F32))
        band_dram = nc.dram_tensor("band", [NBIAS, P * (PITCH + 1) + PITCH], F32, kind="Internal").ap()

        ident = cst[:, C_ID:C_ID + P]
        ones = cst[:, C_ONE:C_ONE + P]
        tri = cst[:, C_TRI:C_TRI + P]
        gates = region[:, 0:4096].rearrange("p (t n) -> p t n", t=TT)
        gate_bias = region[:, 4096:6144]
        dil_mask = region[:, 6144:6144 + M_COLS]
        band = region[:, 0:4096].rearrange("p (h c) -> p h c", h=16)
        kvn = region[:, 4096:5120].rearrange("p (t n) -> p t n", t=TT)
        qiT = region[:, 3072:4096].rearrange("p (b n) -> p b n", b=4)
        kicT = region[:, 5120:5632].rearrange("p (b n) -> p b n", b=2)
        relu_i = region[:, 5632:6656].rearrange("p (s n) -> p s n", s=2)
        cand = region[:, 7040:7296], work[:, 2560:2816]
        eT = work[:, 3072:4608].rearrange("p (s n) -> p s n", s=2)
        nat = work[:, 0:2048].rearrange("p (s t n) -> p s t n", s=2, t=TT)
        cv = work[:, 2048:2560]
        sl = work[:, 2560:3072]
        ut = work[:, 3072:3584]
        junk = work[:, 3072:4096]
        junk2 = qT[:, 0:8, :].rearrange("p b n -> p (b n)")
        junk_act = work[:, 0:2048].rearrange("p (i n) -> p i n", i=4)
        ystep = work[:, 2048:4096].rearrange("p (t n) -> p t n", t=TT)
        rt = work[:, 0:1536].rearrange("p (i t h d) -> p i t h d", i=4, t=TT, h=24)
        gain_rows = work[0:GAIN_ROWS, 0:1024]
        conv_rows = work[0:8, 1024:1024 + FF1]
        band_rows = gain_b[0:NBIAS, 0:BAND_W]
        uk_nat = work[:, 0:512].rearrange("p (b n) -> p b n", b=4)
        ukT = work[:, 512:1024].rearrange("p (b n) -> p b n", b=4)
        uv = work[:, 1024:1536]
        kdup = work[:, 1536:2048]
        lam_rows = misc[:, 0:256]
        subln = misc[:, 256:384]
        akv = misc[:, 384:512]
        sinks = misc[:, 512:528]

        landed = [sem(f"landed{i}") for i in range(RAW)]
        cst_in = sem("cst_in")
        ident_in = sem("ident_in")
        gains_in = sem("gains_in")
        x_in = sem("x_in")
        rows_in = sem("rows_in")
        mask_in = sem("mask_in")
        bgate_in = sem("bgate_in")
        gainb_in = sem("gainb_in")
        mem_in = sem("mem_in")
        misc_in = sem("misc_in")
        small_w_in = sem("small_w_in")
        band_out = sem("band_out")
        band_in = sem("band_in")
        stored = sem("stored")
        hi_done = sem("hi_done")
        lo_done = sem("lo_done")
        pe_out = sem("pe_out")
        pe_grp = sem("pe_grp")
        grp_act = sem("grp_act")
        grp_dve = sem("grp_dve")
        ev_act = sem("ev_act")
        ev_dve = sem("ev_dve")
        x_ready = sem("x_ready")
        ss_ready = sem("ss_ready")
        rstd_ready = sem("rstd_ready")
        pool_chain = sem("pool_chain")
        chain = sem("chain")
        act_chain = sem("act_chain")
        rope_done = sem("rope_done")
        trig_arg = sem("trig_arg")
        trig_done = sem("trig_done")
        gate_pre = sem("gate_pre")
        gate_done = sem("gate_done")
        at_s = sem("at_s")
        at_t = sem("at_t")
        at_e = sem("at_e")
        at_x = sem("at_x")
        at_ya = sem("at_ya")
        at_yd = sem("at_yd")
        at_o = sem("at_o")
        o_ready = sem("o_ready")
        sb_z = sem("sb_z")
        sb_abs = sem("sb_abs")
        sb_ln = sem("sb_ln")
        sb_keep = sem("sb_keep")
        sb_sum = sem("sb_sum")
        sb_arg = sem("sb_arg")
        sb_att = sem("sb_att")
        sb_o = sem("sb_o")
        mixed = sem("mixed")
        silu_ready = sem("silu_ready")
        uhi = sem("uhi")
        ulo = sem("ulo")
        sq_ready = sem("sq_ready")
        relu_ready = sem("relu_ready")
        idx_used = sem("idx_used")
        sel_ready = sem("sel_ready")
        diff_taken = sem("diff_taken")
        ident_ready = sem("ident_ready")
        c_ready = sem("c_ready")
        kdup_ready = sem("kdup_ready")
        lam_arg = sem("lam_arg")
        lam_exp = sem("lam_exp")
        sink_arg = sem("sink_arg")
        sink_exp = sem("sink_exp")
        sub_sq = sem("sub_sq")
        block = ctx.enter_context(nc.Block())

        def yb(tt, c):
            return 2 * tt + c % 2

        def in2_banks(l, p):
            late = (((4, (6, 2)), (5, (7, 3))), ((1, (1, 6)), (2, (7, 3))))[l % 2]
            return dict(late).get(p, (yb(0, p), yb(1, p)))

        def y2b(tt, c):
            return 6 * c + tt

        def unit(qt, slot, w, parts, bias, pv, o_bank, o_col, sel_mask=None):
            return dict(qt=qt, slot=slot, w=w, parts=parts, bias=bias, pv=pv, o_bank=o_bank, o_col=o_col, sel=sel_mask)

        def half(i):
            return 64 * (i % 2)

        def dilated_units():
            us = []
            for qt in range(TT):
                nk = P * (qt + 1)
                for h in range(HG):
                    parts, pv = [], []
                    for g in range(NG):
                        i = g * HG + h
                        b = half(i)
                        parts.append((g * nk, nk, qT[b:b + 64, i // 2, qt * P:qt * P + P], qT[b:b + 64, 6 + i // 2, 0:nk]))
                        pv += [proj[:, s, 1536 + i * HD:1536 + i * HD + HD] for s in range(qt + 1)]
                    at = (0, 3 * P)[qt]
                    us.append(unit(qt, h, 3 * nk, parts, dil_mask[:, at:at + 3 * nk], pv, 6, (qt * HG + h) * HD))
            return us

        def head_unit(qt, q, k, nk_of, bias, v, slot, o, masked):
            nk = nk_of(qt)
            return unit(qt, slot, nk, [(0, nk, q(qt), k(nk))], bias(qt, nk), [v(s) for s in range(nk // P)], *o(qt),
                        sel[:, (0, P)[qt]:(0, P)[qt] + nk] if masked else None)

        def out_at(col):
            return lambda qt: ((6, 2)[qt] + col // 512, col % 512)

        def causal(qt):
            return P * (qt + 1)

        def band_of(h):
            return lambda qt, nk: band[:, h, SEQ - nk:SEQ]

        def even_heads():
            hs = []
            for i in range(2 * HB):
                b = half(i)
                hs.append((lambda qt, i=i, b=b: qT[b:b + 64, i // 2, qt * P:qt * P + P],
                           lambda nk, i=i, b=b: qT[b:b + 64, 4 + i // 2, 0:nk], causal, band_of(HA + i // 2),
                           lambda s, i=i: proj[:, s, 2248 + P * (i // 2):2248 + P * (i // 2) + P], i, out_at(P * i), False))
            return hs

        def dsa_heads():
            hs = []
            for i in range(HA):
                b = half(i)
                hs.append((lambda qt, i=i, b=b: qT[b:b + 64, 8 + i // 2, qt * P:qt * P + P],
                           lambda nk, i=i, b=b: qT[b:b + 64, 12 + i // 2, 0:nk], causal, band_of(i),
                           lambda s, i=i: proj[:, s, HD * i:HD * i + HD], 2 * HB + i, out_at(HD * i), True))
            return hs

        def odd_heads():
            hs = []
            for i in range(HC):
                b, kv = half(i), i // 8
                hs.append((lambda qt, i=i, b=b: qT[b:b + 64, i // 2, qt * P:qt * P + P],
                           lambda nk, kv=kv, b=b: qT[b:b + 64, 8 + kv, 0:nk], causal, band_of(i),
                           lambda s, kv=kv: proj[:, s, 1152 + HD * kv:1152 + HD * kv + HD], i, out_at(HD * i), False))
            return hs

        def cross_heads():
            hs = []
            for i in range(HX):
                b = half(i)
                hs.append((lambda qt, i=i, b=b: qT[b:b + 64, i // 2, qt * P:qt * P + P],
                           lambda nk, i=i, b=b: qT[b:b + 64, 2 + i // 2, 0:nk], lambda qt: SEQ, lambda qt, nk: None,
                           lambda s, i=i: kvn[:, s, 256 + HD * i:256 + HD * i + HD], i, out_at(HD * i), False))
            return hs

        stages = []
        for l in range(DEPTH):
            stages.append((("dil", l), dilated_units()))
        for l in range(DEPTH):
            if l % 2 == 0:
                heads = even_heads() + dsa_heads()
            else:
                heads = odd_heads()
            us = [head_unit(qt, *h) for h in heads for qt in range(TT)]
            stages.append((("even" if l % 2 == 0 else "odd", l), us))
            stages.append((("cross", l), [head_unit(qt, *h) for qt in range(TT) for h in cross_heads()]))
        first_unit, n_units = {}, 0
        units_of = {}
        for k, us in stages:
            for d in us:
                d["wide"] = us[-1]["w"] > SEQ
            first_unit[k], units_of[k] = n_units, us
            n_units += len(us)

        def copies(u):
            return u // 2 + 1, (u + 1) // 2

        def wait_copied(eng, u):
            d, s = copies(u)
            if u % 2 == 0:
                eng.wait_ge(at_yd, d)
            else:
                eng.wait_ge(at_ya, s)

        def x_count(what, l=0):
            if what == "mix":
                return 2 * (2 * l + 1)
            if what == "ffn":
                return 2 * (2 * l + 2)
            if what == "final":
                return 2 * (2 * DEPTH + 1)
            return 2 * (2 * DEPTH + 1 + 3 * l + ("y2", "yx", "ym").index(what) + 1)


        def evs_act(l, what, b=None):
            per1 = 2 * (6 + NFB)
            if b is not None:
                return per1 * l + 12 + 2 * (b + 1)
            return per1 * l + 2 * (what + 1)

        def evs_act2(l, what, j=0):
            base = 2 * (6 + NFB) * DEPTH
            for i in range(l):
                base += 2 * (-(-(EV_COLS if i % 2 == 0 else OD_COLS) // 512) + 2)
            nj = -(-(EV_COLS if l % 2 == 0 else OD_COLS) // 512)
            place = IN2_ORDER[l % 2].index(j) if what == "in2" else 0
            return base + 2 * (1 + {"kv": 0, "in2": 1 + place, "wq": 1 + nj}[what])

        order = [(k, l) for l in range(DEPTH) for k in ("sb", "dil")]
        for l in range(DEPTH):
            order += [("diff", l), ("dsa", l)] if l % 2 == 0 else [("odd a", l), ("odd b", l)]
            order.append(("cross", l))
        o_counts = {k: 2 * (i + 1) for i, k in enumerate(order)}

        rs_count, total = {}, 0
        for k in norms:
            total += 2 if k[0] == "sub" else 1
            rs_count[k] = total

        def sbk(h):
            return work[:, 3072 + 384 * h:3072 + 384 * (h + 1)]

        def sba(h):
            return work[:, 1536 + 384 * h:1536 + 384 * (h + 1)]

        def sbz(h):
            return work[:, 384 * h:384 * (h + 1)]

        def kdup2(tt, kv):
            return kdup[:, (2 * tt + kv) * P:(2 * tt + kv + 1) * P]

        def lag_of(key):
            return 2 if key[0] == "dil" else 3

        def slots_of(key):
            return 2 if key[0] == "dil" else 4

        def step_of(first, u, d):
            at = first + (768 * (u % 2) if d["wide"] else SEQ * (u % 4))
            return work[:, at:at + d["w"]]

        def turned(u, d):
            if d["w"] > SEQ or d["wide"]:
                return ps[:, 4:6, :].rearrange("p b n -> p (b n)")[:, 0:d["w"]]
            return ps[:, 4 + u % 2, 0:d["w"]]

        def group_ready(eng, key):
            eng.wait_ge(pe_grp, plan.groups[key] + 1)

        @block.sync
        def _(sp):
            sp.dma_start(ident, a["cst"][:, C_ID:C_ID + P]).then_inc(ident_in, 16)
            sp.dma_start(x[:], a["x"][0].rearrange("(t p) d -> p t d", p=P)).then_inc(x_in, 16)
            sp.dma_start(gain_rows[0:2, :], a["norm_mix"]).then_inc(gains_in, 16)
            sp.dma_start(gain_rows[2:4, :], a["norm_ffn"]).then_inc(gains_in, 16)
            sp.dma_start(gain_rows[4:16, :], a["norm_g_2"].rearrange("l i d -> (l i) d")).then_inc(gains_in, 16)
            sp.dma_start(gain_rows[16:18, :], a["xa_mem_norm_2"]).then_inc(gains_in, 16)
            for n in range(NCH):
                kc, cols, srcs = plan.chunks[n]
                if n == RAW:
                    sp.dma_start(cst[:, P:], a["cst"][:, P:]).then_inc(cst_in, 16)
                    sp.dma_start(conv_rows[0:6, :], a["conv_w"].rearrange("l i d -> (l i) d")).then_inc(rows_in, 16)
                    sp.dma_start(conv_rows[6:8, :], a["conv_b"]).then_inc(rows_in, 16)
                    sp.dma_start(work[0:NBUCKET, 3840:3840 + NBIAS], a["rel_bias_table_2"]).then_inc(rows_in, 16)
                if n >= RAW:
                    sp.wait_ge(hi_done, 2 * (n - RAW + 1))
                    sp.wait_ge(lo_done, 2 * (n - RAW + 1))
                dst = raw[:, n % RAW, 0:kc * cols].rearrange("p (k n) -> p k n", k=kc)
                for c0, w, src in srcs:
                    sp.dma_start(dst[:, :, c0:c0 + w], src).then_inc(landed[n % RAW], 16)
            sp.wait_ge(x_ready, x_count("ym", DEPTH - 1))
            sp.dma_start(out[0].rearrange("(t p) d -> p t d", p=P), x[:]).then_inc(stored, 16)
            sp.wait_ge(stored, 16)

        @block.gpsimd
        def _(pool):
            pool.dma_start(pos_i[:], a["positions"].rearrange("a (t p) -> p (a t)", p=P),
                           allow_slow_non_contiguous=True).then_inc(misc_in, 16)
            n_chain = [0]

            def link(ins):
                n_chain[0] += 1
                ins.then_inc(pool_chain, 1)
                pool.wait_ge(pool_chain, n_chain[0])

            link(nc.gpsimd.memset(small[:, 0, :], -0.5))
            n_ss = [0]

            def root(key, width, count, eps, halves=False, cols=4):
                i = NORM[key]
                n_ss[0] += count
                pool.wait_ge(ss_ready, n_ss[0])
                if halves:
                    link(nc.gpsimd.tensor_tensor(ss[:, i, 0:2], ss[:, i, 0:2], ss[:, i, 2:4], ALU.add))
                    cols = 2
                link(nc.gpsimd.tensor_scalar(ss[:, i, 0:cols], ss[:, i, 0:cols], 1.0 / width, eps, ALU.mult, ALU.add))
                nc.gpsimd.tensor_tensor(rstd[:, i, 0:cols], ss[:, i, 0:cols], small[:, 0, 0:cols], ALU.pow).then_inc(rstd_ready, 1)

            def band_store(h0, n):
                line = P * (PITCH + 1) + PITCH
                pool.dma_start(bass.AP(band_dram.tensor, h0 * line, [[line, n], [PITCH + 1, P], [1, PITCH]]),
                               band_rows[h0:h0 + n].unsqueeze(1).to_broadcast([n, P, PITCH])).then_inc(band_out, 16)

            def band_load(h0, n):
                return bass.AP(band_dram.tensor, h0 * (P * (PITCH + 1) + PITCH) + P - 1,
                               [[PITCH, P], [P * (PITCH + 1) + PITCH, n], [1, SEQ]])

            for l in range(DEPTH):
                root(("x1", l), D, 2, EPS1, cols=2)
                if l == 0:
                    pool.dma_start(dil_mask, a["masks"]).then_inc(mask_in, 16)
                    pool.dma_start(gate_bias, a["b_gate"][0].partition_broadcast(P)).then_inc(bgate_in, 16)
                    pool.wait_ge(grp_act, plan.by_number[plan.groups["bias"]][1])
                    for i in range(BAND_PARTS):
                        pool.wait_ge(pe_out, 4 * plan.jobs["in1", 0, 2][-1] + 12 * i)
                        band_store(NBIAS // BAND_PARTS * i, NBIAS // BAND_PARTS)
                    pool.wait_ge(band_out, 16 * BAND_PARTS)
                    pool.dma_start(gain_b[:], a["norm_final"].partition_broadcast(P)).then_inc(gainb_in, 16)
                    pool.wait_ge(gate_pre, 2 * NGC)
                    pool.dma_start(gate_bias, a["b_gate"][1].partition_broadcast(P)).then_inc(bgate_in, 16)
                root(("xf", l), D, 2, EPS1, cols=2)
            pool.wait_ge(pe_grp, plan.groups["mix", DEPTH - 1, 3] + 1)
            pool.dma_start(o_nat[:], a["mem_2"][0].rearrange("(t p) d -> p t d", p=P)).then_inc(mem_in, 16)
            root(("mem", 0), D, 2, EPS2, cols=2)
            root(("final",), D, 2, EPS1, cols=2)
            n_final = x_count("final")
            pool.wait_ge(x_ready, n_final)
            pool.dma_start(band[:, 0:12, :], band_load(0, 12)).then_inc(band_in, 16)
            pool.dma_start(gain_b[:], a["norm_g_2"][0, 1].partition_broadcast(P)).then_inc(gainb_in, 16)
            pool.dma_start(lam_rows, a["ev_b_lambda_2"][0].rearrange("a d -> (a d)").partition_broadcast(P)).then_inc(misc_in, 16)
            pool.dma_start(subln, a["ev_b_subln_2"][0].partition_broadcast(P)).then_inc(misc_in, 16)
            pool.dma_start(akv, a["ev_a_kv_norm_2"][0].partition_broadcast(P)).then_inc(misc_in, 16)
            pool.dma_start(sinks, a["od_sinks_2"][0].partition_broadcast(P)).then_inc(misc_in, 16)
            root(("x2", 0), D, 2, EPS2, cols=2)
            pool.dma_start(uk_nat, a["ev_a_w_uk_2"][0].rearrange("(b h) d l -> (h d) b l", h=2)).then_inc(small_w_in, 16)
            pool.dma_start(uv.rearrange("p (h d) -> p h d", h=HA), a["ev_a_w_uv_2"][0].rearrange("h l d -> l h d")).then_inc(small_w_in, 16)
            for l in range(DEPTH):
                if l > 0:
                    pool.wait_ge(x_ready, x_count("ym", l - 1))
                    pool.dma_start(gain_b[:], a["norm_g_2"][l, 1].partition_broadcast(P)).then_inc(gainb_in, 16)
                    pool.dma_start(band[:, 0:16, :], band_load(HA + HB, HC)).then_inc(band_in, 16)
                    root(("x2", l), D, 2, EPS2, cols=2)
                if l % 2 == 0:
                    root(("ckv", l), P, 2, EPS2, cols=2)
                    for qt in range(TT):
                        i = NORM["sub", l]
                        n_ss[0] += 1
                        pool.wait_ge(ss_ready, n_ss[0])
                        t = small[:, 2 + qt, 0:HB]
                        link(nc.gpsimd.tensor_scalar(t, t, 1.0 / P, EPS2, ALU.mult, ALU.add))
                        nc.gpsimd.tensor_tensor(small[:, 4 + qt, 0:HB], t, small[:, 0, 0:HB], ALU.pow).then_inc(rstd_ready, 1)
                for k, key in enumerate(("y2", "yx", "ym")):
                    if key == "ym" and l + 1 < DEPTH:
                        pool.dma_start(o_nat[:], a["mem_2"][0].rearrange("(t p) d -> p t d", p=P)).then_inc(mem_in, 16)
                        root(("mem", l + 1), D, 2, EPS2, cols=2)
                    root((key, l), D, 4, EPS2, halves=True)
                    pool.wait_ge(x_ready, x_count(key, l))
                    if k < 2:
                        pool.dma_start(gain_b[:], a["norm_g_2"][l, 3 + 2 * k].partition_broadcast(P)).then_inc(gainb_in, 16)
                        root((("xx", "xm")[k], l), D, 2, EPS2, cols=2)

        @block.tensor
        def _(pe):
            def half_chunk(n, h, hi, lo, k0, outs, first, final, stream=None, at=(0, 0)):
                kc, cols, _ = plan.chunks[n]
                kh, m = kc // 2, 2 * n + h
                if stream:
                    place = stream["place"]((k0 + (h + 1) * kh - 1) // 2)
                    stream["need"](place)
                pe.wait_ge(lo_done, m + 1)
                wh = whi[:, m % HL, 0:kh * cols].rearrange("p (k n) -> p k n", k=kh)
                wl = wlo[:, m % HL, 0:kh * cols].rearrange("p (k n) -> p k n", k=kh)
                for tt in range(TT):
                    rows_ = slice(tt * P, tt * P + P)
                    for k in range(kh):
                        kx = k0 + h * kh + k
                        for c0, w, bank in outs[tt]:
                            o = ps[:, bank, at[tt]:at[tt] + w]
                            nc.tensor.matmul(o, hi[:, kx, rows_], wh[:, k, c0:c0 + w], start=first and h == 0 and k == 0 and (tt == 0 or at[1] == 0),
                                             stop=False)
                        for c0, w, bank in outs[tt]:
                            o = ps[:, bank, at[tt]:at[tt] + w]
                            nc.tensor.matmul(o, hi[:, kx, rows_], wl[:, k, c0:c0 + w], start=False, stop=False)
                        for c0, w, bank in outs[tt]:
                            o = ps[:, bank, at[tt]:at[tt] + w]
                            mm = nc.tensor.matmul(o, lo[:, kx, rows_], wh[:, k, c0:c0 + w], start=False,
                                                  stop=final and h == 1 and k == kh - 1 and (tt == 1 or at[1] == 0))
                    mm.then_inc(pe_out, 1)
                if stream:
                    stream["turn_to"](place + 2)

            def wide_job(key, hi, lo, banks, n=512, stream=None, before={}, ks=(0, KD // 2)):
                ids = plan.jobs[key]
                for j, i in enumerate(ids):
                    for h in range(2):
                        if 2 * j + h in before:
                            before[2 * j + h]()
                        half_chunk(i, h, hi, lo, ks[j], [[(0, n, banks[tt])] for tt in range(TT)], j == 0, j == len(ids) - 1, stream)

            def tall_job(key, hi, lo, k0, bank, first, final, between=None, stream=None):
                ids = plan.jobs[key]
                for j, i in enumerate(ids):
                    outs = [[(0, 512, bank(tt, 0)), (512, 512, bank(tt, 1))] for tt in range(TT)]
                    for h in range(2):
                        half_chunk(i, h, hi, lo, k0 + 2 * j, outs, first and j == 0, final and j == len(ids) - 1, stream)
                        if between and 2 * j + h == len(ids) - 1:
                            between()

            def group_bank(key):
                t = plan.groups[key]
                if t >= 2:
                    mode, na, nd = plan.by_number[t - 2]
                    if mode == "act":
                        pe.wait_ge(grp_act, na)
                    else:
                        pe.wait_ge(grp_dve, nd)
                return ps[:, 4 + t % 2, :]

            def turn_blocks(key, srcs):
                bank = group_bank(key)
                for j, src in enumerate(srcs):
                    mm = nc.tensor.transpose(bank[:, j * P:j * P + P], src, ident)
                mm.then_inc(pe_grp, 1)

            def stream(tag, l, src, ready, gs=(0, 1, 2, 3)):
                turned, waited = [0], [0]

                def turn_to(i):
                    while turned[0] <= min(i, 3):
                        t = turned[0]
                        if t % 2 == 0:
                            ready(t // 2)
                        g = gs[t]
                        turn_blocks((tag, l, g), [src[:, tt, (2 * g + b) * P:(2 * g + b + 1) * P] for b in range(2) for tt in range(TT)])
                        turned[0] += 1

                def need(i):
                    while waited[0] <= i:
                        turn_to(waited[0] + 1)
                        pe.wait_ge(grp_dve, plan.by_number[plan.groups[tag, l, gs[waited[0]]]][2])
                        waited[0] += 1

                return dict(turn_to=turn_to, need=need, place=gs.index)

            def x_half(n):
                return lambda h: pe.wait_ge(x_ready, n - 1 + h)

            def attention(key, each=None):
                us, u0 = units_of[key], first_unit[key]
                wide_units = us[-1]["w"] > SEQ

                def s_bank(u):
                    return 2 * (u % 2) if wide_units else u % 2

                def scores(i):
                    u, d = u0 + i, us[i]
                    if u >= 2:
                        pe.wait_ge(at_t, u - 1)
                    flat = ps[:, s_bank(u):s_bank(u) + (2 if wide_units else 1), :].rearrange("p b n -> p (b n)")
                    for c0, n, q, k in d["parts"]:
                        mm = nc.tensor.matmul(flat[:, c0:c0 + n], q, k, start=True, stop=d["sel"] is None)
                    if d["sel"] is not None:
                        mm = nc.tensor.matmul(flat[:, 0:d["w"]], ident_b[:], d["sel"], start=False, stop=True)
                    mm.then_inc(at_s, 1)

                def turn(i):
                    u, d = u0 + i, us[i]
                    pe.wait_ge(at_e, u + 1)
                    back = 1 if wide_units else 2
                    if u >= back:
                        wait_copied(pe, u - back)
                    for b in range(d["w"] // P):
                        at = b * P
                        o = ps[:, 4 + at // 512, at % 512:at % 512 + P] if wide_units else ps[:, 4 + u % 2, at:at + P]
                        mm = nc.tensor.transpose(o, step_of(1536, u, d)[:, at:at + P], ident)
                    mm.then_inc(at_x, 1)

                def values(i):
                    u, d = u0 + i, us[i]
                    wait_copied(pe, u)
                    vw = d["pv"][0].shape[-1]
                    o = ps[:, d["o_bank"], d["o_col"]:d["o_col"] + vw]
                    for b, v in enumerate(d["pv"]):
                        mm = nc.tensor.matmul(o, eT[:, u % 2, b * P:b * P + P], v, start=b == 0, stop=b == len(d["pv"]) - 1)
                    mm.then_inc(at_o, 1)

                n, lag = len(us), lag_of(key)
                for i in range(n + lag + 1):
                    if i < n:
                        scores(i)
                    if lag <= i < n + lag:
                        turn(i - lag)
                    if lag + 1 <= i:
                        values(i - lag - 1)
                    if each:
                        each(i)

            def memory_stream(l):
                sm = stream("mem", l, o_nat, lambda h: pe.wait_ge(mem_in, 16 * (l + 1)))
                sm["turn_to"](1)
                return sm

            pe.wait_ge(ident_in, 16)
            pe.wait_ge(gains_in, 16 * 4)
            bank = group_bank("gains")
            for k in range(KD):
                mm = nc.tensor.transpose(bank[:, k * GAIN_ROWS:(k + 1) * GAIN_ROWS], gain_rows[:, k * P:k * P + P], ident[0:GAIN_ROWS, 0:GAIN_ROWS])
            mm.then_inc(pe_grp, 1)

            def turn_conv():
                pe.wait_ge(cst_in, 16)
                pe.wait_ge(rows_in, 16 * 3)
                bank = group_bank("conv")
                for k in range(FF1 // P):
                    mm = nc.tensor.transpose(bank[:, k * 8:(k + 1) * 8], conv_rows[:, k * P:k * P + P], ident[0:8, 0:8])
                mm.then_inc(pe_grp, 1)
                bank = group_bank("bias")
                nc.tensor.matmul(bank[0:NBIAS, :], work[0:NBUCKET, 3840:3840 + NBIAS], cst[0:NBUCKET, C_HOT:C_HOT + BAND_W],
                                 start=True, stop=True).then_inc(pe_grp, 1)

            for l in range(DEPTH):
                sx = stream("x1", l, x, x_half(x_count("ffn", l - 1)) if l else lambda h: pe.wait_ge(x_in, 16))

                def turn_qk(g):
                    c0 = 2 * P * g if g < 6 else 2304 + 2 * P * (g - 6)
                    turn_blocks(("qk1", l, g), [proj[:, tt, c0 + b * P:c0 + (b + 1) * P] for b in range(2) for tt in range(TT)])

                def gate_half(f):
                    c, h = divmod(f, 2)
                    if h == 0 and c:
                        pe.wait_ge(gate_pre, 2 * (NGC * l + c))
                    half_chunk(plan.jobs["gate", l, c][0], h, ahi, alo, 0, [[(0, GC, 7)], [(0, GC, 7)]], True, True, None, (0, GC))

                for j in range(QKV1 // 512):
                    if j >= 2:
                        pe.wait_ge(ev_act, evs_act(l, j - 2))
                    wide_job(("in1", l, j), ahi, alo, [yb(0, j), yb(1, j)], stream=sx if j == 0 else None)
                    if l == 0 and j == 0:
                        turn_conv()
                    if j >= 3:
                        if j == 3:
                            pe.wait_ge(rope_done, l + 1)
                        turn_qk(2 * j - 6)
                        turn_qk(2 * j - 5)
                gate_half(0)
                pe.wait_ge(ev_act, evs_act(l, 5))
                turn_qk(6)
                turn_qk(7)
                gate_half(1)
                pe.wait_ge(grp_act, plan.by_number[plan.groups["qk1", l, 7]][1])
                pe.wait_ge(grp_dve, plan.by_number[plan.groups["qk1", l, 6]][2])
                for h in range(HG):
                    b, blk = half(h), 12 + h // 2
                    z = ps[:, h, 0:384]
                    nc.tensor.matmul(z[:, 0:SEQ], qT[b:b + 64, blk + 2, 0:P], qT[b:b + 64, blk, :], start=True, stop=True)
                    nc.tensor.matmul(z[:, SEQ:384], qT[b:b + 64, blk + 2, P:SEQ], qT[b:b + 64, blk, P:SEQ], start=True, stop=True).then_inc(sb_z, 1)
                for f in (2, 3, 4):
                    gate_half(f)
                for h in range(HG):
                    pe.wait_ge(sb_keep, HG * l + h + 1)
                    keep = sbk(h)
                    c = ps[:, h, 0:384]
                    nc.tensor.matmul(c[:, 0:P], tri, keep[:, 0:P], start=True, stop=True)
                    nc.tensor.matmul(c[:, P:SEQ], tri, keep[:, P:SEQ], start=True, stop=False)
                    nc.tensor.matmul(c[:, P:SEQ], ones, keep[:, SEQ:384], start=False, stop=True)
                    nc.tensor.matmul(c[:, SEQ:384], tri, keep[:, SEQ:384], start=True, stop=True).then_inc(sb_sum, 1)
                gate_half(5)
                for h in range(HG):
                    pe.wait_ge(sb_att, HG * l + h + 1)
                    att = sba(h)
                    v = [proj[:, s, 2816 + h * HD:2816 + (h + 1) * HD] for s in range(TT)]
                    nc.tensor.matmul(ps[:, 6, h * HD:(h + 1) * HD], att[:, 0:P], v[0], start=True, stop=True)
                    at = (HG + h) * HD
                    nc.tensor.matmul(ps[:, 6, at:at + HD], att[:, P:SEQ], v[0], start=True, stop=False)
                    nc.tensor.matmul(ps[:, 6, at:at + HD], att[:, SEQ:384], v[1], start=False, stop=True).then_inc(sb_o, 1)

                def turn_branch(g):
                    c0 = 512 * ("a", "b").index(g)
                    turn_blocks(("y1", l, g), [o_nat[:, tt, c0 + b * P:c0 + (b + 1) * P] for b in range(2) for tt in range(TT)])

                for f in (6, 7):
                    gate_half(f)
                pe.wait_ge(o_ready, o_counts["sb", l])
                turn_branch("b")

                def between_heads(i):
                    if 8 + i < 2 * NGC:
                        gate_half(8 + i)
                    if i == 1:
                        pe.wait_ge(grp_dve, plan.by_number[plan.groups["y1", l, "b"]][2])

                attention(("dil", l), between_heads)
                pe.wait_ge(at_t, first_unit["dil", l] + len(units_of["dil", l]))
                tall_job(("pb", l), mhi, mlo, 2, lambda tt, c: yb(tt, c), True, True)
                pe.wait_ge(o_ready, o_counts["dil", l])
                turn_branch("a")
                pe.wait_ge(grp_dve, plan.by_number[plan.groups["y1", l, "a"]][2])
                pe.wait_ge(gate_pre, 2 * NGC * (l + 1))
                tall_job(("pa", l), mhi, mlo, 0, lambda tt, c: 4 + 2 * c + tt, True, True)
                sx = stream("mix", l, o_nat, lambda h: pe.wait_ge(mixed, 4 * l + 2 * h + 2))
                sf = stream("xf", l, x, x_half(x_count("mix", l)))
                wide_job(("out1", l, 0), mhi, mlo, [yb(0, 0), yb(1, 0)], stream=sx)
                wide_job(("out1", l, 1), mhi, mlo, [yb(0, 1), yb(1, 1)], before={2: lambda: sf["turn_to"](1)})
                wide_job(("up", l, 0), ahi, alo, [6, 7], stream=sf)
                def turn_step(b):
                    pe.wait_ge(ev_act, evs_act(l, "up", b))
                    for i, t in enumerate(("ta", "tb")):
                        turn_blocks((t, l, b), [nat[:, b % 2, tt, i * FB + f * P:i * FB + (f + 1) * P] for f in range(2) for tt in range(TT)])

                def down(b, between=None):
                    pe.wait_ge(ulo, NFB * l + b + 1)
                    tall_job(("down", l, b), mhi, mlo, 2 * (b % 4), lambda tt, c: yb(tt, c), b == 0, b == NFB - 1, between)

                turn_step(0)
                for b in range(NFB):
                    if b + 1 < NFB:
                        wide_job(("up", l, b + 1), ahi, alo, [6, 7])
                    if b == 0:
                        turn_step(1)
                    elif b < NFB - 1:
                        down(b - 1, (lambda: turn_step(NFB - 1)) if b == NFB - 2 else None)
                        if b < NFB - 2:
                            turn_step(b + 1)
                    else:
                        down(b - 1)
                if l == DEPTH - 1:
                    sm = memory_stream(0)
                down(NFB - 1)

            for l in range(DEPTH):
                even = l % 2 == 0
                sx = stream("x2", l, x, x_half(x_count("final") if l == 0 else x_count("ym", l - 1)))
                wide_job(("kv", l), ahi, alo, [6, 7], stream=sm, before={3: lambda: sx["turn_to"](1)})
                cols = EV_COLS if even else OD_COLS
                order = IN2_ORDER[l % 2]

                def blocks_of(c0):
                    return [proj[:, tt, c0 + b * P:c0 + (b + 1) * P] for b in range(2) for tt in range(TT)]

                def taken(*k):
                    pe.wait_ge(grp_act, plan.by_number[plan.groups[(k[0], l) + k[1:]]][1])

                def even_group(k):
                    key = (k[0], l) + k[1:]
                    if k[0] == "qi":
                        pe.wait_ge(ev_act, evs_act2(l, "in2", 2))
                        turn_blocks(key, blocks_of(640 + 2 * P * k[1]))
                    elif k[0] == "ki":
                        pe.wait_ge(kdup_ready, 1)
                        turn_blocks(key, [kdup[:, tt * P:tt * P + P] for tt in range(TT)])
                    elif k[0] == "ck":
                        pe.wait_ge(c_ready, 2)
                        turn_blocks(key, [proj[:, tt, 512:640] for tt in range(TT)])
                    elif k[0] == "qkb":
                        pe.wait_ge(ev_act, evs_act2(l, "in2", (2, 3, 3, 4)[k[1]]))
                        turn_blocks(key, blocks_of(1224 + 2 * P * k[1]))
                    elif k[0] == "qa":
                        pe.wait_ge(ev_act, evs_act2(l, "in2", 0))
                        turn_blocks(key, blocks_of(2 * P * k[1]))
                    elif k[0] == "uk":
                        pe.wait_ge(small_w_in, 32)
                        turn_blocks(key, [uk_nat[:, b, :] for b in range(4)])
                    elif k[0] == "idx":
                        qt, g = k[1:]
                        nk = causal(qt)
                        taken("ki")
                        bank = group_bank(key)
                        for i in range(2):
                            h = 4 * (g // 2) + g % 2 + 2 * i
                            b = half(h)
                            mm = nc.tensor.matmul(bank[:, i * SEQ:i * SEQ + nk], qiT[b:b + 64, h // 2, qt * P:qt * P + P],
                                                  kicT[b:b + 64, 0, 0:nk], start=True, stop=True)
                        mm.then_inc(pe_grp, 1)
                    elif k[0] == "ka":
                        taken("uk")
                        taken("ck")
                        bank = group_bank(key)
                        for b in range(2):
                            mm = nc.tensor.matmul(bank[:, b * SEQ:(b + 1) * SEQ], ukT[:, 2 * k[1] + b, :], kicT[:, 1, :], start=True, stop=True)
                        mm.then_inc(pe_grp, 1)
                    else:
                        bank = group_bank(key)
                        nc.tensor.matmul(bank, kicT[:, 1, k[1] * P:k[1] * P + P], uv, start=True, stop=True).then_inc(pe_grp, 1)

                def odd_group(k):
                    g = k[1]
                    if g < 4:
                        pe.wait_ge(ev_act, evs_act2(l, "in2", g // 2))
                        turn_blocks(("qk2", l, g), blocks_of(2 * P * g))
                    else:
                        pe.wait_ge(kdup_ready, 2)
                        turn_blocks(("qk2", l, g), [kdup2(tt, kv) for kv in range(2) for tt in range(TT)])

                def groups_at(s):
                    for k in (EVEN_GROUPS if even else ODD_GROUPS).get(s, ()):
                        (even_group if even else odd_group)(k)

                def in2_half(p, h):
                    j = order[p]
                    banks = in2_banks(l, p)
                    c, half_of = divmod(h, 2)
                    n = min(512, cols - 512 * j)
                    half_chunk(plan.jobs["in2", l, j][c], half_of, mhi, mlo, c * (KD // 2), [[(0, n, banks[tt])] for tt in range(TT)],
                               c == 0, c == 1, sx if p == 0 else None)

                last = len(order) - 1
                for s in range(4 * last + (0 if even else 1)):
                    p, h = divmod(s, 4)
                    if h == 0 and p >= 2:
                        pe.wait_ge(ev_act, evs_act2(l, "in2", order[p - 2]))
                    groups_at(s)
                    in2_half(p, h)
                if even:
                    groups_at(4 * last)
                    pe.wait_ge(ev_act, evs_act2(l, "in2", order[-3]))
                    taken("qkb", 2)

                    def even_waits(i):
                        if i < 4:
                            in2_half(last, i)
                        if i == 0:
                            groups_at(99)
                        if i == 1:
                            taken("qkb", 3)
                        if i == 5:
                            pe.wait_ge(ev_act, evs_act2(l, "in2", order[-1]))
                        if i + 1 == 4 * HB:
                            pe.wait_ge(sel_ready, TT)
                        if i == 4 * HB + lag_of(("even", l)):
                            pe.wait_ge(diff_taken, TT)

                    attention(("even", l), even_waits)
                else:
                    groups_at(4 * last + 1)
                    pe.wait_ge(grp_dve, plan.by_number[plan.groups["qk2", l, 4]][2])
                    taken("qk2", 1)

                    def odd_waits(i):
                        if i < 3:
                            in2_half(last, i + 1)
                        if i == 8:
                            wait_copied(pe, first_unit["odd", l] + i - lag_of(("odd", l)))
                            groups_at(99)
                            pe.wait_ge(grp_dve, plan.by_number[plan.groups["qk2", l, 2]][2])
                            taken("qk2", 3)

                    attention(("odd", l), odd_waits)
                so = stream("o2", l, o_nat, lambda h: pe.wait_ge(o_ready, o_counts[(("diff", "dsa"), ("odd a", "odd b"))[l % 2][h], l]),
                            O2_GROUPS[l % 2])
                wide_job(("out2", l, 0), ahi, alo, [y2b(0, 0), y2b(1, 0)], stream=so, ks=O2_CHUNKS[l % 2])
                turn_blocks(("qkx", l, 0), [kvn[:, tt, b * P:(b + 1) * P] for b in range(2) for tt in range(TT)])
                wide_job(("out2", l, 1), ahi, alo, [y2b(0, 1), y2b(1, 1)], ks=O2_CHUNKS[l % 2])
                wide_job(("wq", l), mhi, mlo, [6, 7], 256, stream=stream("xx", l, x, x_half(x_count("y2", l))))
                pe.wait_ge(ev_act, evs_act2(l, "wq"))
                turn_blocks(("qkx", l, 1), [proj[:, tt, b * P:(b + 1) * P] for b in range(2) for tt in range(TT)])
                pe.wait_ge(grp_dve, plan.by_number[plan.groups["qkx", l, 0]][2])
                pe.wait_ge(grp_act, plan.by_number[plan.groups["qkx", l, 1]][1])
                attention(("cross", l))
                pe.wait_ge(o_ready, o_counts["cross", l])
                turn_blocks(("ox", l), [o_nat[:, tt, b * P:(b + 1) * P] for b in range(2) for tt in range(TT)])
                pe.wait_ge(grp_dve, plan.by_number[plan.groups["ox", l]][2])
                tall_job(("wo", l), mhi, mlo, 0, lambda tt, c: yb(tt, c), True, True)
                wide_job(("w1", l, 0), ahi, alo, [6, 7], stream=stream("xm", l, x, x_half(x_count("yx", l))))

                def turn_step2(b):
                    pe.wait_ge(sq_ready, 2 * (NMB * l + b + 1))
                    for g in range(2):
                        turn_blocks(("tm", l, b, g), [nat[:, b % 2, tt, (2 * g + f) * P:(2 * g + f + 1) * P] for f in range(2) for tt in range(TT)])

                for b in range(NMB):
                    if b < NMB - 1:
                        turn_step2(b)
                    if b + 1 < NMB:
                        wide_job(("w1", l, b + 1), ahi, alo, [6, 7])
                    pe.wait_ge(grp_dve, plan.by_number[plan.groups["tm", l, b, 1]][2])
                    if b == NMB - 1 and l + 1 < DEPTH:
                        sm = memory_stream(l + 1)
                    tall_job(("w2", l, b), mhi, mlo, 4 * (b % 2), lambda tt, c: yb(tt, c), b == 0, b == NMB - 1,
                             (lambda: turn_step2(NMB - 1)) if b == NMB - 2 else None)

        @block.scalar
        def _(act):
            n_split = [0]
            n_link = [0]

            def link(ins):
                n_link[0] += 1
                ins.then_inc(act_chain, 1)
                act.wait_ge(act_chain, n_link[0])

            def split_half(m_last):
                while n_split[0] <= min(m_last, 2 * NCH - 1):
                    m = n_split[0]
                    n, h = divmod(m, 2)
                    kc, cols, _ = plan.chunks[n]
                    w = kc // 2 * cols
                    if h == 0:
                        act.wait_ge(landed[n % RAW], plan.landed[n])
                    if m >= HL:
                        act.wait_ge(pe_out, 2 * (m - HL + 1))
                    nc.scalar.copy(whi[:, m % HL, 0:w], raw[:, n % RAW, h * w:h * w + w]).then_inc(hi_done, 1)
                    n_split[0] += 1

            def split_to(n):
                split_half(2 * n + 1)

            def product(key, tt):
                act.wait_ge(pe_out, 4 * plan.jobs[key][-1] + 3 + tt)

            def scaled(key, norm, dst, n, banks, func=ACT.Copy, signal=ev_act):
                act.wait_ge(rstd_ready, rs_count[norm])
                for tt in range(TT):
                    product(key, tt)
                    nc.scalar.activation(dst(tt), ps[:, banks[tt], 0:n], func, scale=rstd[:, NORM[norm], tt:tt + 1]).then_inc(signal, 1)

            def stream_hi(tag, l, hi, row=None, gs=range(4)):
                for g in gs:
                    key = (tag, l, g)
                    group_ready(act, key)
                    bank = ps[:, 4 + plan.groups[key] % 2, :]
                    if row is None:
                        nc.scalar.copy(hi[:, 2 * g:2 * g + 2, :].rearrange("p b n -> p (b n)"), bank).then_inc(grp_act, 1)
                    else:
                        nc.scalar.activation(hi[:, 2 * g, :], bank[:, 0:SEQ], ACT.Copy, scale=gains[:, 2 * g, row:row + 1])
                        nc.scalar.activation(hi[:, 2 * g + 1, :], bank[:, SEQ:512], ACT.Copy,
                                             scale=gains[:, 2 * g + 1, row:row + 1]).then_inc(grp_act, 1)

            def take(key, dst, scale=1.0, cols=512, func=ACT.Copy):
                group_ready(act, key)
                bank = ps[:, 4 + plan.groups[key] % 2, 0:cols]
                nc.scalar.activation(dst, bank, func, scale=scale).then_inc(grp_act, 1)

            def blocks(t, b0, n=2):
                return t[:, b0:b0 + n, :].rearrange("p b n -> p (b n)")

            def attention(key, each=None):
                us, u0 = units_of[key], first_unit[key]
                n, lag, slots = len(us), lag_of(key), slots_of(key)
                for i in range(n + lag):
                    if each:
                        each(i)
                    if i < n:
                        u, d = u0 + i, us[i]
                        act.wait_ge(at_t, u + 1)
                        if u >= slots:
                            act.wait_ge(at_x, u - slots + 1)
                        s = d["slot"]
                        nc.scalar.activation(step_of(1536, u, d), step_of(0, u, d), ACT.Exp, scale=-1.0,
                                             bias=low[:, d["qt"], s:s + 1], accum_out=den[:, d["qt"], s:s + 1]).then_inc(at_e, 1)
                    if i >= lag and (u0 + i - lag) % 2 == 1:
                        u, d = u0 + i - lag, us[i - lag]
                        act.wait_ge(at_x, u + 1)
                        if u >= 2:
                            act.wait_ge(at_o, u - 1)
                        nc.scalar.copy(eT[:, u % 2, 0:d["w"]], turned(u, d)).then_inc(at_ya, 1)

            def memory_start(l, n0):
                split_half(n0 + 1)
                stream_hi("mem", l, ahi, row=gain_row["mem", l], gs=(0, 1))
                split_half(n0 + 3)

            def memory_rest(l, n0):
                stream_hi("mem", l, ahi, row=gain_row["mem", l], gs=(2,))
                split_half(n0 + 4)
                stream_hi("mem", l, ahi, row=gain_row["mem", l], gs=(3,))
                split_half(n0 + 6)

            act.wait_ge(ident_in, 16)
            nc.scalar.copy(ident_b[:], ident).then_inc(ident_ready, 1)
            take("gains", gains[:].rearrange("p k r -> p (k r)"), cols=KD * GAIN_ROWS)
            act.wait_ge(grp_act, plan.by_number[plan.groups["gains"]][1])

            def take_conv():
                take("conv", conv[:].rearrange("p k r -> p (k r)"), cols=8 * (FF1 // P))
                group_ready(act, "bias")
                nc.scalar.activation(band_rows, ps[0:NBIAS, 4 + plan.groups["bias"] % 2, :], ACT.Copy, scale=-1.0).then_inc(grp_act, 1)

            for l in range(DEPTH):
                m0 = 2 * plan.jobs["in1", l, 0][0]
                for g in range(4):
                    stream_hi("x1", l, ahi, row=gain_row["x1", l], gs=(g,))
                    split_half(m0 + (g if g < 2 else g + 2))

                def take_qk(g):
                    take(("qk1", l, g), blocks(qT, 2 * g), scale=-SCALE if g in (0, 1, 2, 6) else 1.0)

                f0 = 2 * plan.jobs["gate", l, 0][0]
                for j in range(QKV1 // 512):
                    split_half(2 * plan.jobs["in1", l, j][-1] + 4)
                    scaled(("in1", l, j), ("x1", l), lambda tt: proj[:, tt, 512 * j:512 * j + 512], 512, [yb(0, j), yb(1, j)])
                    if l == 0 and j == 0:
                        take_conv()
                    if l == 0 and j == 1:
                        act.wait_ge(trig_arg, 1)
                        nc.scalar.activation(small[:, 10:12, :], small[:, 8:10, :], ACT.Sin).then_inc(trig_done, 1)
                    split_half(2 * plan.jobs["in1", l, j][-1] + 5)
                    if j >= 3:
                        take_qk(2 * j - 5)
                take_qk(7)
                split_half(f0 + 5)
                for h in range(HG):
                    act.wait_ge(sb_abs, HG * l + h + 1)
                    link(nc.scalar.activation(sba(h), sba(h), ACT.Exp, scale=-1.0))
                for h in range(HG):
                    nc.scalar.activation(sba(h), sba(h), ACT.Ln, bias=1.0).then_inc(sb_ln, 1)
                split_half(f0 + 6)
                for h in range(HG):
                    act.wait_ge(sb_arg, HG * l + h + 1)
                    nc.scalar.activation(sba(h), sba(h), ACT.Exp).then_inc(sb_att, 1)
                split_half(f0 + 10)
                take(("y1", l, "b"), blocks(mhi, 2))
                split_half(f0 + 11)
                attention(("dil", l), each=lambda i: split_half(f0 + 10 + i))
                act.wait_ge(gate_pre, 2 * NGC * (l + 1))
                nc.scalar.activation(gates[:, :, D:2 * D], gates[:, :, D:2 * D], ACT.Sigmoid).then_inc(gate_done, 1)
                take(("y1", l, "a"), blocks(mhi, 0))
                split_half(f0 + 2 * NGC + 3)
                nc.scalar.activation(gates[:, :, 0:D], gates[:, :, 0:D], ACT.Sigmoid).then_inc(gate_done, 1)
                split_to(plan.jobs["pa", l][-1] + 2)
                stream_hi("mix", l, mhi)
                n0 = 2 * plan.jobs["out1", l, 1][0]
                split_half(n0 + 3)
                stream_hi("xf", l, ahi, row=gain_row["xf", l], gs=(0, 1))
                split_half(n0 + 7)
                stream_hi("xf", l, ahi, row=gain_row["xf", l], gs=(2, 3))

                def up_out(b):
                    scaled(("up", l, b), ("xf", l), lambda tt: nat[:, b % 2, tt, :], 512, [6, 7])

                up_out(0)
                split_to(plan.jobs["up", l, 0][-1] + 2)
                for b in range(NFB):
                    n0 = 2 * plan.jobs["up", l, min(b + 1, NFB - 1)][0]
                    if b + 1 < NFB:
                        split_half(n0 + 3)
                    act.wait_ge(grp_dve, plan.by_number[plan.groups["ta", l, b]][2])
                    nc.scalar.activation(sl, cv, ACT.Silu).then_inc(silu_ready, 1)
                    if b + 1 < NFB:
                        split_half(n0 + 4)
                    act.wait_ge(grp_dve, plan.by_number[plan.groups["tb", l, b]][2])
                    nc.scalar.copy(blocks(mhi, 2 * (b % 4)), ut).then_inc(uhi, 1)
                    if b + 1 < NFB:
                        split_half(n0 + 6)
                        up_out(b + 1)
                        if b:
                            split_half(n0 + 8)
                n0 = 2 * plan.jobs["down", l, NFB - 1][-1]
                if l == DEPTH - 1:
                    memory_start(0, n0)
                    act.wait_ge(x_ready, x_count("ffn", l))
                    nc.scalar.activation(junk2[:, D:], x[:, 1, :], ACT.Square, accum_out=ss[:, NORM["final",], 1:2]).then_inc(ss_ready, 1)
                    memory_rest(0, n0)
                split_half(n0 + 4)

            def squares(job, key, l, banks=yb, cs=(0, 1)):
                i = NORM[key, l]
                for c in cs:
                    for tt in range(TT):
                        product(job(c), tt)
                        nc.scalar.activation(junk_act[:, 2 * c + tt, :], ps[:, banks(tt, c), :], ACT.Square,
                                             accum_out=ss[:, i, 2 * c + tt:2 * c + tt + 1]).then_inc(ss_ready, 1)

            for l in range(DEPTH):
                even = l % 2 == 0
                nk = 2 * plan.jobs["kv", l][0]
                stream_hi("x2", l, mhi, row=gain_row["x2", l], gs=(0, 1))
                split_half(nk + 7)
                scaled(("kv", l), ("mem", l), lambda tt: kvn[:, tt, :], 512, [6, 7])
                stream_hi("x2", l, mhi, row=gain_row["x2", l], gs=(2,))
                split_half(nk + 8)
                stream_hi("x2", l, mhi, row=gain_row["x2", l], gs=(3,))
                cols = EV_COLS if even else OD_COLS
                order = IN2_ORDER[l % 2]

                def in2_out(j):
                    n = min(512, cols - 512 * j)
                    scaled(("in2", l, j), ("x2", l), lambda tt: proj[:, tt, 512 * j:512 * j + n], n, in2_banks(l, order.index(j)))

                def even_take(k):
                    key = (k[0], l) + k[1:]
                    if k[0] == "idx":
                        qt, g = k[1:]
                        nk = causal(qt)
                        group_ready(act, key)
                        t = qt * (HA // 2) + g
                        if t >= 2:
                            act.wait_ge(idx_used, t - 1)
                        src = ps[:, 4 + plan.groups[key] % 2, :].rearrange("p (h n) -> p h n", h=2)[:, :, 0:nk]
                        dst = relu_i[:, t % 2, :].rearrange("p (h n) -> p h n", h=2)[:, :, 0:nk]
                        nc.scalar.activation(dst, src, ACT.Relu).then_inc(grp_act, 1)
                    elif k[0] == "qi":
                        take(key, blocks(qiT, 2 * k[1]))
                    elif k[0] == "ki":
                        take(key, kicT[:, 0, :], cols=SEQ)
                    elif k[0] == "ck":
                        take(key, kicT[:, 1, :], cols=SEQ)
                    elif k[0] == "qkb":
                        take(key, blocks(qT, 2 * k[1]), scale=-SCALE if k[1] < 2 else 1.0)
                    elif k[0] == "qa":
                        take(key, blocks(qT, 8 + 2 * k[1]), scale=-SCALE)
                    elif k[0] == "uk":
                        take(key, blocks(ukT, 0, 4))
                    elif k[0] == "ka":
                        take(key, blocks(qT, 12 + 2 * k[1]))
                    else:
                        take(key, proj[:, k[1], 0:512])

                def odd_take(k):
                    if k[1] % 2:
                        take(("qk2", l, k[1]), blocks(qT, 2 * k[1]), scale=-SCALE)

                n0 = 2 * plan.jobs["in2", l, order[0]][0]
                last = 4 * (len(order) - 1)

                def takes_at(s):
                    for k in (EVEN_GROUPS if even else ODD_GROUPS).get(s, ()):
                        (even_take if even else odd_take)(k)

                for s in range(last + (1 if even else 2)):
                    if s % 4 == 0 and s:
                        in2_out(order[s // 4 - 1])
                    split_half(n0 + min(s + 3, last + 3))
                    takes_at(s)
                split_half(n0 + last + 3)

                def last_product(i):
                    if i == 1 and even:
                        takes_at(99)
                    if i == 5:
                        in2_out(order[-1])
                    if i in LATE_SPLITS:
                        split_half(n0 + last + 4 + LATE_SPLITS.index(i))
                    if i == 9 and not even:
                        takes_at(99)

                if even:
                    act.wait_ge(lam_arg, 2)
                    nc.scalar.activation(small[:, 7, 0:2], small[:, 6, 0:2], ACT.Exp).then_inc(lam_exp, 1)
                    attention(("even", l), each=last_product)
                else:
                    def sink_share(part):
                        heads = slice(8 * part, 8 * part + 8)
                        for qt in range(TT):
                            act.wait_ge(sink_arg, 2 * part + qt + 1)
                            nc.scalar.activation(small[:, 12 + qt, heads], small[:, 14 + qt, heads], ACT.Exp).then_inc(sink_exp, 1)

                    def odd_between(i):
                        last_product(i)
                        if i == 18:
                            sink_share(0)

                    attention(("odd", l), each=odd_between)
                    sink_share(1)
                g0, g1, g2, g3 = O2_GROUPS[l % 2]
                n0 = 2 * plan.jobs["out2", l, 0][0]
                stream_hi("o2", l, ahi, gs=(g0, g1))
                stream_hi("o2", l, ahi, gs=(g2,))
                split_half(n0 + 4)
                stream_hi("o2", l, ahi, gs=(g3,))
                split_half(n0 + 7)
                squares(lambda c: ("out2", l, c), "y2", l, y2b, (0,))
                split_half(n0 + 9)
                squares(lambda c: ("out2", l, c), "y2", l, y2b, (1,))
                split_half(n0 + 11)
                stream_hi("xx", l, mhi, row=gain_row["xx", l])
                scaled(("wq", l), ("xx", l), lambda tt: proj[:, tt, 0:256], 256, [6, 7])
                take(("qkx", l, 1), blocks(qT, 0), scale=-SCALE)
                attention(("cross", l), each=lambda i: split_half(n0 + 12 + CROSS_SPLITS.index(i)) if i in CROSS_SPLITS else None)
                take(("ox", l), blocks(mhi, 0))
                squares(lambda c: ("wo", l), "yx", l)
                stream_hi("xm", l, ahi, row=gain_row["xm", l], gs=(0, 1))
                split_half(n0 + 16)
                stream_hi("xm", l, ahi, row=gain_row["xm", l], gs=(2,))
                split_half(n0 + 17)
                stream_hi("xm", l, ahi, row=gain_row["xm", l], gs=(3,))
                split_half(n0 + 18)

                def mlp_out(b):
                    scaled(("w1", l, b), ("xm", l), lambda tt: nat[:, b % 2, tt, :], MB, [6, 7], ACT.Relu, relu_ready)

                mlp_out(0)
                split_to(plan.jobs["w1", l, 0][-1] + 2)
                for b in range(NMB):
                    for g in range(2):
                        take(("tm", l, b, g), blocks(mhi, 4 * (b % 2) + 2 * g))
                    n0 = plan.jobs["w2", l, b][0]
                    split_to(n0 + 1)
                    if b + 1 < NMB:
                        mlp_out(b + 1)
                    split_half(2 * n0 + (6 if b != NMB - 2 else 5))
                n0 = 2 * plan.jobs["w2", l, NMB - 1][-1]
                if l + 1 < DEPTH:
                    memory_start(l + 1, n0)
                squares(lambda c: ("w2", l, NMB - 1), "ym", l)
                if l + 1 < DEPTH:
                    memory_rest(l + 1, n0)

        @block.vector
        def _(dve):
            n_split = [0]
            n_link = [0]

            def mark(ins):
                n_link[0] += 1
                ins.then_inc(chain, 1)
                return n_link[0]

            def after(n):
                dve.wait_ge(chain, n)

            def link(ins):
                after(mark(ins))

            def split_half(m_last):
                while n_split[0] <= min(m_last, 2 * NCH - 1):
                    m = n_split[0]
                    n, h = divmod(m, 2)
                    kc, cols, _ = plan.chunks[n]
                    w = kc // 2 * cols
                    dve.wait_ge(hi_done, m + 1)
                    nc.vector.tensor_tensor(wlo[:, m % HL, 0:w], raw[:, n % RAW, h * w:h * w + w],
                                            whi[:, m % HL, 0:w].bitcast(F32), ALU.subtract).then_inc(lo_done, 1)
                    n_split[0] += 1

            def split_to(n):
                split_half(2 * n + 1)

            def product(key, tt):
                dve.wait_ge(pe_out, 4 * plan.jobs[key][-1] + 3 + tt)

            def group_bank(key):
                return ps[:, 4 + plan.groups[key] % 2, :]

            def hi_ready(key):
                dve.wait_ge(grp_act, plan.by_number[plan.groups[key]][1])

            def stream_lo(tag, l, hi, lo, row=None, gs=range(4)):
                for g in gs:
                    key = (tag, l, g)
                    hi_ready(key)
                    bank = group_bank(key)
                    if row is None:
                        nc.vector.tensor_tensor(blocks(lo, 2 * g), bank, blocks(hi, 2 * g).bitcast(F32), ALU.subtract).then_inc(grp_dve, 1)
                    else:
                        for b in range(2):
                            ins = nc.vector.scalar_tensor_tensor(out=lo[:, 2 * g + b, :], in0=bank[:, b * SEQ:(b + 1) * SEQ],
                                                                 scalar=gains[:, 2 * g + b, row:row + 1],
                                                                 in1=hi[:, 2 * g + b, :].bitcast(F32), op0=ALU.mult, op1=ALU.subtract)
                        ins.then_inc(grp_dve, 1)

            def blocks(t, b0, n=2):
                return t[:, b0:b0 + n, :].rearrange("p b n -> p (b n)")

            def lo_of(key, hi, lo, b0):
                hi_ready(key)
                nc.vector.tensor_tensor(blocks(lo, b0), group_bank(key), blocks(hi, b0).bitcast(F32), ALU.subtract).then_inc(grp_dve, 1)

            n_sq = [0]

            def squares(key, src, width, tiles=range(TT), junk=junk):
                i = NORM[key]
                for tt in tiles:
                    if n_sq[0]:
                        dve.wait_ge(ss_ready, n_sq[0])
                    nc.vector.tensor_tensor_reduce(out=junk[:, 0:width], in0=src(tt), in1=src(tt), scale=1.0, scalar=0.0, op0=ALU.mult,
                                                   op1=ALU.add, accum_out=ss[:, i, tt:tt + 1]).then_inc(ss_ready, 1)
                    n_sq[0] += 1

            def attention(key, before=None, each=None):
                us, u0 = units_of[key], first_unit[key]
                wide_units = us[-1]["w"] > SEQ
                n, lag, slots = len(us), lag_of(key), slots_of(key)
                for i in range(n + lag):
                    if before:
                        before(i)
                    if i < n:
                        u, d = u0 + i, us[i]
                        dve.wait_ge(at_s, u + 1)
                        if u >= slots:
                            dve.wait_ge(at_e, u - slots + 1)
                        b0 = 2 * (u % 2) if wide_units else u % 2
                        flat = ps[:, b0:b0 + (2 if wide_units else 1), :].rearrange("p b n -> p (b n)")[:, 0:d["w"]]
                        s = d["slot"]
                        bias = zero_bias if d["bias"] is None else d["bias"]
                        nc.vector.tensor_tensor_reduce(out=step_of(0, u, d), in0=flat, in1=bias, scale=1.0,
                                                       scalar=nsink[:, s:s + 1] if key[0] == "odd" else 3e38, op0=ALU.add, op1=ALU.min,
                                                       accum_out=low[:, d["qt"], s:s + 1]).then_inc(at_t, 1)
                    if i >= lag and (u0 + i - lag) % 2 == 0:
                        u, d = u0 + i - lag, us[i - lag]
                        dve.wait_ge(at_x, u + 1)
                        if u >= 2:
                            dve.wait_ge(at_o, u - 1)
                        nc.vector.tensor_copy(eT[:, u % 2, 0:d["w"]], turned(u, d)).then_inc(at_yd, 1)
                    if each:
                        each(i)

            def norm_out(key, first, n, dst, ended):
                us, u0 = units_of[key], first_unit[key]
                d = us[first]
                qt, s, bank, col = d["qt"], d["slot"], d["o_bank"], d["o_col"]
                r = rden[:, qt, s:s + n]
                dve.wait_ge(at_o, u0 + ended)
                if key[0] == "odd":
                    link(nc.vector.tensor_tensor(r, den[:, qt, s:s + n], small[:, 12 + qt, s:s + n], ALU.add))
                    link(nc.vector.reciprocal(r, r))
                else:
                    link(nc.vector.reciprocal(r, den[:, qt, s:s + n]))
                nc.vector.tensor_tensor(dst, ps[:, bank, col:col + n * HD].rearrange("p (h d) -> p h d", d=HD),
                                        r.unsqueeze(2).to_broadcast([P, n, HD]), ALU.mult).then_inc(o_ready, 1)

            def heads_of(t, tt, c0, n, d=HD):
                return t[:, tt, c0:c0 + n * d].rearrange("p (h d) -> p h d", d=d)

            def memory_start(l, n0):
                split_half(n0 + 1)
                stream_lo("mem", l, ahi, alo, row=gain_row["mem", l], gs=(0, 1))
                split_half(n0 + 3)

            def memory_squares(l):
                dve.wait_ge(mem_in, 16 * (l + 1))
                squares(("mem", l), lambda tt: o_nat[:, tt, :], D, junk=junk2)

            def memory_next(l, n0, g):
                stream_lo("mem", l, ahi, alo, row=gain_row["mem", l], gs=(g,))
                split_half(n0 + (4 if g == 2 else 6))

            nsink = misc[:, 512:528]
            zero_bias = relu_i[:, 0, 0:SEQ]

            def angles():
                dve.wait_ge(misc_in, 16)
                dve.wait_ge(cst_in, 16)
                pf = small[:, 1, 0:TT]
                link(nc.vector.tensor_copy(pf, pos_i[:]))
                ang, turns, wrap = small[:, 2, :], small[:, 3, :], small[:, 4, :]
                arg = small[:, 8:10, :]
                link(nc.vector.tensor_tensor(ang.rearrange("p (t f) -> p t f", t=TT), pf.unsqueeze(2).to_broadcast([P, TT, 8]),
                                             cst[:, C_INV:C_INV + 8].unsqueeze(1).to_broadcast([P, TT, 8]), ALU.mult))
                link(nc.vector.tensor_scalar(turns, ang, 1.0 / TWO_PI, ROUND, ALU.mult, ALU.add))
                link(nc.vector.tensor_scalar(turns, turns, ROUND, None, ALU.subtract))
                for part in (PI_HI, PI_MID, PI_LO):
                    link(nc.vector.scalar_tensor_tensor(out=ang, in0=turns, scalar=-part, in1=ang, op0=ALU.mult, op1=ALU.add))
                link(nc.vector.tensor_copy(arg[:, 0, :], ang))
                link(nc.vector.tensor_scalar(arg[:, 1, :], ang, float(np.pi / 2), None, ALU.add))
                pi = float(np.float32(np.pi))
                for i in range(2):
                    for cmp, lim, step in ((ALU.is_gt, pi, -TWO_PI), (ALU.is_lt, -pi, TWO_PI)):
                        link(nc.vector.tensor_scalar(wrap, arg[:, i, :], lim, step, cmp, ALU.mult))
                        link(nc.vector.tensor_tensor(arg[:, i, :], arg[:, i, :], wrap, ALU.add))
                link(nc.vector.tensor_scalar(arg, arg, pi, None, ALU.min))
                nc.vector.tensor_scalar(arg, arg, -pi, None, ALU.max).then_inc(trig_arg, 1)

            sin, cos = (small[:, 10 + i, :].rearrange("p (t f) -> p t f", t=TT).unsqueeze(2).to_broadcast([P, TT, 24, 8]) for i in range(2))

            for l in range(DEPTH):
                m0 = 2 * plan.jobs["in1", l, 0][0]
                for g in range(4):
                    stream_lo("x1", l, ahi, alo, row=gain_row["x1", l], gs=(g,))
                    split_half(m0 + (g if g < 2 else g + 2))
                for tt in range(TT):
                    squares(("x1", l), lambda tt: x[:, tt, :], D, (tt,), junk2)
                    split_half(m0 + 6 + tt)
                if l == 0:
                    angles()

                def take_qk(g):
                    key = ("qk1", l, g)
                    group_ready(dve, key)
                    if g in (0, 2, 6):
                        nc.vector.tensor_scalar(blocks(qT, 2 * g), group_bank(key), -SCALE, None, ALU.mult).then_inc(grp_dve, 1)
                    else:
                        nc.vector.tensor_copy(blocks(qT, 2 * g), group_bank(key)).then_inc(grp_dve, 1)

                def gate_out(c):
                    at = slice(GC * c, GC * (c + 1))
                    for tt in range(TT):
                        dve.wait_ge(pe_out, 4 * plan.jobs["gate", l, c][0] + 4)
                        nc.vector.scalar_tensor_tensor(out=gates[:, tt, at], in0=ps[:, 7, GC * tt:GC * (tt + 1)],
                                                       scalar=rstd[:, NORM["x1", l], tt:tt + 1], in1=gate_bias[:, at],
                                                       op0=ALU.mult, op1=ALU.add).then_inc(gate_pre, 1)

                f0 = 2 * plan.jobs["gate", l, 0][0]
                for j in range(QKV1 // 512):
                    split_half(2 * plan.jobs["in1", l, j][-1] + 5)
                    if j == 2:
                        dve.wait_ge(ev_act, evs_act(l, 2))
                        dve.wait_ge(trig_done, 1)
                        qk = proj[:, :, 0:1536].rearrange("p t (h d) -> p t h d", d=HD)
                        x1, x2 = qk[:, :, :, 0:8], qk[:, :, :, 8:16]
                        for i, (u, v) in enumerate(((x1, cos), (x2, sin), (x2, cos), (x1, sin))):
                            n = mark(nc.vector.tensor_tensor(rt[:, i], u, v, ALU.mult))
                        after(n)
                        nc.vector.tensor_tensor(x1, rt[:, 0], rt[:, 1], ALU.subtract)
                        nc.vector.tensor_tensor(x2, rt[:, 2], rt[:, 3], ALU.add).then_inc(rope_done, 1)
                    if j >= 3:
                        take_qk(2 * j - 6)
                take_qk(6)
                split_half(f0 + 4)
                dve.wait_ge(bgate_in, 16 * (l + 1))
                dve.wait_ge(rstd_ready, rs_count["x1", l])
                gate_out(0)
                for h in range(HG):
                    dve.wait_ge(sb_z, HG * l + h + 1)
                    n = mark(nc.vector.tensor_tensor(sbz(h), ps[:, h, 0:384], cst[:, C_SBM:C_SBM + 384], ALU.add))
                    after(n)
                    nc.vector.scalar_tensor_tensor(out=sba(h), in0=sbz(h), scalar=-1.0, in1=sbz(h), op0=ALU.mult, op1=ALU.max).then_inc(sb_abs, 1)
                split_half(f0 + 5)
                gate_out(1)
                for h in range(HG):
                    dve.wait_ge(sb_ln, HG * l + h + 1)
                    nc.vector.scalar_tensor_tensor(out=sbk(h), in0=sbz(h), scalar=0.0, in1=sba(h), op0=ALU.min,
                                                   op1=ALU.subtract).then_inc(sb_keep, 1)
                split_half(f0 + 6)
                for h in range(HG):
                    dve.wait_ge(sb_sum, HG * l + h + 1)
                    nc.vector.tensor_tensor(sba(h), ps[:, h, 0:384], sbz(h), ALU.subtract).then_inc(sb_arg, 1)
                split_half(f0 + 7)
                gate_out(2)
                dve.wait_ge(sb_o, HG * (l + 1))
                for tt in range(TT):
                    nc.vector.tensor_copy(o_nat[:, tt, 512:768], ps[:, 6, SEQ * tt:SEQ * (tt + 1)]).then_inc(o_ready, 1)
                split_half(f0 + 10)
                lo_of(("y1", l, "b"), mhi, mlo, 2)
                gate_out(3)
                split_half(f0 + 11)
                if l == 0:
                    dve.wait_ge(mask_in, 16)

                def between(i):
                    if i % 2 == 0 and i:
                        gate_out(3 + i // 2)
                    split_half(f0 + 10 + i)

                attention(("dil", l), between)
                for qt in range(TT):
                    norm_out(("dil", l), HG * qt, HG, heads_of(o_nat, qt, 0, HG), TT * HG)
                lo_of(("y1", l, "a"), mhi, mlo, 0)
                split_half(f0 + 2 * NGC + 3)
                dve.wait_ge(gate_done, 2 * l + 1)
                for tt in range(TT):
                    product(("pb", l), tt)
                    for c in range(2):
                        gt = gates[:, tt, D + 512 * c:D + 512 * c + 512]
                        nc.vector.tensor_tensor(gt, ps[:, yb(tt, c), :], gt, ALU.mult)
                split_half(2 * plan.jobs["pa", l][-1] + 3)
                dve.wait_ge(gate_done, 2 * l + 2)
                for c in range(2):
                    for tt in range(TT):
                        product(("pa", l), tt)
                        o = o_nat[:, tt, 512 * c:512 * c + 512]
                        n = mark(nc.vector.tensor_tensor(o, ps[:, 4 + 2 * c + tt, :], gates[:, tt, 512 * c:512 * c + 512], ALU.mult))
                    after(n)
                    for tt in range(TT):
                        o = o_nat[:, tt, 512 * c:512 * c + 512]
                        nc.vector.tensor_tensor(o, o, gates[:, tt, D + 512 * c:D + 512 * c + 512], ALU.add).then_inc(mixed, 1)
                stream_lo("mix", l, mhi, mlo, gs=(0,))
                split_to(plan.jobs["pa", l][-1] + 2)
                stream_lo("mix", l, mhi, mlo, gs=(1, 2, 3))

                def add_out(j):
                    for tt in range(TT):
                        product(("out1", l, j), tt)
                        xs = x[:, tt, 512 * j:512 * j + 512]
                        ins = nc.vector.tensor_tensor(xs, xs, ps[:, yb(tt, j), :], ALU.add)
                    ins.then_inc(x_ready, 1)

                n0 = 2 * plan.jobs["out1", l, 1][0]
                split_half(n0 + 1)
                add_out(0)
                split_half(n0 + 3)
                stream_lo("xf", l, ahi, alo, row=gain_row["xf", l], gs=(0, 1))
                split_half(n0 + 5)
                add_out(1)
                split_half(n0 + 7)
                dve.wait_ge(x_ready, x_count("mix", l))
                stream_lo("xf", l, ahi, alo, row=gain_row["xf", l], gs=(2,))
                squares(("xf", l), lambda tt: x[:, tt, :], D)
                stream_lo("xf", l, ahi, alo, row=gain_row["xf", l], gs=(3,))
                split_to(plan.jobs["up", l, 0][-1] + 2)
                for b in range(NFB):
                    if b == NFB - 2 and l == DEPTH - 1:
                        memory_squares(0)
                    n0 = 2 * plan.jobs["up", l, min(b + 1, NFB - 1)][0]
                    group_ready(dve, ("ta", l, b))
                    bank = group_bank(("ta", l, b))
                    if b:
                        dve.wait_ge(silu_ready, NFB * l + b)
                    for f in range(2):
                        w = [conv[:, 2 * b + f, i:i + 1] for i in (3 * l, 3 * l + 1, 3 * l + 2, 6 + l)]
                        n = mark(nc.vector.tensor_scalar(cv[:, f * SEQ:(f + 1) * SEQ], bank[:, f * SEQ:(f + 1) * SEQ], w[2], w[3], ALU.mult, ALU.add))
                    for lag in (1, 2):
                        after(n)
                        for f in range(2):
                            w = conv[:, 2 * b + f, 3 * l + 2 - lag:3 * l + 3 - lag]
                            o = cv[:, f * SEQ + lag:(f + 1) * SEQ]
                            ins = nc.vector.scalar_tensor_tensor(out=o, in0=bank[:, f * SEQ:(f + 1) * SEQ - lag], scalar=w, in1=o,
                                                                 op0=ALU.mult, op1=ALU.add)
                            if lag == 2 and f == 1:
                                ins.then_inc(grp_dve, 1)
                            else:
                                n = mark(ins)
                    if b + 1 < NFB:
                        split_half(n0 + 4)
                    group_ready(dve, ("tb", l, b))
                    dve.wait_ge(silu_ready, NFB * l + b + 1)
                    if b:
                        dve.wait_ge(ulo, NFB * l + b)
                    nc.vector.tensor_tensor(ut, sl, group_bank(("tb", l, b)), ALU.mult).then_inc(grp_dve, 1)
                    dve.wait_ge(grp_dve, plan.by_number[plan.groups["tb", l, b]][2])
                    dve.wait_ge(uhi, NFB * l + b + 1)
                    nc.vector.tensor_tensor(blocks(mlo, 2 * (b % 4)), ut, blocks(mhi, 2 * (b % 4)).bitcast(F32), ALU.subtract).then_inc(ulo, 1)
                    if b + 1 < NFB:
                        split_half(n0 + (8 if b else 6))
                n0 = 2 * plan.jobs["down", l, NFB - 1][-1]
                if l == DEPTH - 1:
                    memory_start(0, n0)
                split_half(n0 + 3)
                for c in range(2):
                    for tt in range(TT):
                        product(("down", l, NFB - 1), tt)
                        xs = x[:, tt, 512 * c:512 * c + 512]
                        ins = nc.vector.tensor_tensor(xs, xs, ps[:, yb(tt, c), :], ALU.add)
                    ins.then_inc(x_ready, 1)
                dve.wait_ge(x_ready, x_count("ffn", l))

            squares(("final",), lambda tt: x[:, tt, :], D, (0,), junk2)
            n_sq[0] += 1
            memory_next(0, n0, 2)
            dve.wait_ge(gainb_in, 16)
            dve.wait_ge(rstd_ready, rs_count["final",])
            for c in range(2):
                cs = slice(512 * c, 512 * c + 512)
                for tt in range(TT):
                    ins = nc.vector.scalar_tensor_tensor(out=x[:, tt, cs], in0=x[:, tt, cs], scalar=rstd[:, NORM["final",], tt:tt + 1],
                                                         in1=gain_b[:, cs], op0=ALU.mult, op1=ALU.mult)
                ins.then_inc(x_ready, 1)

            memory_next(0, n0, 3)

            n_gain = [1]

            def add_normed(key, l, jobs, mid=None, banks=yb, before_second=None):
                n_gain[0] += 1
                n_sq[0] += 4
                dve.wait_ge(gainb_in, 16 * n_gain[0])
                for c in range(2):
                    if c == 1 and before_second:
                        before_second()
                    for tt in range(TT):
                        product(jobs[c], tt)
                        dve.wait_ge(ss_ready, n_sq[0] - 3 + 2 * c + tt)
                        cs = slice(512 * c, 512 * c + 512)
                        n = mark(nc.vector.tensor_tensor(ystep[:, tt, cs], ps[:, banks(tt, c), :], gain_b[:, cs], ALU.mult))
                if mid:
                    mid()
                dve.wait_ge(rstd_ready, rs_count[key, l])
                after(n)
                for c in range(2):
                    for tt in range(TT):
                        cs = slice(512 * c, 512 * c + 512)
                        ins = nc.vector.scalar_tensor_tensor(out=x[:, tt, cs], in0=ystep[:, tt, cs], scalar=rstd[:, NORM[key, l], tt:tt + 1],
                                                             in1=x[:, tt, cs], op0=ALU.mult, op1=ALU.add)
                    ins.then_inc(x_ready, 1)
                dve.wait_ge(x_ready, x_count(key, l))

            for l in range(DEPTH):
                even = l % 2 == 0
                nk = 2 * plan.jobs["kv", l][0]
                if l == 0:
                    dve.wait_ge(x_ready, x_count("final"))
                stream_lo("x2", l, mhi, mlo, row=gain_row["x2", l], gs=(0, 1))
                split_half(nk + 7)
                stream_lo("x2", l, mhi, mlo, row=gain_row["x2", l], gs=(2,))
                split_half(nk + 8)
                squares(("x2", l), lambda tt: x[:, tt, :], D, (0,))
                stream_lo("x2", l, mhi, mlo, row=gain_row["x2", l], gs=(3,))
                split_half(nk + 9)
                squares(("x2", l), lambda tt: x[:, tt, :], D, (1,))
                order = IN2_ORDER[l % 2]
                n0 = 2 * plan.jobs["in2", l, order[0]][0]
                dve.wait_ge(band_in, 16 * (l + 1))
                nc.vector.memset(band[0:64, 0:(HA + HB) if even else HC, 192:256], BIG)
                if not even:
                    nc.vector.memset(band[64:128, 0:HC, 0:64], BIG)

                def latent_sums():
                    dve.wait_ge(ev_act, evs_act2(l, "in2", 2))
                    kd = kdup[:, 0:256].rearrange("p (t i d) -> p t i d", t=TT, i=2)
                    nc.vector.tensor_copy(kd, proj[:, :, 1152:1216].unsqueeze(2).to_broadcast([P, TT, 2, HD])).then_inc(kdup_ready, 1)
                    squares(("ckv", l), lambda tt: proj[:, tt, 512:640], P)

                def latent_out():
                    dve.wait_ge(misc_in, 16 * 5)
                    dve.wait_ge(rstd_ready, rs_count["ckv", l])
                    for tt in range(TT):
                        c = proj[:, tt, 512:640]
                        nc.vector.scalar_tensor_tensor(out=c, in0=c, scalar=rstd[:, NORM["ckv", l], tt:tt + 1], in1=akv,
                                                       op0=ALU.mult, op1=ALU.mult).then_inc(c_ready, 1)

                def lambda_sums():
                    for i in range(2):
                        if i:
                            dve.wait_ge(lam_arg, i)
                        nc.vector.tensor_tensor_reduce(out=junk[:, 512:576], in0=lam_rows[:, 128 * i:128 * i + 64], in1=lam_rows[:, 128 * i + 64:128 * i + 128],
                                                       scale=1.0, scalar=0.0, op0=ALU.mult, op1=ALU.add,
                                                       accum_out=small[:, 6, i:i + 1]).then_inc(lam_arg, 1)
                    link(nc.vector.tensor_scalar(nsink, nsink, -1.0, None, ALU.mult))

                def index_sum(qt, g):
                    nk = causal(qt)
                    adm = cst[:, C_ADM + SEQ - nk:C_ADM + SEQ]
                    t = qt * (HA // 2) + g
                    dve.wait_ge(grp_act, plan.by_number[plan.groups["idx", l, qt, g]][1])
                    for i in range(2):
                        h = 4 * (g // 2) + g % 2 + 2 * i
                        ins = nc.vector.scalar_tensor_tensor(out=cand[qt][:, 0:nk], in0=relu_i[:, t % 2, i * SEQ:i * SEQ + nk],
                                                             scalar=proj[:, qt, 1216 + h:1217 + h], in1=adm if h == 0 else cand[qt][:, 0:nk],
                                                             op0=ALU.mult, op1=ALU.add)
                        if i == 0:
                            link(ins)
                        else:
                            ins.then_inc(idx_used, 1)
                            dve.wait_ge(idx_used, t + 1)

                def top_rounds(qt, r0, r1):
                    nk = causal(qt)
                    top = small[:, 13, 0:8]
                    c = cand[qt][:, 0:nk]
                    for r in range(r0, r1):
                        link(nc.vector.max(top, c))
                        link(nc.vector.match_replace(c, top, c, SENTINEL))
                    if r1 == TOPK // 8:
                        nc.vector.tensor_scalar(sel[:, (0, P)[qt]:(0, P)[qt] + nk], c, SENTINEL / 2, BIG, ALU.is_gt, ALU.mult).then_inc(sel_ready, 1)

                def odd_keys():
                    dve.wait_ge(ev_act, evs_act2(l, "in2", 2))
                    kd = kdup.rearrange("p (t k i d) -> p t k i d", t=TT, k=2, i=2)
                    for tt in range(TT):
                        ins = nc.vector.tensor_copy(kd[:, tt], proj[:, tt, 1024:1152].rearrange("p (k d) -> p k d", d=HD).unsqueeze(2)
                                                    .to_broadcast([P, 2, 2, HD]))
                    ins.then_inc(kdup_ready, 1)

                def qk2_take(g):
                    key = ("qk2", l, g)
                    group_ready(dve, key)
                    if g < 4:
                        nc.vector.tensor_scalar(blocks(qT, 2 * g), group_bank(key), -SCALE, None, ALU.mult).then_inc(grp_dve, 1)
                    else:
                        nc.vector.tensor_copy(blocks(qT, 2 * g), group_bank(key)).then_inc(grp_dve, 1)

                def even_step(s):
                    if s == 8:
                        latent_sums()
                    if s == 9:
                        latent_out()
                    if s == 10:
                        lambda_sums()
                    if s in (11, 12):
                        index_sum(0, 2 * (s - 11))
                        index_sum(0, 2 * (s - 11) + 1)
                    if 13 <= s <= 15:
                        top_rounds(0, (0, 3, 6)[s - 13], (3, 6, 8)[s - 13])
                    if 15 <= s <= 18:
                        index_sum(1, s - 15)
                    if s == 19:
                        top_rounds(1, 0, 2)

                def odd_step(s):
                    if s == 5:
                        qk2_take(0)
                    if s == 8:
                        odd_keys()
                    if s == 9:
                        qk2_take(4)

                last = 4 * (len(order) - 1)
                for s in range(last + (1 if even else 2)):
                    split_half(n0 + min(s + 3, last + 3))
                    (even_step if even else odd_step)(s)
                split_half(n0 + last + 3)
                if even:
                    nlam = small[:, 7, 2:3]

                    def diff_step(qt, k):
                        o = heads_of(o_nat, qt, 512, HB, P)
                        t = heads_of(o_nat, qt, 0, HB, P)
                        if k < 2:
                            hs = slice(2 * k, 2 * k + 2)
                            r = rden[:, qt, 4 * k:4 * k + 4]
                            link(nc.vector.reciprocal(r, den[:, qt, 4 * k:4 * k + 4]))
                            r = r.rearrange("p (h m) -> p h m", m=2)
                            link(nc.vector.tensor_scalar(r[:, :, 1], r[:, :, 1], nlam, None, ALU.mult))
                            y = ps[:, (6, 2)[qt] + k, :].rearrange("p (h m d) -> p h m d", m=2, d=P)
                            nc.vector.tensor_tensor(o[:, hs], y[:, :, 0, :], r[:, :, 0].unsqueeze(2).to_broadcast([P, 2, P]), ALU.mult)
                            nc.vector.tensor_tensor(t[:, hs], y[:, :, 1, :], r[:, :, 1].unsqueeze(2).to_broadcast([P, 2, P]), ALU.mult).then_inc(diff_taken, 1)
                        elif k == 3:
                            dve.wait_ge(diff_taken, 2 * TT)
                            link(nc.vector.tensor_tensor(o, o, t, ALU.add))
                        elif k == 4:
                            link(nc.vector.tensor_tensor(t, o, o, ALU.mult))
                        elif k == 5:
                            nc.vector.tensor_reduce(small[:, 2 + qt, 0:HB], t, AX.X, ALU.add).then_inc(ss_ready, 1)
                            n_sq[0] += 1
                        elif k == 6:
                            dve.wait_ge(rstd_ready, rs_count["ckv", l] + qt + 1)
                            link(nc.vector.tensor_tensor(o, o, small[:, 4 + qt, 0:HB].unsqueeze(2).to_broadcast([P, HB, P]), ALU.mult))
                        else:
                            nc.vector.scalar_tensor_tensor(out=o, in0=o, scalar=1.0 - LAM_INIT, in1=subln.unsqueeze(1).to_broadcast([P, HB, P]),
                                                           op0=ALU.mult, op1=ALU.mult).then_inc(o_ready, 1)

                    def even_between(i):
                        if i == 0:
                            dve.wait_ge(lam_exp, 1)
                            link(nc.vector.tensor_tensor(nlam, small[:, 7, 1:2], small[:, 7, 0:1], ALU.subtract))
                            link(nc.vector.tensor_scalar(nlam, nlam, -LAM_INIT, None, ALU.add))
                        if 1 <= i <= 6:
                            top_rounds(1, 1 + i, 2 + i)
                        if i in LATE_SPLITS:
                            split_half(n0 + last + 4 + LATE_SPLITS.index(i))
                        for part in range(2):
                            if i in (8 * part + 12, 8 * part + 13):
                                dve.wait_ge(at_o, first_unit["even", l] + 8 * (part + 1))
                                diff_step(i - 8 * part - 12, part)
                        if 22 <= i <= 31:
                            diff_step((i - 22) % TT, 3 + (i - 22) // TT)

                    attention(("even", l), each=even_between)
                else:
                    def odd_norm(qt, part):
                        norm_out(("odd", l), 16 * part + qt, 8, heads_of(o_nat, qt, 512 * part, 8), 16 * (part + 1))

                    def sink_args(part):
                        heads = slice(8 * part, 8 * part + 8)
                        dve.wait_ge(at_t, first_unit["odd", l] + 16 * (part + 1))
                        for qt in range(TT):
                            nc.vector.tensor_tensor(small[:, 14 + qt, heads], low[:, qt, heads], nsink[:, heads], ALU.subtract).then_inc(sink_arg, 1)

                    def odd_between(i):
                        if i in LATE_SPLITS:
                            split_half(n0 + last + 4 + LATE_SPLITS.index(i))
                        if i == 8:
                            qk2_take(2)
                        if i == 16:
                            sink_args(0)
                        if i == 20:
                            dve.wait_ge(sink_exp, TT)
                        if i in (20, 21):
                            odd_norm(i - 20, 0)
                        if i == 32:
                            sink_args(1)

                    attention(("odd", l), each=odd_between)
                g0, g1, g2, g3 = O2_GROUPS[l % 2]
                stream_lo("o2", l, ahi, alo, gs=(g0,))
                if not even:
                    dve.wait_ge(sink_exp, 2 * TT)
                for qt in range(TT):
                    if even:
                        norm_out(("even", l), 4 * HB + qt, HA, heads_of(o_nat, qt, 0, HA), 4 * HB + 2 * HA)
                    else:
                        odd_norm(qt, 1)
                stream_lo("o2", l, ahi, alo, gs=(g1, g2))
                n0 = 2 * plan.jobs["out2", l, 0][0]
                split_half(n0 + 4)
                stream_lo("o2", l, ahi, alo, gs=(g3,))
                split_half(n0 + 7)

                def before_second():
                    key = ("qkx", l, 0)
                    group_ready(dve, key)
                    nc.vector.tensor_copy(blocks(qT, 2), group_bank(key)).then_inc(grp_dve, 1)
                    nc.vector.memset(zero_bias, 0.0)
                    split_half(n0 + 9)

                add_normed("y2", l, [("out2", l, 0), ("out2", l, 1)], lambda: split_half(n0 + 10), y2b, before_second)
                split_half(n0 + 11)
                stream_lo("xx", l, mhi, mlo, row=gain_row["xx", l], gs=(0, 1))
                squares(("xx", l), lambda tt: x[:, tt, :], D)
                stream_lo("xx", l, mhi, mlo, row=gain_row["xx", l], gs=(2, 3))

                def cross_between(i):
                    if i in CROSS_SPLITS:
                        split_half(n0 + 12 + CROSS_SPLITS.index(i))
                    if i == HX + lag_of(("cross", l)) + 1:
                        norm_out(("cross", l), 0, HX, heads_of(o_nat, 0, 0, HX), HX)

                attention(("cross", l), cross_between)
                norm_out(("cross", l), HX, HX, heads_of(o_nat, 1, 0, HX), TT * HX)
                lo_of(("ox", l), mhi, mlo, 0)
                add_normed("yx", l, [("wo", l)] * 2)
                stream_lo("xm", l, ahi, alo, row=gain_row["xm", l], gs=(0, 1))
                split_half(n0 + 16)
                stream_lo("xm", l, ahi, alo, row=gain_row["xm", l], gs=(2,))
                split_half(n0 + 17)
                stream_lo("xm", l, ahi, alo, row=gain_row["xm", l], gs=(3,))
                split_half(n0 + 18)
                squares(("xm", l), lambda tt: x[:, tt, :], D)

                def square(b):
                    for tt in range(TT):
                        dve.wait_ge(relu_ready, 2 * (NMB * l + b) + tt + 1)
                        nc.vector.tensor_tensor(nat[:, b % 2, tt, :], nat[:, b % 2, tt, :], nat[:, b % 2, tt, :], ALU.mult).then_inc(sq_ready, 1)

                square(0)
                split_to(plan.jobs["w1", l, 0][-1] + 2)
                for b in range(NMB):
                    if b == NMB - 2 and l + 1 < DEPTH:
                        memory_squares(l + 1)
                    for g in range(2):
                        lo_of(("tm", l, b, g), mhi, mlo, 4 * (b % 2) + 2 * g)
                    n0 = plan.jobs["w2", l, b][0]
                    split_to(n0 + 1)
                    if b + 1 < NMB:
                        square(b + 1)
                    split_half(2 * n0 + (6 if b != NMB - 2 else 5))
                n0 = 2 * plan.jobs["w2", l, NMB - 1][-1]
                if l + 1 < DEPTH:
                    memory_start(l + 1, n0)
                split_half(n0 + 1)
                add_normed("ym", l, [("w2", l, NMB - 1)] * 2, (lambda: memory_next(l + 1, n0, 2)) if l + 1 < DEPTH else None)
                if l + 1 < DEPTH:
                    memory_next(l + 1, n0, 3)


INPUTS = [
    "x", "positions", "norm_mix", "w_in", "b_gate", "w_proj_a", "w_proj_b", "w_out", "norm_ffn", "w_up", "conv_w", "conv_b", "w_down",
    "norm_final", "mem_2", "rel_bias_table_2", "norm_g_2", "ev_w_in_2", "ev_a_kv_norm_2", "ev_a_w_uk_2", "ev_a_w_uv_2", "ev_b_lambda_2",
    "ev_b_subln_2", "ev_w_out_2", "od_w_in_2", "od_sinks_2", "od_w_out_2", "xa_wq_2", "xa_wkv_2", "xa_wo_2", "xa_mem_norm_2", "mlp_w1_2",
    "mlp_w2_2",
]


def kernel(**inputs):
    import numpy as np
    import concourse.bacc as bacc
    from concourse import mybir
    from concourse.bass_utils import run_bass_kernel_spmd

    nc = bacc.Bacc("TRN2", target_bir_lowering=False, num_devices=1)
    cst, masks = shape_constants()
    arrays = {"in_" + n: np.ascontiguousarray(inputs[n]) for n in INPUTS}
    arrays["in_cst"], arrays["in_masks"] = cst, masks
    aps = {n[3:]: nc.dram_tensor(n, v.shape, mybir.dt.from_np(v.dtype), kind="ExternalInput").ap() for n, v in arrays.items()}
    out = nc.dram_tensor("out", (1, SEQ, D), mybir.dt.float32, kind="ExternalOutput").ap()
    build_network(nc, aps, out)
    r = run_bass_kernel_spmd(nc, [arrays], core_ids=[0])
    return r.results[0]["out"]
```

```python
from contextlib import ExitStack

import concourse.bass as bass
import numpy as np
from concourse import mybir

F32 = mybir.dt.float32
F32R = mybir.dt.float32r
BF16 = mybir.dt.bfloat16
I32 = mybir.dt.int32
ALU = mybir.AluOpType
ACT = mybir.ActivationFunctionType
AX = mybir.AxisListType

P = 128
TT = 2
SEQ = TT * P
D = 1024
KD = D // P
DEPTH = 2
HD = 64
DIL = (1, 4, 16)
DIL_WINDOW = (128, 512, 2048)
NG, HG = 3, 4
QKV1 = 3072
GC = 256
NGC = 2 * D // GC
FF1 = 2816
FB = 256
NFB = FF1 // FB
FF2 = 4096
MB = 512
NMB = FF2 // MB
EV_COLS = 2760
OD_COLS = 1280
HA, HB, HC, HX = 8, 4, 16, 4
TOPK = 64
IN2_ORDER = ((1, 2, 0, 3, 4, 5), (0, 2, 1))
EVEN_GROUPS = {9: [("qi", 0), ("qi", 1)], 10: [("ki",), ("uk",)], 11: [("idx", 0, 0), ("idx", 0, 1)], 12: [("idx", 0, 2), ("idx", 0, 3)],
               13: [("ck",), ("qkb", 0)], 14: [("idx", 1, 0), ("qa", 0)], 15: [("idx", 1, 1), ("qa", 1)], 16: [("idx", 1, 2)],
               17: [("idx", 1, 3), ("qkb", 1)], 18: [("qkb", 2), ("ka", 0)], 19: [("ka", 1), ("va", 0)], 20: [("va", 1)], 99: [("qkb", 3)]}
ODD_GROUPS = {5: [("qk2", 0)], 6: [("qk2", 1)], 9: [("qk2", 4)], 99: [("qk2", 2), ("qk2", 3)]}
O2_GROUPS = (2, 3, 0, 1), (0, 1, 2, 3)
O2_CHUNKS = (KD // 2, 0), (0, KD // 2)
NBUCKET = 32
NBIAS = HA + HB + HC
ODD_NORMS = (23, 26)
DIFF_OUT = 13
DIFF_SUMS = (27, 28)
PB_AT = 1
BIG = 1e30
SENTINEL = -3e38
SCALE = HD ** -0.5
EPS1, EPS2 = 1e-5, 1e-6
LAM_INIT = 0.8 - 0.6
TWO_PI = 2.0 * np.pi
PI_HI, PI_MID = 6.28125, float(np.float32(TWO_PI - 6.28125))
PI_LO = float(np.float32(TWO_PI - 6.28125 - np.float64(np.float32(TWO_PI - 6.28125))))
ROUND = 12582912.0

CH = 2048
RAW = 3
HALF = CH // 2
HL = 4

C_ID, C_ONE, C_TRI, C_SBM, C_ADM, C_HOT, C_INV = 0, 128, 256, 384, 768, 1024, 1536
C_COLS = 1544
M_COLS = 3 * P + 3 * SEQ
BAND_PARTS = 7
BAND_W = 512
PITCH = 512


def shape_constants():
    c = np.zeros((P, C_COLS), np.float32)
    i = np.arange(P)
    c[:, C_ID:C_ID + P] = np.eye(P)
    c[:, C_ONE:C_ONE + P] = 1.0
    c[:, C_TRI:C_TRI + P] = i[:, None] >= i[None, :]
    q = np.arange(SEQ)
    c[:, C_SBM:C_SBM + SEQ] = BIG * (i[:, None] >= q[None, :])
    c[:, C_SBM + SEQ:C_SBM + SEQ + P] = BIG * (i[:, None] >= i[None, :])
    c[:64, C_ADM + 192:C_ADM + 256] = -BIG
    r = np.arange(383)
    rel = r - 255
    n = np.abs(rel)
    nf = np.maximum(n, 1).astype(np.float32)
    large = 8 + (np.log(nf / np.float32(8)) / np.float32(np.log(128.0)) * np.float32(8)).astype(np.int32)
    bucket = np.where(rel > 0, 16, 0) + np.where(n < 8, n, np.minimum(large, 15))
    c[bucket, C_HOT + r] = 1.0
    inv = np.float32(500000.0) ** (-np.arange(0, 16, 2, dtype=np.float32) / np.float32(16))
    c[:, C_INV:C_INV + 8] = inv
    m = np.zeros((P, M_COLS), np.float32)
    for qt in range(TT):
        nk = P * (qt + 1)
        for g in range(NG):
            gap = (qt * P + i)[:, None] - np.arange(nk)[None, :]
            ok = (gap >= 0) & (gap <= DIL_WINDOW[g]) & (gap % DIL[g] == 0)
            at = (0, 3 * P)[qt] + g * nk
            m[:, at:at + nk] = BIG * ~ok
    return c, m


class Plan:

    def __init__(self):
        self.chunks = []
        self.jobs = {}
        self.landed = []
        self.slot_total = [0] * RAW
        self.groups = {}
        self.by_number = []
        self.n_act = self.n_dve = 0

    def job(self, key, pieces):
        ids = []
        for kc, n, srcs in pieces:
            s = len(self.chunks) % RAW
            self.slot_total[s] += 16 * len(srcs)
            ids.append(len(self.chunks))
            self.chunks.append((kc, n, srcs))
            self.landed.append(self.slot_total[s])
        self.jobs[key] = ids

    def group(self, key, mode):
        self.n_act += mode in ("act", "split")
        self.n_dve += mode in ("dve", "split")
        self.groups[key] = len(self.by_number)
        self.by_number.append((mode, self.n_act, self.n_dve))


def build_network(nc, a, out):
    plan = Plan()

    def rows(w, k0, kc, c0, n):
        return w[k0 * P:(k0 + kc) * P, c0:c0 + n].rearrange("(k p) n -> p k n", p=P)

    def wide(w, c0, n, ks=(0, KD // 2)):
        return [(KD // 2, n, [(0, n, rows(w, k, KD // 2, c0, n))]) for k in ks]

    def tall(w, r0, k):
        return [(2, D, [(0, D, rows(w, r0 // P + j, 2, 0, D))]) for j in range(0, k, 2)]

    plan.group("gains", "act")
    for l in range(DEPTH):
        w = a["w_in"][l]
        for g in range(4):
            plan.group(("x1", l, g), "split")
        if l == 0:
            plan.group("conv", "act")
            plan.group("bias", "act")
        for j in range(QKV1 // 512):
            plan.job(("in1", l, j), wide(w, 512 * j, 512))
        for i in range(NGC):
            plan.job(("gate", l, i), [(KD, GC, [(0, GC, rows(w, 0, KD, QKV1 + GC * i, GC))])])
        for g in range(8):
            plan.group(("qk1", l, g), "act" if g % 2 else "dve")
        for g in ("b", "a"):
            plan.group(("y1", l, g), "split")
        plan.job(("pb", l), tall(a["w_proj_b"][l], 0, 2))
        plan.job(("pa", l), tall(a["w_proj_a"][l], 0, 2))
        for g in range(4):
            plan.group(("mix", l, g), "split")
        for j in range(2):
            plan.job(("out1", l, j), wide(a["w_out"][l], 512 * j, 512))
        for g in range(4):
            plan.group(("xf", l, g), "split")

        def up(b):
            w = a["w_up"][l]
            plan.job(("up", l, b), [(4, 2 * FB, [(0, FB, rows(w, k, 4, b * FB, FB)),
                                                (FB, FB, rows(w, k, 4, FF1 + b * FB, FB))]) for k in (0, 4)])

        def down(b):
            plan.job(("down", l, b), tall(a["w_down"][l], b * FB, 2))

        up(0)
        up(1)
        for b in range(NFB):
            plan.group(("ta", l, b), "dve")
            plan.group(("tb", l, b), "dve")
            if b + 2 < NFB:
                up(b + 2)
                if b + 3 < NFB:
                    down(b)
        for b in range(NFB - 3, NFB):
            down(b)
    for l in range(DEPTH):
        even = l % 2 == 0
        for g in range(4):
            plan.group(("mem", l, g), "split")
        plan.job(("kv", l), wide(a["xa_wkv_2"][l], 0, 512))
        for g in range(4):
            plan.group(("x2", l, g), "split")
        w, cols = (a["ev_w_in_2"][0], EV_COLS) if even else (a["od_w_in_2"][0], OD_COLS)
        for j in IN2_ORDER[l % 2]:
            plan.job(("in2", l, j), wide(w, 512 * j, min(512, cols - 512 * j)))
        for keys in (EVEN_GROUPS if even else ODD_GROUPS).values():
            for k in keys:
                plan.group((k[0], l) + k[1:], "dve" if k[0] == "qk2" and k[1] % 2 == 0 else "act")
        for g in O2_GROUPS[l % 2]:
            plan.group(("o2", l, g), "split")
        w = a["ev_w_out_2"][0] if even else a["od_w_out_2"][0]
        for j in range(2):
            plan.job(("out2", l, j), wide(w, 512 * j, 512, O2_CHUNKS[l % 2]))
        plan.group(("qkx", l, 0), "dve")
        for g in range(4):
            plan.group(("xx", l, g), "split")
        plan.job(("wq", l), wide(a["xa_wq_2"][l], 0, 256))
        plan.group(("qkx", l, 1), "act")
        plan.group(("ox", l), "split")
        plan.job(("wo", l), tall(a["xa_wo_2"][l], 0, 2))
        for g in range(4):
            plan.group(("xm", l, g), "split")
        for b in range(2):
            plan.job(("w1", l, b), wide(a["mlp_w1_2"][l], MB * b, MB))
        for b in range(NMB):
            for g in range(2):
                plan.group(("tm", l, b, g), "split")
            if b + 2 < NMB:
                plan.job(("w1", l, b + 2), wide(a["mlp_w1_2"][l], MB * (b + 2), MB))
            plan.job(("w2", l, b), tall(a["mlp_w2_2"][l], MB * b, MB // P))
    NCH = len(plan.chunks)

    norms = []
    for l in range(DEPTH):
        norms += [("x1", l), ("xf", l)]
    norms += [("mem", 0), ("final",)]
    for l in range(DEPTH):
        norms += [("x2", l)] + ([("ckv", l)] if l % 2 == 0 else [])
        norms += [("y2", l), ("xx", l), ("yx", l), ("xm", l)]
        norms += [("mem", l + 1)] * (l + 1 < DEPTH) + [("ym", l)]
    NORM = {k: i for i, k in enumerate(norms)}
    GAIN_ROWS = 18
    gain_row = {}
    for l in range(DEPTH):
        gain_row["x1", l] = l
        gain_row["xf", l] = 2 + l
        gain_row["x2", l], gain_row["xx", l], gain_row["xm", l] = 4 + 6 * l, 6 + 6 * l, 8 + 6 * l
        gain_row["mem", l] = 16 + l

    with ExitStack() as ctx:
        def sb(name, shape, dt=F32):
            return ctx.enter_context(nc.sbuf_tensor(name, shape, dt))

        def sem(name):
            return ctx.enter_context(nc.semaphore(name))

        cst = sb("cst", [P, C_COLS])
        raw = sb("raw", [P, RAW, CH])
        whi = sb("whi", [P, HL, HALF], F32R)
        wlo = sb("wlo", [P, HL, HALF], F32R)
        x = sb("x", [P, TT, D])
        ahi = sb("ahi", [P, KD, SEQ], F32R)
        alo = sb("alo", [P, KD, SEQ], F32R)
        mhi = sb("mhi", [P, KD, SEQ], F32R)
        mlo = sb("mlo", [P, KD, SEQ], F32R)
        proj = sb("proj", [P, TT, QKV1])
        region = sb("region", [P, 7296])
        qT = sb("qT", [P, 16, SEQ])
        work = sb("work", [P, 4608])
        o_nat = sb("o_nat", [P, TT, D])
        gain_b = sb("gain_b", [P, D])
        misc = sb("misc", [P, 528])
        gains = sb("gains", [P, KD, GAIN_ROWS])
        conv = sb("conv", [P, FF1 // P, 8])
        ss = sb("ss", [P, len(norms), 4])
        rstd = sb("rstd", [P, len(norms), 4])
        small = sb("small", [P, 16, 16])
        pos_i = sb("pos_i", [P, TT], I32)
        sel = sb("sel", [P, 3 * P], BF16)
        ident_b = sb("ident_b", [P, P], BF16)
        den = sb("den", [P, TT, 16])
        rden = sb("rden", [P, TT, 16])
        low = sb("low", [P, TT, 16])
        ps = ctx.enter_context(nc.psum_tensor("ps", [P, 8, 512], F32))
        band_dram = nc.dram_tensor("band", [NBIAS, P * (PITCH + 1) + PITCH], F32, kind="Internal").ap()

        ident = cst[:, C_ID:C_ID + P]
        ones = cst[:, C_ONE:C_ONE + P]
        tri = cst[:, C_TRI:C_TRI + P]
        gates = region[:, 0:4096].rearrange("p (t n) -> p t n", t=TT)
        gate_bias = region[:, 4096:6144]
        dil_mask = region[:, 6144:6144 + M_COLS]
        band = region[:, 0:4096].rearrange("p (h c) -> p h c", h=16)
        kvn = region[:, 4096:5120].rearrange("p (t n) -> p t n", t=TT)
        qiT = region[:, 3072:4096].rearrange("p (b n) -> p b n", b=4)
        kicT = region[:, 5120:5632].rearrange("p (b n) -> p b n", b=2)
        relu_i = region[:, 5632:6656].rearrange("p (s n) -> p s n", s=2)
        cand = region[:, 7040:7296], work[:, 2560:2816]
        eT = work[:, 3072:4608].rearrange("p (s n) -> p s n", s=2)
        nat = work[:, 0:2048].rearrange("p (s t n) -> p s t n", s=2, t=TT)
        cv = work[:, 2048:2560]
        sl = work[:, 2560:3072]
        ut = work[:, 3072:3584]
        junk = work[:, 3072:4096]
        junk2 = qT[:, 0:8, :].rearrange("p b n -> p (b n)")
        junk_act = work[:, 0:2048].rearrange("p (i n) -> p i n", i=4)
        ystep = work[:, 2048:4096].rearrange("p (t n) -> p t n", t=TT)
        rt = work[:, 0:1536].rearrange("p (i t h d) -> p i t h d", i=4, t=TT, h=24)
        gain_rows = work[0:GAIN_ROWS, 0:1024]
        conv_rows = work[0:8, 1024:1024 + FF1]
        band_rows = gain_b[0:NBIAS, 0:BAND_W]
        uk_nat = work[:, 0:512].rearrange("p (b n) -> p b n", b=4)
        ukT = work[:, 512:1024].rearrange("p (b n) -> p b n", b=4)
        uv = work[:, 1024:1536]
        kdup = work[:, 1536:2048]
        lam_rows = misc[:, 0:256]
        subln = misc[:, 256:384]
        akv = misc[:, 384:512]
        sinks = misc[:, 512:528]

        landed = [sem(f"landed{i}") for i in range(RAW)]
        cst_in = sem("cst_in")
        ident_in = sem("ident_in")
        gains_in = sem("gains_in")
        x_in = sem("x_in")
        rows_in = sem("rows_in")
        mask_in = sem("mask_in")
        bgate_in = sem("bgate_in")
        gainb_in = sem("gainb_in")
        mem_in = sem("mem_in")
        misc_in = sem("misc_in")
        small_w_in = sem("small_w_in")
        band_out = sem("band_out")
        band_in = sem("band_in")
        stored = sem("stored")
        hi_done = sem("hi_done")
        lo_done = sem("lo_done")
        pe_out = sem("pe_out")
        pe_grp = sem("pe_grp")
        grp_act = sem("grp_act")
        grp_dve = sem("grp_dve")
        ev_act = sem("ev_act")
        ev_dve = sem("ev_dve")
        x_ready = sem("x_ready")
        ss_ready = sem("ss_ready")
        rstd_ready = sem("rstd_ready")
        power_set = sem("power_set")
        mean_ready = sem("mean_ready")
        chain = sem("chain")
        act_chain = sem("act_chain")
        rope_done = sem("rope_done")
        trig_arg = sem("trig_arg")
        trig_done = sem("trig_done")
        gate_pre = sem("gate_pre")
        gate_done = sem("gate_done")
        at_s = sem("at_s")
        at_t = sem("at_t")
        at_e = sem("at_e")
        at_x = sem("at_x")
        at_ya = sem("at_ya")
        at_yd = sem("at_yd")
        at_o = sem("at_o")
        o_ready = sem("o_ready")
        sb_z = sem("sb_z")
        sb_abs = sem("sb_abs")
        sb_ln = sem("sb_ln")
        sb_keep = sem("sb_keep")
        sb_sum = sem("sb_sum")
        sb_arg = sem("sb_arg")
        sb_att = sem("sb_att")
        cols_out = sem("cols_out")
        sb_o = sem("sb_o")
        mixed = sem("mixed")
        silu_ready = sem("silu_ready")
        uhi = sem("uhi")
        ulo = sem("ulo")
        sq_ready = sem("sq_ready")
        relu_ready = sem("relu_ready")
        idx_used = sem("idx_used")
        sel_ready = sem("sel_ready")
        diff_taken = sem("diff_taken")
        diff_step = sem("diff_step")
        diff_sq = sem("diff_sq")
        diff_sum = sem("diff_sum")
        diff_ready = sem("diff_ready")
        c_ready = sem("c_ready")
        kdup_ready = sem("kdup_ready")
        lam_arg = sem("lam_arg")
        lam_exp = sem("lam_exp")
        sink_arg = sem("sink_arg")
        sink_exp = sem("sink_exp")
        block = ctx.enter_context(nc.Block())

        def yb(tt, c):
            return 2 * tt + c % 2

        def in2_banks(l, p):
            late = (((4, (6, 2)), (5, (7, 3))), ((1, (1, 6)), (2, (7, 3))))[l % 2]
            return dict(late).get(p, (yb(0, p), yb(1, p)))

        def y2b(tt, c):
            return 6 * c + tt

        def unit(qt, slot, w, parts, bias, pv, o_bank, o_col, sel_mask=None):
            return dict(qt=qt, slot=slot, w=w, parts=parts, bias=bias, pv=pv, o_bank=o_bank, o_col=o_col, sel=sel_mask)

        def half(i):
            return 64 * (i % 2)

        def dilated_units():
            us = []
            for qt in range(TT):
                nk = P * (qt + 1)
                for h in range(HG):
                    parts, pv = [], []
                    for g in range(NG):
                        i = g * HG + h
                        b = half(i)
                        parts.append((g * nk, nk, qT[b:b + 64, i // 2, qt * P:qt * P + P], qT[b:b + 64, 6 + i // 2, 0:nk]))
                        pv += [proj[:, s, 1536 + i * HD:1536 + i * HD + HD] for s in range(qt + 1)]
                    at = (0, 3 * P)[qt]
                    us.append(unit(qt, h, 3 * nk, parts, dil_mask[:, at:at + 3 * nk], pv, 6, (qt * HG + h) * HD))
            return us

        def head_unit(qt, q, k, nk_of, bias, v, slot, o, masked):
            nk = nk_of(qt)
            return unit(qt, slot, nk, [(0, nk, q(qt), k(nk))], bias(qt, nk), [v(s) for s in range(nk // P)], *o(qt),
                        sel[:, (0, P)[qt]:(0, P)[qt] + nk] if masked else None)

        def out_at(col):
            return lambda qt: ((6, 2)[qt] + col // 512, col % 512)

        def causal(qt):
            return P * (qt + 1)

        def band_of(h):
            return lambda qt, nk: band[:, h, SEQ - nk:SEQ]

        def even_heads():
            hs = []
            for i in range(2 * HB):
                b = half(i)
                hs.append((lambda qt, i=i, b=b: qT[b:b + 64, i // 2, qt * P:qt * P + P],
                           lambda nk, i=i, b=b: qT[b:b + 64, 4 + i // 2, 0:nk], causal, band_of(HA + i // 2),
                           lambda s, i=i: proj[:, s, 2248 + P * (i // 2):2248 + P * (i // 2) + P], i, out_at(P * i), False))
            return hs

        def dsa_heads():
            hs = []
            for i in range(HA):
                b = half(i)
                hs.append((lambda qt, i=i, b=b: qT[b:b + 64, 8 + i // 2, qt * P:qt * P + P],
                           lambda nk, i=i, b=b: qT[b:b + 64, 12 + i // 2, 0:nk], causal, band_of(i),
                           lambda s, i=i: proj[:, s, HD * i:HD * i + HD], 2 * HB + i, out_at(HD * i), True))
            return hs

        def odd_heads():
            hs = []
            for i in range(HC):
                b, kv = half(i), i // 8
                hs.append((lambda qt, i=i, b=b: qT[b:b + 64, i // 2, qt * P:qt * P + P],
                           lambda nk, kv=kv, b=b: qT[b:b + 64, 8 + kv, 0:nk], causal, band_of(i),
                           lambda s, kv=kv: proj[:, s, 1152 + HD * kv:1152 + HD * kv + HD], i, out_at(HD * i), False))
            return hs

        def cross_heads():
            hs = []
            for i in range(HX):
                b = half(i)
                hs.append((lambda qt, i=i, b=b: qT[b:b + 64, i // 2, qt * P:qt * P + P],
                           lambda nk, i=i, b=b: qT[b:b + 64, 2 + i // 2, 0:nk], lambda qt: SEQ, lambda qt, nk: None,
                           lambda s, i=i: kvn[:, s, 256 + HD * i:256 + HD * i + HD], i, out_at(HD * i), False))
            return hs

        stages = []
        for l in range(DEPTH):
            stages.append((("dil", l), dilated_units()))
        for l in range(DEPTH):
            if l % 2 == 0:
                heads = even_heads() + dsa_heads()
            else:
                heads = odd_heads()
            us = [head_unit(qt, *h) for h in heads for qt in range(TT)]
            stages.append((("even" if l % 2 == 0 else "odd", l), us))
            stages.append((("cross", l), [head_unit(qt, *h) for qt in range(TT) for h in cross_heads()]))
        first_unit, n_units = {}, 0
        units_of = {}
        for k, us in stages:
            for d in us:
                d["wide"] = us[-1]["w"] > SEQ
            first_unit[k], units_of[k] = n_units, us
            n_units += len(us)

        def copies(u):
            return u // 2 + 1, (u + 1) // 2

        def wait_copied(eng, u):
            d, s = copies(u)
            if u % 2 == 0:
                eng.wait_ge(at_yd, d)
            else:
                eng.wait_ge(at_ya, s)

        def x_count(what, l=0):
            if what == "mix":
                return 2 * (2 * l + 1)
            if what == "ffn":
                return 2 * (2 * l + 2)
            if what == "final":
                return 2 * (2 * DEPTH + 1)
            return 2 * (2 * DEPTH + 1 + 3 * l + ("y2", "yx", "ym").index(what) + 1)


        by_columns = [k for l in range(DEPTH) for k in (("pa", l), ("down", l, NFB - 1))]
        by_columns += [k for l in range(DEPTH) for k in (("wo", l), ("w2", l, NMB - 1))]

        def wait_product(eng, key, tt, c=1):
            if c == 0 and key in by_columns:
                eng.wait_ge(cols_out, TT * by_columns.index(key) + tt + 1)
            else:
                eng.wait_ge(pe_out, 4 * plan.jobs[key][-1] + 3 + tt)

        def step_banks(b):
            return [0, 1] if b == 1 else [6, 7]

        def evs_act(l, what, b=None):
            per1 = 2 * (6 + NFB)
            if b is not None:
                return per1 * l + 12 + 2 * (b + 1)
            return per1 * l + 2 * (what + 1)

        def evs_act2(l, what, j=0):
            base = 2 * (6 + NFB) * DEPTH
            for i in range(l):
                base += 2 * (-(-(EV_COLS if i % 2 == 0 else OD_COLS) // 512) + 2)
            nj = -(-(EV_COLS if l % 2 == 0 else OD_COLS) // 512)
            place = IN2_ORDER[l % 2].index(j) if what == "in2" else 0
            return base + 2 * (1 + {"kv": 0, "in2": 1 + place, "wq": 1 + nj}[what])

        order = [(k, l) for l in range(DEPTH) for k in ("sb", "dil")]
        for l in range(DEPTH):
            order += [("dsa", l)] if l % 2 == 0 else [("odd a", l), ("odd b", l)]
            order.append(("cross", l))
        o_counts = {k: 2 * (i + 1) for i, k in enumerate(order)}

        rs_count, total = {}, 0
        for k in norms:
            total += 1
            rs_count[k] = total

        def sbk(h):
            return work[:, 3072 + 384 * h:3072 + 384 * (h + 1)]

        def sba(h):
            return work[:, 1536 + 384 * h:1536 + 384 * (h + 1)]

        def sbz(h):
            return work[:, 384 * h:384 * (h + 1)]

        def kdup2(tt, kv):
            return kdup[:, (2 * tt + kv) * P:(2 * tt + kv + 1) * P]

        def lag_of(key):
            return 2 if key[0] == "dil" else 3

        def slots_of(key):
            return 2 if key[0] == "dil" else 4

        def step_of(first, u, d):
            at = first + (768 * (u % 2) if d["wide"] else SEQ * (u % 4))
            return work[:, at:at + d["w"]]

        def turned(u, d):
            if d["w"] > SEQ or d["wide"]:
                return ps[:, 4:6, :].rearrange("p b n -> p (b n)")[:, 0:d["w"]]
            return ps[:, 4 + u % 2, 0:d["w"]]

        def bank_of(key):
            if key[0] == "qk2" and key[2] in (2, 3):
                return {2: 7, 3: 3}[key[2]]
            return 4 + plan.groups[key] % 2

        def group_ready(eng, key):
            eng.wait_ge(pe_grp, plan.groups[key] + 1)

        @block.sync
        def _(sp):
            sp.dma_start(ident, a["cst"][:, C_ID:C_ID + P]).then_inc(ident_in, 16)
            sp.dma_start(x[:], a["x"][0].rearrange("(t p) d -> p t d", p=P)).then_inc(x_in, 16)
            sp.dma_start(gain_rows[0:2, :], a["norm_mix"]).then_inc(gains_in, 16)
            sp.dma_start(gain_rows[2:4, :], a["norm_ffn"]).then_inc(gains_in, 16)
            sp.dma_start(gain_rows[4:16, :], a["norm_g_2"].rearrange("l i d -> (l i) d")).then_inc(gains_in, 16)
            sp.dma_start(gain_rows[16:18, :], a["xa_mem_norm_2"]).then_inc(gains_in, 16)
            for n in range(NCH):
                kc, cols, srcs = plan.chunks[n]
                if n == RAW:
                    sp.dma_start(cst[:, P:], a["cst"][:, P:]).then_inc(cst_in, 16)
                    sp.dma_start(conv_rows[0:6, :], a["conv_w"].rearrange("l i d -> (l i) d")).then_inc(rows_in, 16)
                    sp.dma_start(conv_rows[6:8, :], a["conv_b"]).then_inc(rows_in, 16)
                    sp.dma_start(work[0:NBUCKET, 3840:3840 + NBIAS], a["rel_bias_table_2"]).then_inc(rows_in, 16)
                if n >= RAW:
                    sp.wait_ge(hi_done, 2 * (n - RAW + 1))
                    sp.wait_ge(lo_done, 2 * (n - RAW + 1))
                dst = raw[:, n % RAW, 0:kc * cols].rearrange("p (k n) -> p k n", k=kc)
                for c0, w, src in srcs:
                    sp.dma_start(dst[:, :, c0:c0 + w], src).then_inc(landed[n % RAW], 16)
            sp.wait_ge(x_ready, x_count("ym", DEPTH - 1))
            sp.dma_start(out[0].rearrange("(t p) d -> p t d", p=P), x[:]).then_inc(stored, 16)
            sp.wait_ge(stored, 16)

        @block.gpsimd
        def _(pool):
            pool.dma_start(pos_i[:], a["positions"].rearrange("a (t p) -> p (a t)", p=P),
                           allow_slow_non_contiguous=True).then_inc(misc_in, 16)
            nc.gpsimd.memset(small[:, 0, :], -0.5).then_inc(power_set, 1)
            pool.wait_ge(power_set, 1)
            n_ss, n_mean = [0], [0]

            def root(key, n_sums, mean=False, src=None, dst=None):
                i = NORM[key]
                n_ss[0] += n_sums
                if mean:
                    n_mean[0] += 1
                    pool.wait_ge(mean_ready, n_mean[0])
                else:
                    pool.wait_ge(ss_ready, n_ss[0])
                src = ss[:, i, 0:TT] if src is None else src
                dst = rstd[:, i, 0:TT] if dst is None else dst
                nc.gpsimd.tensor_tensor(dst, src, small[:, 0, 0:src.shape[-1]], ALU.pow).then_inc(rstd_ready, 1)

            def band_store(h0, n):
                line = P * (PITCH + 1) + PITCH
                pool.dma_start(bass.AP(band_dram.tensor, h0 * line, [[line, n], [PITCH + 1, P], [1, PITCH]]),
                               band_rows[h0:h0 + n].unsqueeze(1).to_broadcast([n, P, PITCH])).then_inc(band_out, 16)

            def band_load(h0, n):
                return bass.AP(band_dram.tensor, h0 * (P * (PITCH + 1) + PITCH) + P - 1,
                               [[PITCH, P], [P * (PITCH + 1) + PITCH, n], [1, SEQ]])

            for l in range(DEPTH):
                root(("x1", l), 2)
                if l == 0:
                    pool.dma_start(dil_mask, a["masks"]).then_inc(mask_in, 16)
                    pool.dma_start(gate_bias, a["b_gate"][0].partition_broadcast(P)).then_inc(bgate_in, 16)
                    pool.wait_ge(grp_act, plan.by_number[plan.groups["bias"]][1])
                    for i in range(BAND_PARTS):
                        pool.wait_ge(pe_out, 4 * plan.jobs["in1", 0, 2][-1] + 12 * i)
                        band_store(NBIAS // BAND_PARTS * i, NBIAS // BAND_PARTS)
                    pool.wait_ge(band_out, 16 * BAND_PARTS)
                    pool.dma_start(gain_b[:], a["norm_final"].partition_broadcast(P)).then_inc(gainb_in, 16)
                    pool.wait_ge(gate_pre, 2 * NGC)
                    pool.dma_start(gate_bias, a["b_gate"][1].partition_broadcast(P)).then_inc(bgate_in, 16)
                root(("xf", l), 2)
            pool.wait_ge(pe_grp, plan.groups["mix", DEPTH - 1, 3] + 1)
            pool.dma_start(o_nat[:], a["mem_2"][0].rearrange("(t p) d -> p t d", p=P)).then_inc(mem_in, 16)
            root(("mem", 0), 2)
            root(("final",), 2, True)
            n_final = x_count("final")
            pool.wait_ge(x_ready, n_final)
            pool.dma_start(band[:, 0:12, :], band_load(0, 12)).then_inc(band_in, 16)
            pool.dma_start(gain_b[:], a["norm_g_2"][0, 1].partition_broadcast(P)).then_inc(gainb_in, 16)
            pool.dma_start(lam_rows, a["ev_b_lambda_2"][0].rearrange("a d -> (a d)").partition_broadcast(P)).then_inc(misc_in, 16)
            pool.dma_start(subln, a["ev_b_subln_2"][0].partition_broadcast(P)).then_inc(misc_in, 16)
            pool.dma_start(akv, a["ev_a_kv_norm_2"][0].partition_broadcast(P)).then_inc(misc_in, 16)
            pool.dma_start(sinks, a["od_sinks_2"][0].partition_broadcast(P)).then_inc(misc_in, 16)
            root(("x2", 0), 2)
            pool.dma_start(uk_nat, a["ev_a_w_uk_2"][0].rearrange("(b h) d l -> (h d) b l", h=2)).then_inc(small_w_in, 16)
            pool.dma_start(uv.rearrange("p (h d) -> p h d", h=HA), a["ev_a_w_uv_2"][0].rearrange("h l d -> l h d")).then_inc(small_w_in, 16)
            for l in range(DEPTH):
                if l > 0:
                    pool.wait_ge(x_ready, x_count("ym", l - 1))
                    pool.dma_start(gain_b[:], a["norm_g_2"][l, 1].partition_broadcast(P)).then_inc(gainb_in, 16)
                    pool.dma_start(band[:, 0:16, :], band_load(HA + HB, HC)).then_inc(band_in, 16)
                    root(("x2", l), 2)
                if l % 2 == 0:
                    root(("ckv", l), 2)
                    n_diff = [0]

                    def step(ins):
                        n_diff[0] += 1
                        ins.then_inc(diff_step, 1)
                        pool.wait_ge(diff_step, (2 * TT + 2) * (l // 2) + n_diff[0])

                    parts = [[o_nat[:, qt, c0:c0 + 512].rearrange("p (h d) -> p h d", d=P) for c0 in (512, 0)] for qt in range(TT)]
                    for qt, (o, t) in enumerate(parts):
                        pool.wait_ge(diff_taken, 4 * TT * (l // 2) + 2 * (TT + qt + 1))
                        step(nc.gpsimd.tensor_tensor(o, o, t, ALU.add))
                        nc.gpsimd.tensor_tensor(t, o, o, ALU.mult).then_inc(diff_sq, 1)
                    pool.wait_ge(diff_sq, TT * (l // 2 + 1))
                    for o, t in parts:
                        step(nc.gpsimd.tensor_tensor(o, o, subln.unsqueeze(1).to_broadcast([P, HB, P]), ALU.mult))
                    pool.wait_ge(diff_sum, TT * (l // 2 + 1))
                    mean, r = small[:, 2:2 + TT, 0:HB], small[:, 4:4 + TT, 0:HB]
                    keep = (1.0 - LAM_INIT) ** 2
                    step(nc.gpsimd.tensor_scalar(mean, mean, 1.0 / (P * keep), EPS2 / keep, ALU.mult, ALU.add))
                    step(nc.gpsimd.tensor_tensor(r, mean, small[:, 0, 0:TT * HB].rearrange("p (t h) -> p t h", t=TT), ALU.pow))
                    for qt, (o, t) in enumerate(parts):
                        nc.gpsimd.tensor_tensor(o, o, r[:, qt].unsqueeze(2).to_broadcast([P, HB, P]), ALU.mult).then_inc(diff_ready, 1)
                for k, key in enumerate(("y2", "yx", "ym")):
                    if key == "ym" and l + 1 < DEPTH:
                        pool.dma_start(o_nat[:], a["mem_2"][0].rearrange("(t p) d -> p t d", p=P)).then_inc(mem_in, 16)
                        root(("mem", l + 1), 2)
                    root((key, l), 4, True)
                    pool.wait_ge(x_ready, x_count(key, l))
                    if k < 2:
                        pool.dma_start(gain_b[:], a["norm_g_2"][l, 3 + 2 * k].partition_broadcast(P)).then_inc(gainb_in, 16)
                        root((("xx", "xm")[k], l), 2)

        @block.tensor
        def _(pe):
            def half_chunk(n, h, hi, lo, k0, outs, first, final, stream=None, at=(0, 0)):
                kc, cols, _ = plan.chunks[n]
                kh, m = kc // 2, 2 * n + h
                if stream:
                    place = stream["place"]((k0 + (h + 1) * kh - 1) // 2)
                    stream["need"](place)
                pe.wait_ge(lo_done, m + 1)
                wh = whi[:, m % HL, 0:kh * cols].rearrange("p (k n) -> p k n", k=kh)
                wl = wlo[:, m % HL, 0:kh * cols].rearrange("p (k n) -> p k n", k=kh)
                for tt in range(TT):
                    rows_ = slice(tt * P, tt * P + P)
                    for k in range(kh):
                        kx = k0 + h * kh + k
                        for c0, w, bank in outs[tt]:
                            o = ps[:, bank, at[tt]:at[tt] + w]
                            nc.tensor.matmul(o, hi[:, kx, rows_], wh[:, k, c0:c0 + w], start=first and h == 0 and k == 0 and (tt == 0 or at[1] == 0),
                                             stop=False)
                        for c0, w, bank in outs[tt]:
                            o = ps[:, bank, at[tt]:at[tt] + w]
                            nc.tensor.matmul(o, hi[:, kx, rows_], wl[:, k, c0:c0 + w], start=False, stop=False)
                        for c0, w, bank in outs[tt]:
                            o = ps[:, bank, at[tt]:at[tt] + w]
                            mm = nc.tensor.matmul(o, lo[:, kx, rows_], wh[:, k, c0:c0 + w], start=False,
                                                  stop=final and h == 1 and k == kh - 1 and (tt == 1 or at[1] == 0))
                    mm.then_inc(pe_out, 1)
                if stream:
                    stream["turn_to"](place + 2)

            def wide_job(key, hi, lo, banks, n=512, stream=None, before={}, ks=(0, KD // 2)):
                ids = plan.jobs[key]
                for j, i in enumerate(ids):
                    for h in range(2):
                        if 2 * j + h in before:
                            before[2 * j + h]()
                        half_chunk(i, h, hi, lo, ks[j], [[(0, n, banks[tt])] for tt in range(TT)], j == 0, j == len(ids) - 1, stream)

            def column_chunk(n, hi, lo, k0, bank, first):
                for c in range(2):
                    for h in range(2):
                        m = 2 * n + h
                        if c == 0:
                            pe.wait_ge(lo_done, m + 1)
                        wh, wl = (w[:, m % HL, 512 * c:512 * c + 512] for w in (whi, wlo))
                        for tt in range(TT):
                            xh, xl = (t[:, k0 + h, tt * P:tt * P + P] for t in (hi, lo))
                            o = ps[:, bank(tt, c), :]
                            nc.tensor.matmul(o, xh, wh, start=first and h == 0, stop=False)
                            nc.tensor.matmul(o, xh, wl, start=False, stop=False)
                            mm = nc.tensor.matmul(o, xl, wh, start=False, stop=h == 1)
                            if c == 1:
                                mm.then_inc(pe_out, 1)
                            elif h == 1:
                                mm.then_inc(cols_out, 1)

            def tall_job(key, hi, lo, k0, bank, first, final, between=None, stream=None):
                ids = plan.jobs[key]
                for j, i in enumerate(ids):
                    if key in by_columns and i == ids[-1]:
                        column_chunk(i, hi, lo, k0 + 2 * j, bank, first and j == 0)
                        continue
                    outs = [[(0, 512, bank(tt, 0)), (512, 512, bank(tt, 1))] for tt in range(TT)]
                    for h in range(2):
                        half_chunk(i, h, hi, lo, k0 + 2 * j, outs, first and j == 0, final and j == len(ids) - 1, stream)
                        if between and 2 * j + h == len(ids) - 1:
                            between()

            def group_bank(key):
                t = plan.groups[key]
                if t >= 2:
                    mode, na, nd = plan.by_number[t - 2]
                    if mode == "act":
                        pe.wait_ge(grp_act, na)
                    else:
                        pe.wait_ge(grp_dve, nd)
                return ps[:, bank_of(key), :]

            def turn_blocks(key, srcs):
                bank = group_bank(key)
                for j, src in enumerate(srcs):
                    mm = nc.tensor.transpose(bank[:, j * P:j * P + P], src, ident)
                mm.then_inc(pe_grp, 1)

            def stream(tag, l, src, ready, gs=(0, 1, 2, 3)):
                turned, waited = [0], [0]

                def turn_to(i):
                    while turned[0] <= min(i, 3):
                        t = turned[0]
                        if t % 2 == 0:
                            ready(t // 2)
                        g = gs[t]
                        turn_blocks((tag, l, g), [src[:, tt, (2 * g + b) * P:(2 * g + b + 1) * P] for b in range(2) for tt in range(TT)])
                        turned[0] += 1

                def need(i):
                    while waited[0] <= i:
                        turn_to(waited[0] + 1)
                        pe.wait_ge(grp_dve, plan.by_number[plan.groups[tag, l, gs[waited[0]]]][2])
                        waited[0] += 1

                return dict(turn_to=turn_to, need=need, place=gs.index)

            def x_half(n):
                return lambda h: pe.wait_ge(x_ready, n - 1 + h)

            def attention(key, each=None):
                us, u0 = units_of[key], first_unit[key]
                wide_units = us[-1]["w"] > SEQ

                def s_bank(u):
                    return 2 * (u % 2) if wide_units else u % 2

                def scores(i):
                    u, d = u0 + i, us[i]
                    if u >= 2:
                        pe.wait_ge(at_t, u - 1)
                    flat = ps[:, s_bank(u):s_bank(u) + (2 if wide_units else 1), :].rearrange("p b n -> p (b n)")
                    for c0, n, q, k in d["parts"]:
                        mm = nc.tensor.matmul(flat[:, c0:c0 + n], q, k, start=True, stop=d["sel"] is None)
                    if d["sel"] is not None:
                        mm = nc.tensor.matmul(flat[:, 0:d["w"]], ident_b[:], d["sel"], start=False, stop=True)
                    mm.then_inc(at_s, 1)

                def turn(i):
                    u, d = u0 + i, us[i]
                    pe.wait_ge(at_e, u + 1)
                    back = 1 if wide_units else 2
                    if u >= back:
                        wait_copied(pe, u - back)
                    for b in range(d["w"] // P):
                        at = b * P
                        o = ps[:, 4 + at // 512, at % 512:at % 512 + P] if wide_units else ps[:, 4 + u % 2, at:at + P]
                        mm = nc.tensor.transpose(o, step_of(1536, u, d)[:, at:at + P], ident)
                    mm.then_inc(at_x, 1)

                def values(i):
                    u, d = u0 + i, us[i]
                    wait_copied(pe, u)
                    vw = d["pv"][0].shape[-1]
                    o = ps[:, d["o_bank"], d["o_col"]:d["o_col"] + vw]
                    for b, v in enumerate(d["pv"]):
                        mm = nc.tensor.matmul(o, eT[:, u % 2, b * P:b * P + P], v, start=b == 0, stop=b == len(d["pv"]) - 1)
                    mm.then_inc(at_o, 1)

                n, lag = len(us), lag_of(key)
                for i in range(n + lag + 1):
                    if i < n:
                        scores(i)
                    if lag <= i < n + lag:
                        turn(i - lag)
                    if lag + 1 <= i:
                        values(i - lag - 1)
                    if each:
                        each(i)

            def memory_stream(l):
                sm = stream("mem", l, o_nat, lambda h: pe.wait_ge(mem_in, 16 * (l + 1)))
                sm["turn_to"](1)
                return sm

            pe.wait_ge(ident_in, 16)
            pe.wait_ge(gains_in, 16 * 4)
            bank = group_bank("gains")
            for k in range(KD):
                mm = nc.tensor.transpose(bank[:, k * GAIN_ROWS:(k + 1) * GAIN_ROWS], gain_rows[:, k * P:k * P + P], ident[0:GAIN_ROWS, 0:GAIN_ROWS])
            mm.then_inc(pe_grp, 1)

            def turn_conv():
                pe.wait_ge(cst_in, 16)
                pe.wait_ge(rows_in, 16 * 3)
                bank = group_bank("conv")
                for k in range(FF1 // P):
                    mm = nc.tensor.transpose(bank[:, k * 8:(k + 1) * 8], conv_rows[:, k * P:k * P + P], ident[0:8, 0:8])
                mm.then_inc(pe_grp, 1)
                bank = group_bank("bias")
                nc.tensor.matmul(bank[0:NBIAS, :], work[0:NBUCKET, 3840:3840 + NBIAS], cst[0:NBUCKET, C_HOT:C_HOT + BAND_W],
                                 start=True, stop=True).then_inc(pe_grp, 1)

            for l in range(DEPTH):
                sx = stream("x1", l, x, x_half(x_count("ffn", l - 1)) if l else lambda h: pe.wait_ge(x_in, 16))

                def turn_qk(g):
                    c0 = 2 * P * g if g < 6 else 2304 + 2 * P * (g - 6)
                    turn_blocks(("qk1", l, g), [proj[:, tt, c0 + b * P:c0 + (b + 1) * P] for b in range(2) for tt in range(TT)])

                def gate_half(f):
                    c, h = divmod(f, 2)
                    if h == 0 and c:
                        pe.wait_ge(gate_pre, 2 * (NGC * l + c))
                    half_chunk(plan.jobs["gate", l, c][0], h, ahi, alo, 0, [[(0, GC, 7)], [(0, GC, 7)]], True, True, None, (0, GC))

                for j in range(QKV1 // 512):
                    if j >= 2:
                        pe.wait_ge(ev_act, evs_act(l, j - 2))
                    wide_job(("in1", l, j), ahi, alo, [yb(0, j), yb(1, j)], stream=sx if j == 0 else None)
                    if l == 0 and j == 0:
                        turn_conv()
                    if j >= 3:
                        if j == 3:
                            pe.wait_ge(rope_done, l + 1)
                        turn_qk(2 * j - 6)
                        turn_qk(2 * j - 5)
                gate_half(0)
                pe.wait_ge(ev_act, evs_act(l, 5))
                turn_qk(6)
                turn_qk(7)
                gate_half(1)
                pe.wait_ge(grp_act, plan.by_number[plan.groups["qk1", l, 7]][1])
                pe.wait_ge(grp_dve, plan.by_number[plan.groups["qk1", l, 6]][2])
                for h in range(HG):
                    b, blk = half(h), 12 + h // 2
                    z = ps[:, h, 0:384]
                    nc.tensor.matmul(z[:, 0:SEQ], qT[b:b + 64, blk + 2, 0:P], qT[b:b + 64, blk, :], start=True, stop=True)
                    nc.tensor.matmul(z[:, SEQ:384], qT[b:b + 64, blk + 2, P:SEQ], qT[b:b + 64, blk, P:SEQ], start=True, stop=True).then_inc(sb_z, 1)
                for f in (2, 3, 4):
                    gate_half(f)
                for h in range(HG):
                    pe.wait_ge(sb_keep, HG * l + h + 1)
                    keep = sbk(h)
                    c = ps[:, h, 0:384]
                    nc.tensor.matmul(c[:, 0:P], tri, keep[:, 0:P], start=True, stop=True)
                    nc.tensor.matmul(c[:, P:SEQ], tri, keep[:, P:SEQ], start=True, stop=False)
                    nc.tensor.matmul(c[:, P:SEQ], ones, keep[:, SEQ:384], start=False, stop=True)
                    nc.tensor.matmul(c[:, SEQ:384], tri, keep[:, SEQ:384], start=True, stop=True).then_inc(sb_sum, 1)
                gate_half(5)
                for h in range(HG):
                    pe.wait_ge(sb_att, HG * l + h + 1)
                    att = sba(h)
                    v = [proj[:, s, 2816 + h * HD:2816 + (h + 1) * HD] for s in range(TT)]
                    nc.tensor.matmul(ps[:, 6, h * HD:(h + 1) * HD], att[:, 0:P], v[0], start=True, stop=True)
                    at = (HG + h) * HD
                    nc.tensor.matmul(ps[:, 6, at:at + HD], att[:, P:SEQ], v[0], start=True, stop=False)
                    nc.tensor.matmul(ps[:, 6, at:at + HD], att[:, SEQ:384], v[1], start=False, stop=True).then_inc(sb_o, 1)

                def turn_branch(g):
                    c0 = 512 * ("a", "b").index(g)
                    turn_blocks(("y1", l, g), [o_nat[:, tt, c0 + b * P:c0 + (b + 1) * P] for b in range(2) for tt in range(TT)])

                for f in (6, 7):
                    gate_half(f)
                pe.wait_ge(o_ready, o_counts["sb", l])
                turn_branch("b")

                def between_heads(i):
                    if 8 + i < 2 * NGC:
                        gate_half(8 + i)
                    h = i - len(units_of["dil", l]) - PB_AT
                    if 0 <= h < 2:
                        if h == 0:
                            pe.wait_ge(at_t, first_unit["dil", l] + len(units_of["dil", l]))
                        half_chunk(plan.jobs["pb", l][0], h, mhi, mlo, 2, [[(0, 512, yb(tt, 0)), (512, 512, yb(tt, 1))] for tt in range(TT)], True, True)
                    if i == 1:
                        pe.wait_ge(grp_dve, plan.by_number[plan.groups["y1", l, "b"]][2])

                attention(("dil", l), between_heads)
                pe.wait_ge(o_ready, o_counts["dil", l])
                turn_branch("a")
                pe.wait_ge(grp_dve, plan.by_number[plan.groups["y1", l, "a"]][2])
                pe.wait_ge(gate_pre, 2 * NGC * (l + 1))
                tall_job(("pa", l), mhi, mlo, 0, lambda tt, c: 4 + 2 * c + tt, True, True)
                sx = stream("mix", l, o_nat, lambda h: pe.wait_ge(mixed, 4 * l + 2 * h + 2))
                sf = stream("xf", l, x, x_half(x_count("mix", l)))
                wide_job(("out1", l, 0), mhi, mlo, [yb(0, 0), yb(1, 0)], stream=sx)
                wide_job(("out1", l, 1), mhi, mlo, [yb(0, 1), yb(1, 1)], before={2: lambda: sf["turn_to"](1)})

                def turn_step(b):
                    pe.wait_ge(ev_act, evs_act(l, "up", b))
                    for i, t in enumerate(("ta", "tb")):
                        turn_blocks((t, l, b), [nat[:, b % 2, tt, i * FB + f * P:i * FB + (f + 1) * P] for f in range(2) for tt in range(TT)])

                def down(b, between=None):
                    pe.wait_ge(ulo, NFB * l + b + 1)
                    tall_job(("down", l, b), mhi, mlo, 2 * (b % 4), lambda tt, c: yb(tt, c), b == 0, b == NFB - 1, between)

                wide_job(("up", l, 0), ahi, alo, step_banks(0), stream=sf)
                wide_job(("up", l, 1), ahi, alo, step_banks(1))
                for b in range(NFB - 2):
                    turn_step(b)
                    if b:
                        pe.wait_ge(ev_act, evs_act(l, "up", b + 1))
                    last = b == NFB - 3
                    wide_job(("up", l, b + 2), ahi, alo, step_banks(b + 2), before={3: lambda: turn_step(NFB - 2)} if last else {})
                    if b == 0:
                        pe.wait_ge(ev_act, evs_act(l, "up", 1))
                    down(b, (lambda: turn_step(NFB - 1)) if last else None)
                down(NFB - 2)
                if l == DEPTH - 1:
                    sm = memory_stream(0)
                down(NFB - 1)

            for l in range(DEPTH):
                even = l % 2 == 0
                sx = stream("x2", l, x, x_half(x_count("final") if l == 0 else x_count("ym", l - 1)))
                wide_job(("kv", l), ahi, alo, [6, 7], stream=sm, before={3: lambda: sx["turn_to"](1)})
                cols = EV_COLS if even else OD_COLS
                order = IN2_ORDER[l % 2]

                def blocks_of(c0):
                    return [proj[:, tt, c0 + b * P:c0 + (b + 1) * P] for b in range(2) for tt in range(TT)]

                def taken(*k):
                    pe.wait_ge(grp_act, plan.by_number[plan.groups[(k[0], l) + k[1:]]][1])

                def even_group(k):
                    key = (k[0], l) + k[1:]
                    if k[0] == "qi":
                        pe.wait_ge(ev_act, evs_act2(l, "in2", 2))
                        turn_blocks(key, blocks_of(640 + 2 * P * k[1]))
                    elif k[0] == "ki":
                        pe.wait_ge(kdup_ready, 1)
                        turn_blocks(key, [kdup[:, tt * P:tt * P + P] for tt in range(TT)])
                    elif k[0] == "ck":
                        pe.wait_ge(c_ready, 2)
                        turn_blocks(key, [proj[:, tt, 512:640] for tt in range(TT)])
                    elif k[0] == "qkb":
                        pe.wait_ge(ev_act, evs_act2(l, "in2", (2, 3, 3, 4)[k[1]]))
                        turn_blocks(key, blocks_of(1224 + 2 * P * k[1]))
                    elif k[0] == "qa":
                        pe.wait_ge(ev_act, evs_act2(l, "in2", 0))
                        turn_blocks(key, blocks_of(2 * P * k[1]))
                    elif k[0] == "uk":
                        pe.wait_ge(small_w_in, 32)
                        turn_blocks(key, [uk_nat[:, b, :] for b in range(4)])
                    elif k[0] == "idx":
                        qt, g = k[1:]
                        nk = causal(qt)
                        taken("ki")
                        bank = group_bank(key)
                        for i in range(2):
                            h = 4 * (g // 2) + g % 2 + 2 * i
                            b = half(h)
                            mm = nc.tensor.matmul(bank[:, i * SEQ:i * SEQ + nk], qiT[b:b + 64, h // 2, qt * P:qt * P + P],
                                                  kicT[b:b + 64, 0, 0:nk], start=True, stop=True)
                        mm.then_inc(pe_grp, 1)
                    elif k[0] == "ka":
                        taken("uk")
                        taken("ck")
                        bank = group_bank(key)
                        for b in range(2):
                            mm = nc.tensor.matmul(bank[:, b * SEQ:(b + 1) * SEQ], ukT[:, 2 * k[1] + b, :], kicT[:, 1, :], start=True, stop=True)
                        mm.then_inc(pe_grp, 1)
                    else:
                        bank = group_bank(key)
                        nc.tensor.matmul(bank, kicT[:, 1, k[1] * P:k[1] * P + P], uv, start=True, stop=True).then_inc(pe_grp, 1)

                def odd_group(k):
                    g = k[1]
                    if g < 4:
                        pe.wait_ge(ev_act, evs_act2(l, "in2", g // 2))
                        turn_blocks(("qk2", l, g), blocks_of(2 * P * g))
                    else:
                        pe.wait_ge(kdup_ready, 2)
                        turn_blocks(("qk2", l, g), [kdup2(tt, kv) for kv in range(2) for tt in range(TT)])

                def groups_at(s):
                    for k in (EVEN_GROUPS if even else ODD_GROUPS).get(s, ()):
                        (even_group if even else odd_group)(k)

                def in2_half(p, h):
                    j = order[p]
                    banks = in2_banks(l, p)
                    c, half_of = divmod(h, 2)
                    n = min(512, cols - 512 * j)
                    half_chunk(plan.jobs["in2", l, j][c], half_of, mhi, mlo, c * (KD // 2), [[(0, n, banks[tt])] for tt in range(TT)],
                               c == 0, c == 1, sx if p == 0 else None)

                last = len(order) - 1
                for s in range(4 * last + (0 if even else 1)):
                    p, h = divmod(s, 4)
                    if h == 0 and p >= 2:
                        pe.wait_ge(ev_act, evs_act2(l, "in2", order[p - 2]))
                    groups_at(s)
                    in2_half(p, h)
                if even:
                    groups_at(4 * last)
                    pe.wait_ge(ev_act, evs_act2(l, "in2", order[-3]))
                    taken("qkb", 2)

                    def even_waits(i):
                        if i < 4:
                            in2_half(last, i)
                        if i == 0:
                            groups_at(99)
                        if i == 1:
                            taken("qkb", 3)
                        if i == 5:
                            pe.wait_ge(ev_act, evs_act2(l, "in2", order[-1]))
                        if i + 1 == 4 * HB:
                            pe.wait_ge(sel_ready, TT)
                        if i == 4 * HB + lag_of(("even", l)):
                            pe.wait_ge(diff_taken, 2 * TT)

                    attention(("even", l), even_waits)
                else:
                    groups_at(4 * last + 1)
                    pe.wait_ge(grp_dve, plan.by_number[plan.groups["qk2", l, 4]][2])
                    taken("qk2", 1)

                    def odd_waits(i):
                        if i < 3:
                            in2_half(last, i + 1)
                        if i == 8:
                            groups_at(99)
                        if i + 1 == HC:
                            pe.wait_ge(grp_dve, plan.by_number[plan.groups["qk2", l, 2]][2])
                            taken("qk2", 3)

                    attention(("odd", l), odd_waits)
                so = stream("o2", l, o_nat, lambda h: pe.wait_ge(diff_ready, TT * (l // 2 + 1)) if even and h == 0 else pe.wait_ge(
                    o_ready, o_counts["dsa" if even else ("odd a", "odd b")[h], l]),
                            O2_GROUPS[l % 2])
                wide_job(("out2", l, 0), ahi, alo, [y2b(0, 0), y2b(1, 0)], stream=so, ks=O2_CHUNKS[l % 2])
                turn_blocks(("qkx", l, 0), [kvn[:, tt, b * P:(b + 1) * P] for b in range(2) for tt in range(TT)])
                wide_job(("out2", l, 1), ahi, alo, [y2b(0, 1), y2b(1, 1)], ks=O2_CHUNKS[l % 2])
                wide_job(("wq", l), mhi, mlo, [6, 7], 256, stream=stream("xx", l, x, x_half(x_count("y2", l))))
                pe.wait_ge(ev_act, evs_act2(l, "wq"))
                turn_blocks(("qkx", l, 1), [proj[:, tt, b * P:(b + 1) * P] for b in range(2) for tt in range(TT)])
                pe.wait_ge(grp_dve, plan.by_number[plan.groups["qkx", l, 0]][2])
                pe.wait_ge(grp_act, plan.by_number[plan.groups["qkx", l, 1]][1])
                attention(("cross", l))
                pe.wait_ge(o_ready, o_counts["cross", l])
                turn_blocks(("ox", l), [o_nat[:, tt, b * P:(b + 1) * P] for b in range(2) for tt in range(TT)])
                pe.wait_ge(grp_dve, plan.by_number[plan.groups["ox", l]][2])
                tall_job(("wo", l), mhi, mlo, 0, lambda tt, c: yb(tt, c), True, True)
                wide_job(("w1", l, 0), ahi, alo, step_banks(0), stream=stream("xm", l, x, x_half(x_count("yx", l))))
                wide_job(("w1", l, 1), ahi, alo, step_banks(1))

                def turn_step2(b):
                    pe.wait_ge(sq_ready, 2 * (NMB * l + b + 1))
                    for g in range(2):
                        turn_blocks(("tm", l, b, g), [nat[:, b % 2, tt, (2 * g + f) * P:(2 * g + f + 1) * P] for f in range(2) for tt in range(TT)])

                for b in range(NMB):
                    if b < NMB - 2:
                        turn_step2(b)
                    if b + 2 < NMB:
                        if b:
                            pe.wait_ge(relu_ready, 2 * (NMB * l + b + 2))
                        wide_job(("w1", l, b + 2), ahi, alo, step_banks(b + 2))
                    pe.wait_ge(grp_dve, plan.by_number[plan.groups["tm", l, b, 1]][2])
                    if b == 0:
                        pe.wait_ge(relu_ready, 2 * (NMB * l + 2))
                    if b == NMB - 1 and l + 1 < DEPTH:
                        sm = memory_stream(l + 1)
                    tall_job(("w2", l, b), mhi, mlo, 4 * (b % 2), lambda tt, c: yb(tt, c), b == 0, b == NMB - 1,
                             (lambda: turn_step2(b + 1)) if NMB - 3 <= b < NMB - 1 else None)

        @block.scalar
        def _(act):
            n_split = [0]
            n_link = [0]

            def link(ins):
                n_link[0] += 1
                ins.then_inc(act_chain, 1)
                act.wait_ge(act_chain, n_link[0])

            def split_half(m_last):
                while n_split[0] <= min(m_last, 2 * NCH - 1):
                    m = n_split[0]
                    n, h = divmod(m, 2)
                    kc, cols, _ = plan.chunks[n]
                    w = kc // 2 * cols
                    if h == 0:
                        act.wait_ge(landed[n % RAW], plan.landed[n])
                    if m >= HL:
                        act.wait_ge(pe_out, 2 * (m - HL + 1))
                    nc.scalar.copy(whi[:, m % HL, 0:w], raw[:, n % RAW, h * w:h * w + w]).then_inc(hi_done, 1)
                    n_split[0] += 1

            def product(key, tt, c=1):
                wait_product(act, key, tt, c)

            def scaled(key, norm, dst, n, banks, func=ACT.Copy, signal=ev_act):
                act.wait_ge(rstd_ready, rs_count[norm])
                for tt in range(TT):
                    product(key, tt)
                    nc.scalar.activation(dst(tt), ps[:, banks[tt], 0:n], func, scale=rstd[:, NORM[norm], tt:tt + 1]).then_inc(signal, 1)

            def stream_hi(tag, l, hi, row=None, gs=range(4)):
                for g in gs:
                    key = (tag, l, g)
                    group_ready(act, key)
                    bank = ps[:, bank_of(key), :]
                    if row is None:
                        nc.scalar.copy(hi[:, 2 * g:2 * g + 2, :].rearrange("p b n -> p (b n)"), bank).then_inc(grp_act, 1)
                    else:
                        nc.scalar.activation(hi[:, 2 * g, :], bank[:, 0:SEQ], ACT.Copy, scale=gains[:, 2 * g, row:row + 1])
                        nc.scalar.activation(hi[:, 2 * g + 1, :], bank[:, SEQ:512], ACT.Copy,
                                             scale=gains[:, 2 * g + 1, row:row + 1]).then_inc(grp_act, 1)

            def take(key, dst, scale=1.0, cols=512, func=ACT.Copy):
                group_ready(act, key)
                bank = ps[:, bank_of(key), 0:cols]
                nc.scalar.activation(dst, bank, func, scale=scale).then_inc(grp_act, 1)

            def blocks(t, b0, n=2):
                return t[:, b0:b0 + n, :].rearrange("p b n -> p (b n)")

            def attention(key, each=None):
                us, u0 = units_of[key], first_unit[key]
                n, lag, slots = len(us), lag_of(key), slots_of(key)
                for i in range(n + lag):
                    if each:
                        each(i)
                    if i < n:
                        u, d = u0 + i, us[i]
                        act.wait_ge(at_t, u + 1)
                        if u >= slots:
                            act.wait_ge(at_x, u - slots + 1)
                        s = d["slot"]
                        nc.scalar.activation(step_of(1536, u, d), step_of(0, u, d), ACT.Exp, scale=-1.0,
                                             bias=low[:, d["qt"], s:s + 1], accum_out=den[:, d["qt"], s:s + 1]).then_inc(at_e, 1)
                    if i >= lag and (u0 + i - lag) % 2 == 1:
                        u, d = u0 + i - lag, us[i - lag]
                        act.wait_ge(at_x, u + 1)
                        if u >= 2:
                            act.wait_ge(at_o, u - 1)
                        nc.scalar.copy(eT[:, u % 2, 0:d["w"]], turned(u, d)).then_inc(at_ya, 1)

            def memory_start(l, n0):
                split_half(n0 + 1)
                stream_hi("mem", l, ahi, row=gain_row["mem", l], gs=(0, 1))
                split_half(n0 + 3)

            def memory_rest(l, n0):
                stream_hi("mem", l, ahi, row=gain_row["mem", l], gs=(2,))
                split_half(n0 + 4)
                stream_hi("mem", l, ahi, row=gain_row["mem", l], gs=(3,))
                split_half(n0 + 6)

            act.wait_ge(ident_in, 16)
            nc.scalar.copy(ident_b[:], ident)
            take("gains", gains[:].rearrange("p k r -> p (k r)"), cols=KD * GAIN_ROWS)
            act.wait_ge(grp_act, plan.by_number[plan.groups["gains"]][1])

            def take_conv():
                take("conv", conv[:].rearrange("p k r -> p (k r)"), cols=8 * (FF1 // P))
                group_ready(act, "bias")
                nc.scalar.activation(band_rows, ps[0:NBIAS, 4 + plan.groups["bias"] % 2, :], ACT.Copy, scale=-1.0).then_inc(grp_act, 1)

            for l in range(DEPTH):
                m0 = 2 * plan.jobs["in1", l, 0][0]
                for g in range(4):
                    stream_hi("x1", l, ahi, row=gain_row["x1", l], gs=(g,))
                    split_half(m0 + (g if g < 2 else g + 2))

                def take_qk(g):
                    take(("qk1", l, g), blocks(qT, 2 * g), scale=-SCALE if g in (0, 1, 2, 6) else 1.0)

                f0 = 2 * plan.jobs["gate", l, 0][0]
                for j in range(QKV1 // 512):
                    split_half(2 * plan.jobs["in1", l, j][-1] + 4)
                    scaled(("in1", l, j), ("x1", l), lambda tt: proj[:, tt, 512 * j:512 * j + 512], 512, [yb(0, j), yb(1, j)])
                    if l == 0 and j == 0:
                        take_conv()
                    if l == 0 and j == 1:
                        act.wait_ge(trig_arg, 1)
                        nc.scalar.activation(small[:, 10:12, :], small[:, 8:10, :], ACT.Sin).then_inc(trig_done, 1)
                    split_half(2 * plan.jobs["in1", l, j][-1] + 5)
                    if j >= 3:
                        take_qk(2 * j - 5)
                take_qk(7)
                split_half(f0 + 5)
                for h in range(HG):
                    act.wait_ge(sb_abs, HG * l + h + 1)
                    link(nc.scalar.activation(sba(h), sba(h), ACT.Exp, scale=-1.0))
                for h in range(HG):
                    nc.scalar.activation(sba(h), sba(h), ACT.Ln, bias=1.0).then_inc(sb_ln, 1)
                split_half(f0 + 6)
                for h in range(HG):
                    act.wait_ge(sb_arg, HG * l + h + 1)
                    nc.scalar.activation(sba(h), sba(h), ACT.Exp).then_inc(sb_att, 1)
                split_half(f0 + 10)
                take(("y1", l, "b"), blocks(mhi, 2))
                split_half(f0 + 11)
                attention(("dil", l), each=lambda i: split_half(f0 + 10 + i))
                act.wait_ge(gate_pre, 2 * NGC * (l + 1))
                nc.scalar.activation(gates[:, :, D:2 * D], gates[:, :, D:2 * D], ACT.Sigmoid).then_inc(gate_done, 1)
                take(("y1", l, "a"), blocks(mhi, 0))
                split_half(f0 + 2 * NGC + 5)
                nc.scalar.activation(gates[:, :, 0:D], gates[:, :, 0:D], ACT.Sigmoid).then_inc(gate_done, 1)
                stream_hi("mix", l, mhi, gs=(0, 1))
                split_half(f0 + 2 * NGC + 7)
                stream_hi("mix", l, mhi, gs=(2, 3))
                n0 = 2 * plan.jobs["out1", l, 1][0]
                split_half(n0 + 3)
                stream_hi("xf", l, ahi, row=gain_row["xf", l], gs=(0, 1))
                split_half(n0 + 7)
                stream_hi("xf", l, ahi, row=gain_row["xf", l], gs=(2, 3))

                def up_out(b):
                    scaled(("up", l, b), ("xf", l), lambda tt: nat[:, b % 2, tt, :], 512, step_banks(b))

                def activate(b):
                    act.wait_ge(grp_dve, plan.by_number[plan.groups["ta", l, b]][2])
                    nc.scalar.activation(sl, cv, ACT.Silu).then_inc(silu_ready, 1)

                def upper(b):
                    act.wait_ge(grp_dve, plan.by_number[plan.groups["tb", l, b]][2])
                    nc.scalar.copy(blocks(mhi, 2 * (b % 4)), ut).then_inc(uhi, 1)

                for b in range(2):
                    split_half(2 * plan.jobs["up", l, b + 1][0] + 2)
                    up_out(b)
                for b in range(NFB - 2):
                    n0 = 2 * plan.jobs["up", l, b + 2][0]
                    split_half(n0 + 3)
                    activate(b)
                    split_half(n0 + 4)
                    upper(b)
                    split_half(n0 + 6)
                    up_out(b + 2)
                    if b == NFB - 3:
                        activate(NFB - 2)
                        upper(NFB - 2)
                    split_half(n0 + (8 if b < NFB - 3 else 7))
                activate(NFB - 1)
                upper(NFB - 1)
                n0 = 2 * plan.jobs["down", l, NFB - 1][-1]
                if l == DEPTH - 1:
                    memory_start(0, n0)
                    act.wait_ge(x_ready, x_count("ffn", l))
                    nc.scalar.activation(junk2[:, D:], x[:, 1, :], ACT.Square, scale=D ** -0.5, accum_out=ss[:, NORM["final",], 1:2]).then_inc(ss_ready, 1)
                    memory_rest(0, n0)
                split_half(n0 + 4)

            def squares(job, key, l, banks=yb, cs=(0, 1)):
                i = NORM[key, l]
                for c in cs:
                    for tt in range(TT):
                        product(job(c), tt, c)
                        nc.scalar.activation(junk_act[:, 2 * c + tt, :], ps[:, banks(tt, c), :], ACT.Square, scale=D ** -0.5,
                                             accum_out=ss[:, i, 2 * c + tt:2 * c + tt + 1]).then_inc(ss_ready, 1)

            for l in range(DEPTH):
                even = l % 2 == 0
                nk = 2 * plan.jobs["kv", l][0]
                stream_hi("x2", l, mhi, row=gain_row["x2", l], gs=(0, 1))
                split_half(nk + 7)
                scaled(("kv", l), ("mem", l), lambda tt: kvn[:, tt, :], 512, [6, 7])
                stream_hi("x2", l, mhi, row=gain_row["x2", l], gs=(2,))
                split_half(nk + 8)
                stream_hi("x2", l, mhi, row=gain_row["x2", l], gs=(3,))
                cols = EV_COLS if even else OD_COLS
                order = IN2_ORDER[l % 2]

                def in2_out(j):
                    n = min(512, cols - 512 * j)
                    scaled(("in2", l, j), ("x2", l), lambda tt: proj[:, tt, 512 * j:512 * j + n], n, in2_banks(l, order.index(j)))

                def even_take(k):
                    key = (k[0], l) + k[1:]
                    if k[0] == "idx":
                        qt, g = k[1:]
                        nk = causal(qt)
                        group_ready(act, key)
                        t = qt * (HA // 2) + g
                        if t >= 2:
                            act.wait_ge(idx_used, t - 1)
                        src = ps[:, bank_of(key), :].rearrange("p (h n) -> p h n", h=2)[:, :, 0:nk]
                        dst = relu_i[:, t % 2, :].rearrange("p (h n) -> p h n", h=2)[:, :, 0:nk]
                        nc.scalar.activation(dst, src, ACT.Relu).then_inc(grp_act, 1)
                    elif k[0] == "qi":
                        take(key, blocks(qiT, 2 * k[1]))
                    elif k[0] == "ki":
                        take(key, kicT[:, 0, :], cols=SEQ)
                    elif k[0] == "ck":
                        take(key, kicT[:, 1, :], cols=SEQ)
                    elif k[0] == "qkb":
                        take(key, blocks(qT, 2 * k[1]), scale=-SCALE if k[1] < 2 else 1.0)
                    elif k[0] == "qa":
                        take(key, blocks(qT, 8 + 2 * k[1]), scale=-SCALE)
                    elif k[0] == "uk":
                        take(key, blocks(ukT, 0, 4))
                    elif k[0] == "ka":
                        take(key, blocks(qT, 12 + 2 * k[1]))
                    else:
                        take(key, proj[:, k[1], 0:512])

                def odd_take(k):
                    if k[1] % 2:
                        take(("qk2", l, k[1]), blocks(qT, 2 * k[1]), scale=-SCALE)

                n0 = 2 * plan.jobs["in2", l, order[0]][0]
                last = 4 * (len(order) - 1)

                def takes_at(s):
                    for k in (EVEN_GROUPS if even else ODD_GROUPS).get(s, ()):
                        (even_take if even else odd_take)(k)

                for s in range(last + (1 if even else 2)):
                    if s % 4 == 0 and s:
                        in2_out(order[s // 4 - 1])
                    split_half(n0 + min(s + 3, last + 3))
                    takes_at(s)
                split_half(n0 + last + 3)

                def last_product(i):
                    if i == 1 and even:
                        takes_at(99)
                    if i == 5:
                        in2_out(order[-1])
                    if i == 11 and not even:
                        takes_at(99)

                if even:
                    act.wait_ge(lam_arg, 2)
                    nc.scalar.activation(small[:, 7, 0:2], small[:, 6, 0:2], ACT.Exp).then_inc(lam_exp, 1)
                    attention(("even", l), each=last_product)
                else:
                    def sink_share(part):
                        heads = slice(8 * part, 8 * part + 8)
                        for qt in range(TT):
                            act.wait_ge(sink_arg, 2 * part + qt + 1)
                            nc.scalar.activation(small[:, 12 + qt, heads], small[:, 14 + qt, heads], ACT.Exp).then_inc(sink_exp, 1)

                    def odd_between(i):
                        last_product(i)
                        if i == 18:
                            sink_share(0)

                    attention(("odd", l), each=odd_between)
                    sink_share(1)
                g0, g1, g2, g3 = O2_GROUPS[l % 2]
                n0 = 2 * plan.jobs["out2", l, 0][0]
                split_half(n0)
                stream_hi("o2", l, ahi, gs=(g0, g1))
                split_half(n0 + 2)
                stream_hi("o2", l, ahi, gs=(g2,))
                split_half(n0 + 4)
                stream_hi("o2", l, ahi, gs=(g3,))
                split_half(n0 + 7)
                squares(lambda c: ("out2", l, c), "y2", l, y2b, (0,))
                split_half(n0 + 9)
                squares(lambda c: ("out2", l, c), "y2", l, y2b, (1,))
                split_half(n0 + 11)
                stream_hi("xx", l, mhi, row=gain_row["xx", l])
                split_half(n0 + 12)
                scaled(("wq", l), ("xx", l), lambda tt: proj[:, tt, 0:256], 256, [6, 7])
                split_half(n0 + 13)
                take(("qkx", l, 1), blocks(qT, 0), scale=-SCALE)
                attention(("cross", l))
                take(("ox", l), blocks(mhi, 0))
                split_half(n0 + 15)
                squares(lambda c: ("wo", l), "yx", l)
                stream_hi("xm", l, ahi, row=gain_row["xm", l], gs=(0, 1))
                split_half(n0 + 16)
                stream_hi("xm", l, ahi, row=gain_row["xm", l], gs=(2,))
                split_half(n0 + 17)
                stream_hi("xm", l, ahi, row=gain_row["xm", l], gs=(3,))
                split_half(n0 + 18)

                def mlp_out(b):
                    scaled(("w1", l, b), ("xm", l), lambda tt: nat[:, b % 2, tt, :], MB, step_banks(b), ACT.Relu, relu_ready)

                def take_step(b):
                    for g in range(2):
                        take(("tm", l, b, g), blocks(mhi, 4 * (b % 2) + 2 * g))

                for b in range(2):
                    split_half(2 * plan.jobs["w1", l, b + 1][0] + 2)
                    mlp_out(b)
                split_half(2 * plan.jobs["w1", l, 2][0] + 3)
                for b in range(NMB - 2):
                    take_step(b)
                    n0 = 2 * plan.jobs["w2", l, b][0]
                    split_half(n0 + 3)
                    mlp_out(b + 2)
                    if b < NMB - 3:
                        split_half(n0 + 6)
                for b in (NMB - 2, NMB - 1):
                    split_half(n0 + 5)
                    take_step(b)
                    split_half(n0 + 7)
                    n0 += 4
                n0 = 2 * plan.jobs["w2", l, NMB - 1][-1]
                split_half(n0 + 1)
                if l + 1 < DEPTH:
                    memory_start(l + 1, n0)
                squares(lambda c: ("w2", l, NMB - 1), "ym", l)
                if l + 1 < DEPTH:
                    memory_rest(l + 1, n0)

        @block.vector
        def _(dve):
            n_split = [0]
            n_link = [0]

            def mark(ins):
                n_link[0] += 1
                ins.then_inc(chain, 1)
                return n_link[0]

            def after(n):
                dve.wait_ge(chain, n)

            def link(ins):
                after(mark(ins))

            def split_half(m_last):
                while n_split[0] <= min(m_last, 2 * NCH - 1):
                    m = n_split[0]
                    n, h = divmod(m, 2)
                    kc, cols, _ = plan.chunks[n]
                    w = kc // 2 * cols
                    dve.wait_ge(hi_done, m + 1)
                    nc.vector.tensor_tensor(wlo[:, m % HL, 0:w], raw[:, n % RAW, h * w:h * w + w],
                                            whi[:, m % HL, 0:w].bitcast(F32), ALU.subtract).then_inc(lo_done, 1)
                    n_split[0] += 1

            def product(key, tt, c=1):
                wait_product(dve, key, tt, c)

            def group_bank(key):
                return ps[:, bank_of(key), :]

            def hi_ready(key):
                dve.wait_ge(grp_act, plan.by_number[plan.groups[key]][1])

            def stream_lo(tag, l, hi, lo, row=None, gs=range(4)):
                for g in gs:
                    key = (tag, l, g)
                    hi_ready(key)
                    bank = group_bank(key)
                    if row is None:
                        nc.vector.tensor_tensor(blocks(lo, 2 * g), bank, blocks(hi, 2 * g).bitcast(F32), ALU.subtract).then_inc(grp_dve, 1)
                    else:
                        for b in range(2):
                            ins = nc.vector.scalar_tensor_tensor(out=lo[:, 2 * g + b, :], in0=bank[:, b * SEQ:(b + 1) * SEQ],
                                                                 scalar=gains[:, 2 * g + b, row:row + 1],
                                                                 in1=hi[:, 2 * g + b, :].bitcast(F32), op0=ALU.mult, op1=ALU.subtract)
                        ins.then_inc(grp_dve, 1)

            def blocks(t, b0, n=2):
                return t[:, b0:b0 + n, :].rearrange("p b n -> p (b n)")

            def lo_of(key, hi, lo, b0):
                hi_ready(key)
                nc.vector.tensor_tensor(blocks(lo, b0), group_bank(key), blocks(hi, b0).bitcast(F32), ALU.subtract).then_inc(grp_dve, 1)

            n_sq = [0]

            def eps_of(key):
                return EPS1 if key[0] in ("x1", "xf", "final") else EPS2

            def squares(key, src, width, tiles=range(TT), junk=junk):
                i = NORM[key]
                for tt in tiles:
                    if n_sq[0]:
                        dve.wait_ge(ss_ready, n_sq[0])
                    nc.vector.tensor_tensor_reduce(out=junk[:, 0:width], in0=src(tt), in1=src(tt), scale=1.0 / width, scalar=eps_of(key), op0=ALU.mult,
                                                   op1=ALU.add, accum_out=ss[:, i, tt:tt + 1]).then_inc(ss_ready, 1)
                    n_sq[0] += 1

            def attention(key, before=None, each=None):
                us, u0 = units_of[key], first_unit[key]
                wide_units = us[-1]["w"] > SEQ
                n, lag, slots = len(us), lag_of(key), slots_of(key)
                for i in range(n + lag):
                    if before:
                        before(i)
                    if i < n:
                        u, d = u0 + i, us[i]
                        dve.wait_ge(at_s, u + 1)
                        if u >= slots:
                            dve.wait_ge(at_e, u - slots + 1)
                        b0 = 2 * (u % 2) if wide_units else u % 2
                        flat = ps[:, b0:b0 + (2 if wide_units else 1), :].rearrange("p b n -> p (b n)")[:, 0:d["w"]]
                        s = d["slot"]
                        bias = zero_bias if d["bias"] is None else d["bias"]
                        nc.vector.tensor_tensor_reduce(out=step_of(0, u, d), in0=flat, in1=bias, scale=1.0,
                                                       scalar=nsink[:, s:s + 1] if key[0] == "odd" else 3e38, op0=ALU.add, op1=ALU.min,
                                                       accum_out=low[:, d["qt"], s:s + 1]).then_inc(at_t, 1)
                    if i >= lag and (u0 + i - lag) % 2 == 0:
                        u, d = u0 + i - lag, us[i - lag]
                        dve.wait_ge(at_x, u + 1)
                        if u >= 2:
                            dve.wait_ge(at_o, u - 1)
                        nc.vector.tensor_copy(eT[:, u % 2, 0:d["w"]], turned(u, d)).then_inc(at_yd, 1)
                    if each:
                        each(i)

            def norm_out(key, first, n, dst, ended, sums=True, outputs=True):
                us, u0 = units_of[key], first_unit[key]
                d = us[first]
                qt, s, bank, col = d["qt"], d["slot"], d["o_bank"], d["o_col"]
                r = rden[:, qt, s:s + n]
                dve.wait_ge(at_o, u0 + ended)
                if sums and key[0] == "odd":
                    link(nc.vector.tensor_tensor(r, den[:, qt, s:s + n], small[:, 12 + qt, s:s + n], ALU.add))
                    link(nc.vector.reciprocal(r, r))
                elif sums:
                    link(nc.vector.reciprocal(r, den[:, qt, s:s + n]))
                if outputs:
                    nc.vector.tensor_tensor(dst, ps[:, bank, col:col + n * HD].rearrange("p (h d) -> p h d", d=HD),
                                            r.unsqueeze(2).to_broadcast([P, n, HD]), ALU.mult).then_inc(o_ready, 1)

            def heads_of(t, tt, c0, n, d=HD):
                return t[:, tt, c0:c0 + n * d].rearrange("p (h d) -> p h d", d=d)

            def memory_start(l, n0):
                split_half(n0 + 1)
                stream_lo("mem", l, ahi, alo, row=gain_row["mem", l], gs=(0, 1))
                split_half(n0 + 3)

            def memory_squares(l):
                dve.wait_ge(mem_in, 16 * (l + 1))
                squares(("mem", l), lambda tt: o_nat[:, tt, :], D, junk=junk2)

            def memory_next(l, n0, g):
                stream_lo("mem", l, ahi, alo, row=gain_row["mem", l], gs=(g,))
                split_half(n0 + (4 if g == 2 else 6))

            nsink = misc[:, 512:528]
            zero_bias = relu_i[:, 0, 0:SEQ]

            def angles():
                dve.wait_ge(misc_in, 16)
                dve.wait_ge(cst_in, 16)
                pf = small[:, 1, 0:TT]
                link(nc.vector.tensor_copy(pf, pos_i[:]))
                ang, turns, wrap = small[:, 2, :], small[:, 3, :], small[:, 4, :]
                arg = small[:, 8:10, :]
                link(nc.vector.tensor_tensor(ang.rearrange("p (t f) -> p t f", t=TT), pf.unsqueeze(2).to_broadcast([P, TT, 8]),
                                             cst[:, C_INV:C_INV + 8].unsqueeze(1).to_broadcast([P, TT, 8]), ALU.mult))
                link(nc.vector.tensor_scalar(turns, ang, 1.0 / TWO_PI, ROUND, ALU.mult, ALU.add))
                link(nc.vector.tensor_scalar(turns, turns, ROUND, None, ALU.subtract))
                for part in (PI_HI, PI_MID, PI_LO):
                    link(nc.vector.scalar_tensor_tensor(out=ang, in0=turns, scalar=-part, in1=ang, op0=ALU.mult, op1=ALU.add))
                link(nc.vector.tensor_copy(arg[:, 0, :], ang))
                link(nc.vector.tensor_scalar(arg[:, 1, :], ang, float(np.pi / 2), None, ALU.add))
                pi = float(np.float32(np.pi))
                for i in range(2):
                    for cmp, lim, step in ((ALU.is_gt, pi, -TWO_PI), (ALU.is_lt, -pi, TWO_PI)):
                        link(nc.vector.tensor_scalar(wrap, arg[:, i, :], lim, step, cmp, ALU.mult))
                        link(nc.vector.tensor_tensor(arg[:, i, :], arg[:, i, :], wrap, ALU.add))
                link(nc.vector.tensor_scalar(arg, arg, pi, None, ALU.min))
                nc.vector.tensor_scalar(arg, arg, -pi, None, ALU.max).then_inc(trig_arg, 1)

            sin, cos = (small[:, 10 + i, :].rearrange("p (t f) -> p t f", t=TT).unsqueeze(2).to_broadcast([P, TT, 24, 8]) for i in range(2))

            for l in range(DEPTH):
                m0 = 2 * plan.jobs["in1", l, 0][0]
                for g in range(4):
                    stream_lo("x1", l, ahi, alo, row=gain_row["x1", l], gs=(g,))
                    split_half(m0 + (g if g < 2 else g + 2))
                for tt in range(TT):
                    squares(("x1", l), lambda tt: x[:, tt, :], D, (tt,), junk2)
                    split_half(m0 + 6 + tt)
                if l == 0:
                    angles()

                def take_qk(g):
                    key = ("qk1", l, g)
                    group_ready(dve, key)
                    if g in (0, 2, 6):
                        nc.vector.tensor_scalar(blocks(qT, 2 * g), group_bank(key), -SCALE, None, ALU.mult).then_inc(grp_dve, 1)
                    else:
                        nc.vector.tensor_copy(blocks(qT, 2 * g), group_bank(key)).then_inc(grp_dve, 1)

                def gate_out(c):
                    at = slice(GC * c, GC * (c + 1))
                    for tt in range(TT):
                        dve.wait_ge(pe_out, 4 * plan.jobs["gate", l, c][0] + 4)
                        nc.vector.scalar_tensor_tensor(out=gates[:, tt, at], in0=ps[:, 7, GC * tt:GC * (tt + 1)],
                                                       scalar=rstd[:, NORM["x1", l], tt:tt + 1], in1=gate_bias[:, at],
                                                       op0=ALU.mult, op1=ALU.add).then_inc(gate_pre, 1)

                f0 = 2 * plan.jobs["gate", l, 0][0]
                for j in range(QKV1 // 512):
                    split_half(2 * plan.jobs["in1", l, j][-1] + 5)
                    if j == 2:
                        dve.wait_ge(ev_act, evs_act(l, 2))
                        dve.wait_ge(trig_done, 1)
                        qk = proj[:, :, 0:1536].rearrange("p t (h d) -> p t h d", d=HD)
                        x1, x2 = qk[:, :, :, 0:8], qk[:, :, :, 8:16]
                        for i, (u, v) in enumerate(((x1, cos), (x2, sin), (x2, cos), (x1, sin))):
                            n = mark(nc.vector.tensor_tensor(rt[:, i], u, v, ALU.mult))
                        after(n)
                        nc.vector.tensor_tensor(x1, rt[:, 0], rt[:, 1], ALU.subtract)
                        nc.vector.tensor_tensor(x2, rt[:, 2], rt[:, 3], ALU.add).then_inc(rope_done, 1)
                    if j >= 3:
                        take_qk(2 * j - 6)
                take_qk(6)
                split_half(f0 + 4)
                dve.wait_ge(bgate_in, 16 * (l + 1))
                dve.wait_ge(rstd_ready, rs_count["x1", l])
                gate_out(0)
                for h in range(HG):
                    dve.wait_ge(sb_z, HG * l + h + 1)
                    n = mark(nc.vector.tensor_tensor(sbz(h), ps[:, h, 0:384], cst[:, C_SBM:C_SBM + 384], ALU.add))
                    after(n)
                    nc.vector.scalar_tensor_tensor(out=sba(h), in0=sbz(h), scalar=-1.0, in1=sbz(h), op0=ALU.mult, op1=ALU.max).then_inc(sb_abs, 1)
                split_half(f0 + 5)
                gate_out(1)
                for h in range(HG):
                    dve.wait_ge(sb_ln, HG * l + h + 1)
                    nc.vector.scalar_tensor_tensor(out=sbk(h), in0=sbz(h), scalar=0.0, in1=sba(h), op0=ALU.min,
                                                   op1=ALU.subtract).then_inc(sb_keep, 1)
                split_half(f0 + 6)
                for h in range(HG):
                    dve.wait_ge(sb_sum, HG * l + h + 1)
                    nc.vector.tensor_tensor(sba(h), ps[:, h, 0:384], sbz(h), ALU.subtract).then_inc(sb_arg, 1)
                split_half(f0 + 7)
                gate_out(2)
                dve.wait_ge(sb_o, HG * (l + 1))
                for tt in range(TT):
                    nc.vector.tensor_copy(o_nat[:, tt, 512:768], ps[:, 6, SEQ * tt:SEQ * (tt + 1)]).then_inc(o_ready, 1)
                split_half(f0 + 10)
                lo_of(("y1", l, "b"), mhi, mlo, 2)
                gate_out(3)
                split_half(f0 + 11)
                if l == 0:
                    dve.wait_ge(mask_in, 16)

                def between(i, after=False):
                    if after != (i >= len(units_of["dil", l])):
                        return
                    if i % 2 == 0 and i:
                        gate_out(3 + i // 2)
                    split_half(f0 + 10 + i)

                attention(("dil", l), between, lambda i: between(i, True))
                for qt in range(TT):
                    norm_out(("dil", l), HG * qt, HG, heads_of(o_nat, qt, 0, HG), TT * HG)
                def gate_b(c):
                    for tt in range(TT):
                        product(("pb", l), tt)
                        gt = gates[:, tt, D + 512 * c:D + 512 * c + 512]
                        n = mark(nc.vector.tensor_tensor(gt, ps[:, yb(tt, c), :], gt, ALU.mult))
                    return n

                def gate_a(c, n):
                    for tt in range(TT):
                        product(("pa", l), tt, c)
                        o = o_nat[:, tt, 512 * c:512 * c + 512]
                        n = mark(nc.vector.tensor_tensor(o, ps[:, 4 + 2 * c + tt, :], gates[:, tt, 512 * c:512 * c + 512], ALU.mult))
                    after(n)
                    for tt in range(TT):
                        o = o_nat[:, tt, 512 * c:512 * c + 512]
                        nc.vector.tensor_tensor(o, o, gates[:, tt, D + 512 * c:D + 512 * c + 512], ALU.add).then_inc(mixed, 1)

                dve.wait_ge(gate_done, 2 * l + 1)
                n = gate_b(0)
                lo_of(("y1", l, "a"), mhi, mlo, 0)
                n1 = gate_b(1)
                split_half(f0 + 2 * NGC + 4)
                dve.wait_ge(gate_done, 2 * l + 2)
                gate_a(0, n)
                split_half(f0 + 2 * NGC + 5)
                stream_lo("mix", l, mhi, mlo, gs=(0, 1))
                gate_a(1, n1)
                split_half(f0 + 2 * NGC + 7)
                stream_lo("mix", l, mhi, mlo, gs=(2, 3))

                def add_out(j):
                    for tt in range(TT):
                        product(("out1", l, j), tt)
                        xs = x[:, tt, 512 * j:512 * j + 512]
                        ins = nc.vector.tensor_tensor(xs, xs, ps[:, yb(tt, j), :], ALU.add)
                    ins.then_inc(x_ready, 1)

                n0 = 2 * plan.jobs["out1", l, 1][0]
                split_half(n0 + 1)
                add_out(0)
                split_half(n0 + 3)
                stream_lo("xf", l, ahi, alo, row=gain_row["xf", l], gs=(0, 1))
                split_half(n0 + 5)
                add_out(1)
                split_half(n0 + 7)
                dve.wait_ge(x_ready, x_count("mix", l))
                stream_lo("xf", l, ahi, alo, row=gain_row["xf", l], gs=(2,))
                squares(("xf", l), lambda tt: x[:, tt, :], D)
                stream_lo("xf", l, ahi, alo, row=gain_row["xf", l], gs=(3,))
                split_half(2 * plan.jobs["up", l, 2][0] + 2)
                for b in range(NFB):
                    n0 = 2 * plan.jobs["up", l, min(b + 2, NFB - 1)][0]
                    group_ready(dve, ("ta", l, b))
                    bank = group_bank(("ta", l, b))
                    if b:
                        dve.wait_ge(silu_ready, NFB * l + b)
                    for f in range(2):
                        w = [conv[:, 2 * b + f, i:i + 1] for i in (3 * l, 3 * l + 1, 3 * l + 2, 6 + l)]
                        n = mark(nc.vector.tensor_scalar(cv[:, f * SEQ:(f + 1) * SEQ], bank[:, f * SEQ:(f + 1) * SEQ], w[2], w[3], ALU.mult, ALU.add))
                    for lag in (1, 2):
                        after(n)
                        for f in range(2):
                            w = conv[:, 2 * b + f, 3 * l + 2 - lag:3 * l + 3 - lag]
                            o = cv[:, f * SEQ + lag:(f + 1) * SEQ]
                            ins = nc.vector.scalar_tensor_tensor(out=o, in0=bank[:, f * SEQ:(f + 1) * SEQ - lag], scalar=w, in1=o,
                                                                 op0=ALU.mult, op1=ALU.add)
                            if lag == 2 and f == 1:
                                ins.then_inc(grp_dve, 1)
                            else:
                                n = mark(ins)
                    if b + 2 < NFB:
                        split_half(n0 + 4)
                    group_ready(dve, ("tb", l, b))
                    dve.wait_ge(silu_ready, NFB * l + b + 1)
                    if b:
                        dve.wait_ge(ulo, NFB * l + b)
                    nc.vector.tensor_tensor(ut, sl, group_bank(("tb", l, b)), ALU.mult).then_inc(grp_dve, 1)
                    dve.wait_ge(grp_dve, plan.by_number[plan.groups["tb", l, b]][2])
                    dve.wait_ge(uhi, NFB * l + b + 1)
                    nc.vector.tensor_tensor(blocks(mlo, 2 * (b % 4)), ut, blocks(mhi, 2 * (b % 4)).bitcast(F32), ALU.subtract).then_inc(ulo, 1)
                    split_half(n0 + {NFB - 3: 5, NFB - 2: 7}.get(b, 8))
                    if b == NFB - 2 and l == DEPTH - 1:
                        memory_squares(0)
                n0 = 2 * plan.jobs["down", l, NFB - 1][-1]
                if l == DEPTH - 1:
                    memory_start(0, n0)
                split_half(n0 + 3)
                for c in range(2):
                    for tt in range(TT):
                        product(("down", l, NFB - 1), tt, c)
                        xs = x[:, tt, 512 * c:512 * c + 512]
                        ins = nc.vector.tensor_tensor(xs, xs, ps[:, yb(tt, c), :], ALU.add)
                    ins.then_inc(x_ready, 1)
                dve.wait_ge(x_ready, x_count("ffn", l))

            squares(("final",), lambda tt: x[:, tt, :], D, (0,), junk2)
            n_sq[0] += 1
            memory_next(0, n0, 2)
            dve.wait_ge(gainb_in, 16)
            dve.wait_ge(ss_ready, n_sq[0])
            t = ss[:, NORM["final",], 1:2]
            nc.vector.tensor_scalar(t, t, EPS1, None, ALU.add).then_inc(mean_ready, 1)
            dve.wait_ge(rstd_ready, rs_count["final",])
            for c in range(2):
                cs = slice(512 * c, 512 * c + 512)
                for tt in range(TT):
                    ins = nc.vector.scalar_tensor_tensor(out=x[:, tt, cs], in0=x[:, tt, cs], scalar=rstd[:, NORM["final",], tt:tt + 1],
                                                         in1=gain_b[:, cs], op0=ALU.mult, op1=ALU.mult)
                ins.then_inc(x_ready, 1)

            memory_next(0, n0, 3)

            n_gain = [1]

            def add_normed(key, l, jobs, mid=None, banks=yb, before_second=None):
                n_gain[0] += 1
                n_sq[0] += 4
                dve.wait_ge(gainb_in, 16 * n_gain[0])

                def gain(c, tt):
                    product(jobs[c], tt, c)
                    dve.wait_ge(ss_ready, n_sq[0] - 3 + 2 * c + tt)
                    cs = slice(512 * c, 512 * c + 512)
                    return mark(nc.vector.tensor_tensor(ystep[:, tt, cs], ps[:, banks(tt, c), :], gain_b[:, cs], ALU.mult))

                def add(c):
                    for tt in range(TT):
                        cs = slice(512 * c, 512 * c + 512)
                        ins = nc.vector.scalar_tensor_tensor(out=x[:, tt, cs], in0=ystep[:, tt, cs], scalar=rstd[:, NORM[key, l], tt:tt + 1],
                                                             in1=x[:, tt, cs], op0=ALU.mult, op1=ALU.add)
                    ins.then_inc(x_ready, 1)

                for tt in range(TT):
                    gain(0, tt)
                if before_second:
                    before_second()
                gain(1, 0)
                i = NORM[key, l]
                dve.wait_ge(ss_ready, n_sq[0])
                nc.vector.scalar_tensor_tensor(out=ss[:, i, 0:TT], in0=ss[:, i, 0:TT], scalar=EPS2, in1=ss[:, i, TT:2 * TT],
                                               op0=ALU.add, op1=ALU.add).then_inc(mean_ready, 1)
                n = gain(1, 1)
                dve.wait_ge(rstd_ready, rs_count[key, l])
                after(n)
                add(0)
                if mid:
                    mid()
                add(1)
                dve.wait_ge(x_ready, x_count(key, l))

            for l in range(DEPTH):
                even = l % 2 == 0
                nk = 2 * plan.jobs["kv", l][0]
                if l == 0:
                    dve.wait_ge(x_ready, x_count("final"))
                stream_lo("x2", l, mhi, mlo, row=gain_row["x2", l], gs=(0, 1))
                split_half(nk + 7)
                stream_lo("x2", l, mhi, mlo, row=gain_row["x2", l], gs=(2,))
                split_half(nk + 8)
                squares(("x2", l), lambda tt: x[:, tt, :], D, (0,))
                stream_lo("x2", l, mhi, mlo, row=gain_row["x2", l], gs=(3,))
                split_half(nk + 9)
                squares(("x2", l), lambda tt: x[:, tt, :], D, (1,))
                order = IN2_ORDER[l % 2]
                n0 = 2 * plan.jobs["in2", l, order[0]][0]
                dve.wait_ge(band_in, 16 * (l + 1))
                nc.vector.memset(band[0:64, 0:(HA + HB) if even else HC, 192:256], BIG)
                if not even:
                    nc.vector.memset(band[64:128, 0:HC, 0:64], BIG)

                def latent_sums():
                    dve.wait_ge(ev_act, evs_act2(l, "in2", 2))
                    kd = kdup[:, 0:256].rearrange("p (t i d) -> p t i d", t=TT, i=2)
                    nc.vector.tensor_copy(kd, proj[:, :, 1152:1216].unsqueeze(2).to_broadcast([P, TT, 2, HD])).then_inc(kdup_ready, 1)
                    squares(("ckv", l), lambda tt: proj[:, tt, 512:640], P)

                def latent_out():
                    dve.wait_ge(misc_in, 16 * 5)
                    dve.wait_ge(rstd_ready, rs_count["ckv", l])
                    for tt in range(TT):
                        c = proj[:, tt, 512:640]
                        nc.vector.scalar_tensor_tensor(out=c, in0=c, scalar=rstd[:, NORM["ckv", l], tt:tt + 1], in1=akv,
                                                       op0=ALU.mult, op1=ALU.mult).then_inc(c_ready, 1)

                def lambda_sums():
                    for i in range(2):
                        if i:
                            dve.wait_ge(lam_arg, i)
                        nc.vector.tensor_tensor_reduce(out=junk[:, 512:576], in0=lam_rows[:, 128 * i:128 * i + 64], in1=lam_rows[:, 128 * i + 64:128 * i + 128],
                                                       scale=1.0, scalar=0.0, op0=ALU.mult, op1=ALU.add,
                                                       accum_out=small[:, 6, i:i + 1]).then_inc(lam_arg, 1)
                    link(nc.vector.tensor_scalar(nsink, nsink, -1.0, None, ALU.mult))

                def index_sum(qt, g):
                    nk = causal(qt)
                    adm = cst[:, C_ADM + SEQ - nk:C_ADM + SEQ]
                    t = qt * (HA // 2) + g
                    dve.wait_ge(grp_act, plan.by_number[plan.groups["idx", l, qt, g]][1])
                    for i in range(2):
                        h = 4 * (g // 2) + g % 2 + 2 * i
                        ins = nc.vector.scalar_tensor_tensor(out=cand[qt][:, 0:nk], in0=relu_i[:, t % 2, i * SEQ:i * SEQ + nk],
                                                             scalar=proj[:, qt, 1216 + h:1217 + h], in1=adm if h == 0 else cand[qt][:, 0:nk],
                                                             op0=ALU.mult, op1=ALU.add)
                        if i == 0:
                            link(ins)
                        else:
                            ins.then_inc(idx_used, 1)
                            dve.wait_ge(idx_used, t + 1)

                def top_rounds(qt, r0, r1):
                    nk = causal(qt)
                    top = small[:, 13, 0:8]
                    c = cand[qt][:, 0:nk]
                    for r in range(r0, r1):
                        link(nc.vector.max(top, c))
                        link(nc.vector.match_replace(c, top, c, SENTINEL))
                    if r1 == TOPK // 8:
                        nc.vector.tensor_scalar(sel[:, (0, P)[qt]:(0, P)[qt] + nk], c, SENTINEL / 2, BIG, ALU.is_gt, ALU.mult).then_inc(sel_ready, 1)

                def odd_keys():
                    dve.wait_ge(ev_act, evs_act2(l, "in2", 2))
                    kd = kdup.rearrange("p (t k i d) -> p t k i d", t=TT, k=2, i=2)
                    for tt in range(TT):
                        ins = nc.vector.tensor_copy(kd[:, tt], proj[:, tt, 1024:1152].rearrange("p (k d) -> p k d", d=HD).unsqueeze(2)
                                                    .to_broadcast([P, 2, 2, HD]))
                    ins.then_inc(kdup_ready, 1)

                def qk2_take(g):
                    key = ("qk2", l, g)
                    group_ready(dve, key)
                    if g < 4:
                        nc.vector.tensor_scalar(blocks(qT, 2 * g), group_bank(key), -SCALE, None, ALU.mult).then_inc(grp_dve, 1)
                    else:
                        nc.vector.tensor_copy(blocks(qT, 2 * g), group_bank(key)).then_inc(grp_dve, 1)

                def even_step(s):
                    if s == 8:
                        latent_sums()
                    if s == 9:
                        latent_out()
                    if s == 10:
                        lambda_sums()
                    if s in (11, 12):
                        index_sum(0, 2 * (s - 11))
                        index_sum(0, 2 * (s - 11) + 1)
                    if 13 <= s <= 15:
                        top_rounds(0, (0, 3, 6)[s - 13], (3, 6, 8)[s - 13])
                    if 15 <= s <= 18:
                        index_sum(1, s - 15)
                    if s == 19:
                        top_rounds(1, 0, 2)

                def odd_step(s):
                    if s == 5:
                        qk2_take(0)
                    if s == 8:
                        odd_keys()
                    if s == 9:
                        qk2_take(4)

                last = 4 * (len(order) - 1)
                for s in range(last + (1 if even else 2)):
                    split_half(n0 + min(s + 3, last + 3))
                    (even_step if even else odd_step)(s)
                split_half(n0 + last + 3)
                if even:
                    nlam = small[:, 7, 2:3]

                    def diff_out(qt, k, m):
                        o = heads_of(o_nat, qt, 512, HB, P)
                        t = heads_of(o_nat, qt, 0, HB, P)
                        hs = slice(2 * k, 2 * k + 2)
                        r = rden[:, qt, 4 * k:4 * k + 4]
                        if m == 0:
                            link(nc.vector.reciprocal(r, den[:, qt, 4 * k:4 * k + 4]))
                        r = r.rearrange("p (h m) -> p h m", m=2)[:, :, m]
                        if m == 1:
                            link(nc.vector.tensor_scalar(r, r, nlam, None, ALU.mult))
                        y = ps[:, (6, 2)[qt] + k, :].rearrange("p (h m d) -> p h m d", m=2, d=P)[:, :, m, :]
                        nc.vector.tensor_tensor((o, t)[m][:, hs], y, r.unsqueeze(2).to_broadcast([P, 2, P]), ALU.mult).then_inc(diff_taken, 1)

                    def even_between(i):
                        if i == 0:
                            dve.wait_ge(lam_exp, 1)
                            link(nc.vector.tensor_tensor(nlam, small[:, 7, 1:2], small[:, 7, 0:1], ALU.subtract))
                            link(nc.vector.tensor_scalar(nlam, nlam, -LAM_INIT, None, ALU.add))
                        if 1 <= i <= 6:
                            top_rounds(1, 1 + i, 2 + i)
                        for part in range(2):
                            step = i - 8 * part - DIFF_OUT
                            if 0 <= step < 2 * TT:
                                dve.wait_ge(at_o, first_unit["even", l] + 8 * (part + 1))
                                diff_out(step // 2, part, step % 2)
                        if i in DIFF_SUMS:
                            qt = DIFF_SUMS.index(i)
                            dve.wait_ge(diff_sq, TT * (l // 2) + qt + 1)
                            nc.vector.tensor_reduce(small[:, 2 + qt, 0:HB], heads_of(o_nat, qt, 0, HB, P), AX.X, ALU.add).then_inc(diff_sum, 1)

                    attention(("even", l), each=even_between)
                else:
                    def odd_norm(qt, part, sums=True, outputs=True):
                        norm_out(("odd", l), 16 * part + qt, 8, heads_of(o_nat, qt, 512 * part, 8), 16 * (part + 1), sums, outputs)

                    def sink_args(part):
                        heads = slice(8 * part, 8 * part + 8)
                        dve.wait_ge(at_t, first_unit["odd", l] + 16 * (part + 1))
                        for qt in range(TT):
                            nc.vector.tensor_tensor(small[:, 14 + qt, heads], low[:, qt, heads], nsink[:, heads], ALU.subtract).then_inc(sink_arg, 1)

                    def odd_between(i):
                        if i == 10:
                            qk2_take(2)
                        if i == 16:
                            sink_args(0)
                        if i == 20:
                            dve.wait_ge(sink_exp, TT)
                            for qt in range(TT):
                                odd_norm(qt, 0, outputs=False)
                        if i in ODD_NORMS:
                            odd_norm(ODD_NORMS.index(i), 0, sums=False)
                        if i == 32:
                            sink_args(1)

                    attention(("odd", l), each=odd_between)
                g0, g1, g2, g3 = O2_GROUPS[l % 2]
                n0 = 2 * plan.jobs["out2", l, 0][0]
                split_half(n0)
                stream_lo("o2", l, ahi, alo, gs=(g0,))
                split_half(n0 + 1)
                if not even:
                    dve.wait_ge(sink_exp, 2 * TT)
                if even:
                    dve.wait_ge(diff_ready, TT * (l // 2 + 1))
                for qt in range(TT):
                    if even:
                        norm_out(("even", l), 4 * HB + qt, HA, heads_of(o_nat, qt, 0, HA), 4 * HB + 2 * HA)
                    else:
                        odd_norm(qt, 1)
                stream_lo("o2", l, ahi, alo, gs=(g1,))
                n0 = 2 * plan.jobs["out2", l, 0][0]
                split_half(n0 + 2)
                stream_lo("o2", l, ahi, alo, gs=(g2,))
                split_half(n0 + 4)
                stream_lo("o2", l, ahi, alo, gs=(g3,))
                split_half(n0 + 7)

                def before_second():
                    key = ("qkx", l, 0)
                    group_ready(dve, key)
                    nc.vector.tensor_copy(blocks(qT, 2), group_bank(key)).then_inc(grp_dve, 1)
                    nc.vector.memset(zero_bias, 0.0)
                    split_half(n0 + 9)

                add_normed("y2", l, [("out2", l, 0), ("out2", l, 1)], None, y2b, before_second)
                split_half(n0 + 10)
                stream_lo("xx", l, mhi, mlo, row=gain_row["xx", l], gs=(0, 1))
                split_half(n0 + 11)
                squares(("xx", l), lambda tt: x[:, tt, :], D)
                stream_lo("xx", l, mhi, mlo, row=gain_row["xx", l], gs=(2, 3))

                def cross_between(i):
                    if i == HX + lag_of(("cross", l)) + 1:
                        norm_out(("cross", l), 0, HX, heads_of(o_nat, 0, 0, HX), HX)

                split_half(n0 + 13)
                attention(("cross", l), cross_between)
                norm_out(("cross", l), HX, HX, heads_of(o_nat, 1, 0, HX), TT * HX)
                lo_of(("ox", l), mhi, mlo, 0)
                split_half(n0 + 15)
                add_normed("yx", l, [("wo", l)] * 2)
                stream_lo("xm", l, ahi, alo, row=gain_row["xm", l], gs=(0, 1))
                split_half(n0 + 16)
                stream_lo("xm", l, ahi, alo, row=gain_row["xm", l], gs=(2,))
                split_half(n0 + 17)
                stream_lo("xm", l, ahi, alo, row=gain_row["xm", l], gs=(3,))
                split_half(n0 + 18)
                squares(("xm", l), lambda tt: x[:, tt, :], D)

                def square(b):
                    for tt in range(TT):
                        dve.wait_ge(relu_ready, 2 * (NMB * l + b) + tt + 1)
                        nc.vector.tensor_tensor(nat[:, b % 2, tt, :], nat[:, b % 2, tt, :], nat[:, b % 2, tt, :], ALU.mult).then_inc(sq_ready, 1)

                def take_step(b):
                    for g in range(2):
                        lo_of(("tm", l, b, g), mhi, mlo, 4 * (b % 2) + 2 * g)

                for b in range(2):
                    split_half(2 * plan.jobs["w1", l, b + 1][0] + 2)
                    square(b)
                split_half(2 * plan.jobs["w1", l, 2][0] + 3)
                for b in range(NMB - 2):
                    take_step(b)
                    n0 = 2 * plan.jobs["w2", l, b][0]
                    split_half(n0 + 3)
                    square(b + 2)
                    if b < NMB - 3:
                        split_half(n0 + 6)
                if l + 1 < DEPTH:
                    memory_squares(l + 1)
                for b in (NMB - 2, NMB - 1):
                    split_half(n0 + 5)
                    take_step(b)
                    split_half(n0 + 7)
                    n0 += 4
                n0 = 2 * plan.jobs["w2", l, NMB - 1][-1]
                if l + 1 < DEPTH:
                    memory_start(l + 1, n0)
                split_half(n0 + 1)
                add_normed("ym", l, [("w2", l, NMB - 1)] * 2, (lambda: memory_next(l + 1, n0, 2)) if l + 1 < DEPTH else None)
                if l + 1 < DEPTH:
                    memory_next(l + 1, n0, 3)


INPUTS = [
    "x", "positions", "norm_mix", "w_in", "b_gate", "w_proj_a", "w_proj_b", "w_out", "norm_ffn", "w_up", "conv_w", "conv_b", "w_down",
    "norm_final", "mem_2", "rel_bias_table_2", "norm_g_2", "ev_w_in_2", "ev_a_kv_norm_2", "ev_a_w_uk_2", "ev_a_w_uv_2", "ev_b_lambda_2",
    "ev_b_subln_2", "ev_w_out_2", "od_w_in_2", "od_sinks_2", "od_w_out_2", "xa_wq_2", "xa_wkv_2", "xa_wo_2", "xa_mem_norm_2", "mlp_w1_2",
    "mlp_w2_2",
]


def kernel(**inputs):
    import numpy as np
    import concourse.bacc as bacc
    from concourse import mybir
    from concourse.bass_utils import run_bass_kernel_spmd

    nc = bacc.Bacc("TRN2", target_bir_lowering=False, num_devices=1)
    cst, masks = shape_constants()
    arrays = {"in_" + n: np.ascontiguousarray(inputs[n]) for n in INPUTS}
    arrays["in_cst"], arrays["in_masks"] = cst, masks
    aps = {n[3:]: nc.dram_tensor(n, v.shape, mybir.dt.from_np(v.dtype), kind="ExternalInput").ap() for n, v in arrays.items()}
    out = nc.dram_tensor("out", (1, SEQ, D), mybir.dt.float32, kind="ExternalOutput").ap()
    build_network(nc, aps, out)
    r = run_bass_kernel_spmd(nc, [arrays], core_ids=[0])
    return r.results[0]["out"]
```
